# Optimizing a Trainium2 kernel written in Bass

```python
import math
import jax
import jax.numpy as jnp
from jax import lax
import numpy as np

D_MODEL = 1024
BATCH = 1
SEQ = 128
DEPTH = 1
DEC_BATCH = 1
DEC_SEQ = 512
PAST_LEN = 128

GRID_W = 64
DN_HEADS = 4
DN_DK = 128
DN_DV = 128
DN_WIDTH = DN_HEADS * DN_DV
DN_CHUNK = 64
SHORT_CONV = 3
HY_WIDTH = D_MODEL // 2
HY_SHORT = 3
HY_EMB = 33
HY_FFN = 64
HY_TARGET = 1e-2
HY_FAST_DECAY = 0.3
HY_SLOW_DECAY = 1.5
N_EXPERTS = 16
EC_FACTOR = 2
EXPERT_FF = D_MODEL
N_MOD = 6
ALPHA = (2 * DEPTH) ** 0.25
BETA = (8 * DEPTH) ** -0.25
LN_EPS = 1e-5
RMS_EPS = 1e-6
QKV_WIDTH = 2 * DN_HEADS * DN_DK + DN_WIDTH
IN_SPLITS = (QKV_WIDTH, DN_WIDTH, 2 * DN_HEADS, 2 * DN_HEADS, 3 * HY_WIDTH, 2 * D_MODEL)
N_IN = QKV_WIDTH + DN_WIDTH + 4 * DN_HEADS + 3 * HY_WIDTH + 2 * D_MODEL

kernel_name = 'hybrid_deltanet_hyena_ec_diffusion_step'

def _split_points(sizes):
    return [int(s) for s in np.cumsum(np.array(sizes))[:-1]]

def layer_norm(x, g=None, b=None):
    xf = x.astype(jnp.float32)
    mu = jnp.mean(xf, -1, keepdims=True)
    var = jnp.mean(jnp.square(xf - mu), -1, keepdims=True)
    y = (xf - mu) * lax.rsqrt(var + LN_EPS)
    if g is not None:
        y = y * g.astype(jnp.float32) + b.astype(jnp.float32)
    return y.astype(x.dtype)

def grid_pos_embed(rows, dim):
    r = jnp.repeat(jnp.arange(rows), GRID_W)
    col = jnp.tile(jnp.arange(GRID_W), rows)
    quarter = dim // 4
    omega = 1.0 / (10000.0 ** (jnp.arange(quarter, dtype=jnp.float32) / quarter))

    def enc(p):
        ang = p.astype(jnp.float32)[:, None] * omega[None, :]
        return jnp.concatenate([jnp.sin(ang), jnp.cos(ang)], -1)

    return jnp.concatenate([enc(r), enc(col)], -1)

def short_conv(x, w, b=None):
    k, ch = w.shape
    pad = k // 2
    y = lax.conv_general_dilated(x, w[:, None, :].astype(x.dtype), window_strides=(1,),
                                 padding=[(pad, pad)], dimension_numbers=('NWC', 'WIO', 'NWC'),
                                 feature_group_count=ch)
    if b is not None:
        y = y + b.astype(x.dtype)
    return y

def l2norm(x):
    return x * lax.rsqrt(jnp.sum(jnp.square(x), -1, keepdims=True) + 1e-6)

def chunk_gated_delta(q, k, v, g, beta, s0):
    b, h, l, dk = q.shape
    dv = v.shape[-1]
    c = DN_CHUNK
    n = l // c
    q = q.reshape(b, h, n, c, dk)
    k = k.reshape(b, h, n, c, dk)
    v = v.reshape(b, h, n, c, dv)
    g = g.reshape(b, h, n, c)
    beta = beta.reshape(b, h, n, c)
    gc = jnp.cumsum(g, -1)
    incl = jnp.tril(jnp.ones((c, c), dtype=bool))
    strict = jnp.tril(jnp.ones((c, c), dtype=bool), -1)
    decay = jnp.exp(jnp.where(incl, gc[..., :, None] - gc[..., None, :], -jnp.inf))
    kb = k * beta[..., None]
    lower = jnp.where(strict, jnp.einsum('bhncd,bhnsd->bhncs', kb, k) * decay, 0.0)
    eye = jnp.eye(c, dtype=jnp.float32)
    rhs = jnp.concatenate([v * beta[..., None], kb * jnp.exp(gc)[..., None]], -1)
    sol = lax.linalg.triangular_solve(eye + lower, rhs, left_side=True, lower=True, unit_diagonal=True)
    u, w = sol[..., :dv], sol[..., dv:]
    a_intra = jnp.einsum('bhncd,bhnsd->bhncs', q, k) * decay

    def step(s, xs):
        qi, ki, ui, wi, gi, ai = xs
        v_new = ui - jnp.einsum('bhck,bhkv->bhcv', wi, s)
        o = (jnp.einsum('bhck,bhkv->bhcv', qi * jnp.exp(gi)[..., None], s)
             + jnp.einsum('bhcs,bhsv->bhcv', ai, v_new))
        gl = gi[..., -1:]
        s = s * jnp.exp(gl)[..., None] + jnp.einsum('bhck,bhcv->bhkv', ki * jnp.exp(gl - gi)[..., None], v_new)
        return s, o

    xs = tuple(jnp.moveaxis(t, 2, 0) for t in (q, k, u, w, gc, a_intra))
    s_fin, o = lax.scan(step, s0, xs)
    o = jnp.moveaxis(o, 0, 2).reshape(b, h, l, dv)
    return o, s_fin

def deltanet_branch(qkv_raw, z, b_raw, a_raw, conv_w, a_log, dt_bias, gnorm_w, s0_f, s0_b):
    bsz, l, _ = qkv_raw.shape
    hk = DN_HEADS * DN_DK
    qkv = jax.nn.silu(short_conv(qkv_raw, conv_w)).astype(jnp.float32)
    q, k, v = jnp.split(qkv, [hk, 2 * hk], -1)

    def heads(t, d):
        return t.reshape(bsz, l, DN_HEADS, d).transpose(0, 2, 1, 3)

    q = l2norm(heads(q, DN_DK)) * (DN_DK ** -0.5)
    k = l2norm(heads(k, DN_DK))
    v = heads(v, DN_DV)

    def per_dir(t):
        return t.astype(jnp.float32).reshape(bsz, l, 2, DN_HEADS).transpose(2, 0, 3, 1)

    beta = jax.nn.sigmoid(per_dir(b_raw))
    g = -jnp.exp(a_log.astype(jnp.float32))[:, None, :, None] * jax.nn.softplus(
        per_dir(a_raw) + dt_bias.astype(jnp.float32)[:, None, :, None])
    o_f, s_f = chunk_gated_delta(q, k, v, g[0], beta[0], s0_f.astype(jnp.float32))

    def rev(t):
        return jnp.flip(t, 2)

    o_b, s_b = chunk_gated_delta(rev(q), rev(k), rev(v), rev(g[1]), rev(beta[1]), s0_b.astype(jnp.float32))
    o = o_f + rev(o_b)
    o = o * lax.rsqrt(jnp.mean(jnp.square(o), -1, keepdims=True) + RMS_EPS) * gnorm_w.astype(jnp.float32)
    o = o * jax.nn.silu(heads(z.astype(jnp.float32), DN_DV))
    return o.transpose(0, 2, 1, 3).reshape(bsz, l, DN_WIDTH).astype(qkv_raw.dtype), s_f, s_b

def hyena_filter(l, w1, b1, w2, b2, w3, freq):
    f32 = jnp.float32
    t = jnp.linspace(0.0, 1.0, l, dtype=f32)[:, None]
    bands = (HY_EMB - 1) // 2
    ang = (2.0 * math.pi * jnp.arange(l, dtype=f32) / l)[:, None] * jnp.linspace(1e-4, bands - 1, bands, dtype=f32)[None, :]
    feats = jnp.concatenate([t, jnp.cos(ang), -jnp.sin(ang)], -1)
    fr = freq.astype(f32)
    hid = jnp.sin(fr * (feats @ w1.astype(f32) + b1.astype(f32)))
    hid = jnp.sin(fr * (hid @ w2.astype(f32) + b2.astype(f32)))
    filt = hid @ w3.astype(f32)
    deltas = jnp.abs(jnp.linspace(math.log(HY_TARGET) / HY_SLOW_DECAY, math.log(HY_TARGET) / HY_FAST_DECAY,
                                  HY_WIDTH, dtype=f32))
    offset = jnp.abs(jnp.arange(l) - l // 2).astype(f32) / (l // 2)
    filt = filt * jnp.exp(-offset[:, None] * deltas[None, :])
    return filt / (jnp.sum(jnp.abs(filt), 0, keepdims=True) + 1e-6)

def hyena_branch(hy, conv_w, conv_b, w1, b1, w2, b2, w3, freq, skip):
    l = hy.shape[1]
    x0, x1, v = jnp.split(short_conv(hy, conv_w, conv_b).astype(jnp.float32), 3, -1)
    filt = hyena_filter(l, w1, b1, w2, b2, w3, freq)
    uu = x1 * v
    n_fft = 2 * l
    spec = jnp.fft.rfft(uu, n=n_fft, axis=1) * jnp.fft.rfft(filt, n=n_fft, axis=0)[None]
    conv = jnp.fft.irfft(spec, n=n_fft, axis=1)[:, l // 2: l // 2 + l]
    y = x0 * (conv + uu * skip.astype(jnp.float32))
    return y.astype(hy.dtype)

def expert_choice_ffn(u, w_router, w_gate, w_up, w_down):
    bsz, l, _ = u.shape
    cap = EC_FACTOR * l // N_EXPERTS
    probs = jax.nn.softmax((u @ w_router).astype(jnp.float32), axis=-1)
    aff, idx = lax.top_k(jnp.swapaxes(probs, 1, 2), cap)
    bidx = jnp.arange(bsz)[:, None, None]
    xs = u[bidx, idx]
    hid = jax.nn.silu(jnp.einsum('becd,edf->becf', xs, w_gate)) * jnp.einsum('becd,edf->becf', xs, w_up)
    ys = jnp.einsum('becf,efd->becd', hid, w_down) * aff[..., None].astype(u.dtype)
    return jnp.zeros_like(u).at[bidx, idx].add(ys)

def trunk_layer(x, cond, s0_f, s0_b, w_mod, b_mod, w_in, conv_a_w, a_log, dt_bias, gnorm_w,
                conv_b_w, conv_b_b, hy_w1, hy_b1, hy_w2, hy_b2, hy_w3, hy_freq, hy_bias,
                w_up_a, w_up_b, w_out, ln1_g, ln1_b, w_router, w_e_gate, w_e_up, w_e_down, ln2_g, ln2_b):
    mod = jax.nn.silu(cond) @ w_mod + b_mod
    sh1, sc1, g1, sh2, sc2, g2 = [m[:, None, :] for m in jnp.split(mod, N_MOD, -1)]
    u = layer_norm(x) * (1.0 + sc1) + sh1
    proj = u @ w_in
    qkv, z, b_raw, a_raw, hy, gates = jnp.split(proj, _split_points(IN_SPLITS), -1)
    o_a, s_f, s_b = deltanet_branch(qkv, z, b_raw, a_raw, conv_a_w, a_log, dt_bias, gnorm_w, s0_f, s0_b)
    o_b = hyena_branch(hy, conv_b_w, conv_b_b, hy_w1, hy_b1, hy_w2, hy_b2, hy_w3, hy_freq, hy_bias)
    gate_a, gate_b = jnp.split(jax.nn.sigmoid(gates), 2, -1)
    mixed = (gate_a * (o_a @ w_up_a) + gate_b * (o_b @ w_up_b)) @ w_out
    x = layer_norm(ALPHA * x + g1 * mixed, ln1_g, ln1_b)
    u = layer_norm(x) * (1.0 + sc2) + sh2
    x = layer_norm(ALPHA * x + g2 * expert_choice_ffn(u, w_router, w_e_gate, w_e_up, w_e_down), ln2_g, ln2_b)
    return x, s_f, s_b

def setup_inputs(seed: int = 0) -> dict:
    key = jax.random.key(seed)
    keys = jax.random.split(key, 40)
    f32 = jnp.float32
    L = DEPTH
    D = D_MODEL

    def nrm(i, shape, scale):
        return scale * jax.random.normal(keys[i], shape, f32)

    a_log = jnp.log(jax.random.uniform(keys[10], (L, 2, DN_HEADS), f32, 1.0, 16.0))
    dt = jnp.exp(jax.random.uniform(keys[11], (L, 2, DN_HEADS), f32, math.log(1e-3), math.log(1e-1)))
    dt_bias = dt + jnp.log(-jnp.expm1(-dt))
    return {
        'x_prompt': nrm(0, (BATCH, SEQ, D), 1.0),
        'x_sample': nrm(1, (DEC_BATCH, DEC_SEQ, D), 1.0),
        'state_delta_fwd': nrm(2, (DEC_BATCH, L, DN_HEADS, DN_DK, DN_DV), 0.3),
        'state_delta_bwd': nrm(3, (DEC_BATCH, L, DN_HEADS, DN_DK, DN_DV), 0.3),
        'c': nrm(4, (DEC_BATCH, D), 1.0),
        'c_ctx': nrm(5, (D,), 1.0),
        'w_mod': nrm(6, (L, D, N_MOD * D), D ** -0.5),
        'b_mod': nrm(7, (L, N_MOD * D), 0.1),
        'w_in': nrm(8, (L, D, N_IN), D ** -0.5),
        'conv_a_w': nrm(9, (L, SHORT_CONV, QKV_WIDTH), SHORT_CONV ** -0.5),
        'a_log': a_log,
        'dt_bias': dt_bias,
        'gnorm_w': 1.0 + nrm(12, (L, DN_DV), 0.02),
        'conv_b_w': nrm(13, (L, HY_SHORT, 3 * HY_WIDTH), HY_SHORT ** -0.5),
        'conv_b_b': nrm(14, (L, 3 * HY_WIDTH), 0.02),
        'hy_w1': nrm(15, (L, HY_EMB, HY_FFN), HY_EMB ** -0.5),
        'hy_b1': nrm(16, (L, HY_FFN), 0.02),
        'hy_w2': nrm(17, (L, HY_FFN, HY_FFN), HY_FFN ** -0.5),
        'hy_b2': nrm(18, (L, HY_FFN), 0.02),
        'hy_w3': nrm(19, (L, HY_FFN, HY_WIDTH), HY_FFN ** -0.5),
        'hy_freq': 1.0 + nrm(20, (L, HY_FFN), 0.1),
        'hy_bias': nrm(21, (L, HY_WIDTH), 1.0),
        'w_up_a': nrm(22, (L, DN_WIDTH, D), BETA * DN_WIDTH ** -0.5),
        'w_up_b': nrm(23, (L, HY_WIDTH, D), BETA * HY_WIDTH ** -0.5),
        'w_out': nrm(24, (L, D, D), BETA * D ** -0.5),
        'ln1_g': 1.0 + nrm(25, (L, D), 0.02),
        'ln1_b': nrm(26, (L, D), 0.02),
        'w_router': nrm(27, (L, D, N_EXPERTS), D ** -0.5),
        'w_e_gate': nrm(28, (L, N_EXPERTS, D, EXPERT_FF), D ** -0.5),
        'w_e_up': nrm(29, (L, N_EXPERTS, D, EXPERT_FF), D ** -0.5),
        'w_e_down': nrm(30, (L, N_EXPERTS, EXPERT_FF, D), BETA * EXPERT_FF ** -0.5),
        'ln2_g': 1.0 + nrm(31, (L, D), 0.02),
        'ln2_b': nrm(32, (L, D), 0.02),
    }

def reference(x_prompt, x_sample, state_delta_fwd, state_delta_bwd, c, c_ctx, w_mod, b_mod, w_in,
              conv_a_w, a_log, dt_bias, gnorm_w, conv_b_w, conv_b_b, hy_w1, hy_b1, hy_w2, hy_b2, hy_w3,
              hy_freq, hy_bias, w_up_a, w_up_b, w_out, ln1_g, ln1_b, w_router, w_e_gate, w_e_up,
              w_e_down, ln2_g, ln2_b):
    def layer_params(l):
        return (w_mod[l], b_mod[l], w_in[l], conv_a_w[l], a_log[l], dt_bias[l], gnorm_w[l],
                conv_b_w[l], conv_b_b[l], hy_w1[l], hy_b1[l], hy_w2[l], hy_b2[l], hy_w3[l],
                hy_freq[l], hy_bias[l], w_up_a[l], w_up_b[l], w_out[l], ln1_g[l], ln1_b[l],
                w_router[l], w_e_gate[l], w_e_up[l], w_e_down[l], ln2_g[l], ln2_b[l])

    n_req = x_prompt.shape[0]
    zero_state = jnp.zeros((n_req, DN_HEADS, DN_DK, DN_DV), jnp.float32)
    h = x_prompt
    fwd_states = []
    bwd_states = []
    for l in range(DEPTH):
        h, s_f, s_b = trunk_layer(h, c_ctx[None, :], zero_state, zero_state, *layer_params(l))
        fwd_states.append(s_f)
        bwd_states.append(s_b)
    y_prompt = h
    new_state_delta_fwd = jnp.stack(fwd_states, axis=1).astype(x_prompt.dtype)
    new_state_delta_bwd = jnp.stack(bwd_states, axis=1).astype(x_prompt.dtype)

    rows = x_sample.shape[1] // GRID_W
    h = x_sample + grid_pos_embed(rows, D_MODEL).astype(x_sample.dtype)[None]
    for l in range(DEPTH):
        h, _, _ = trunk_layer(h, c, state_delta_fwd[:, l], state_delta_bwd[:, l], *layer_params(l))
    y_sample = h
    return (y_prompt, y_sample, new_state_delta_fwd, new_state_delta_bwd)


_drawn_inputs = setup_inputs


def setup_inputs(seed=0):
    import zlib

    import numpy as np

    out = dict(_drawn_inputs(seed))
    spreads = {}
    factors = {'state_delta_fwd': 7.818,
     'state_delta_bwd': 4.451,
     'gnorm_w': 8.0,
     'conv_b_b': 7.399,
     'hy_b1': 8.0,
     'hy_b2': 8.0,
     'hy_freq': 8.0,
     'ln1_b': 2.678,
     'ln2_g': 2.9,
     'ln2_b': 2.743}
    for name, (base, spread) in spreads.items():
        noise = np.random.default_rng([zlib.crc32(name.encode()), seed]).standard_normal(out[name].shape)
        drawn = base * np.exp(spread * noise) if base else spread * noise
        out[name] = jnp.asarray(drawn.astype(out[name].dtype))
    for name, factor in factors.items():
        out[name] = (out[name] * factor).astype(out[name].dtype)
    return out
```

```python
from contextlib import ExitStack
import math

import numpy as np
import concourse.bass as bass
from concourse import mybir

F32 = mybir.dt.float32
U32 = mybir.dt.uint32
ALU = mybir.AluOpType
ACT = mybir.ActivationFunctionType
AX = mybir.AxisListType.X

P = 128
D = 1024
KB = D // P
SEQ_S, SEQ_C = 512, 128
TOK = SEQ_S + SEQ_C
NT = TOK // P
ST = SEQ_S // P
HEADS = 4
E = 16
CAP_S, CAP_C = 2 * SEQ_S // E, 2 * SEQ_C // E
ALPHA = 2.0 ** 0.25
HYW = 512
HY_EMB = 33
FREQ_S, FREQ_C = 3 * SEQ_S // 4, 3 * SEQ_C // 4
FT = FREQ_S // P
N_IN = 5648
COL_Q, COL_K, COL_V, COL_Z, COL_BA, COL_HY, COL_G = 0, 512, 1024, 1536, 2048, 2064, 3600
LEVELS = 7
GRID_W = 64

PK = {}
_at = 0
for _name, _n in (("cond", KB * 2), ("b_mod", 48), ("conv_a", 36), ("conv_b", 36), ("conv_bb", 12), ("skip", 4),
                  ("gnorm", 1), ("a_log", 8), ("dt_bias", 8), ("hy_b1", 1), ("hy_b2", 1), ("hy_freq", 1),
                  ("w_router", KB * E), ("w_ba", KB * 16), ("hy_w1", 64), ("hy_w2", 64), ("hy_w3", HYW)):
    PK[_name] = (_at, _n)
    _at += _n
PK_N = _at

CK = {}
_at = 0
for _name, _n in (("ident", P), ("tri_f", P), ("tri_b", P), ("neg_f", P), ("neg_b", P), ("mask_lo", LEVELS * P),
                  ("mask_up", LEVELS * P), ("iota64", P), ("iota32", P), ("ones", P), ("eps", 4), ("offset", NT)):
    CK[_name] = (_at, _n)
    _at += _n
CK_N = _at
FEATS_N = TOK + HYW


def filter_features(l):
    f = np.float32
    t = np.linspace(0.0, 1.0, l, dtype=f)[:, None]
    bands = (HY_EMB - 1) // 2
    w = (f(2.0 * math.pi) * np.arange(l, dtype=f) / f(l))[:, None].astype(f)
    ang = (w * np.linspace(1e-4, bands - 1, bands, dtype=f)[None, :]).astype(f)
    return np.concatenate([t, np.cos(ang), -np.sin(ang)], -1).astype(f).T


def constants():
    ck = np.zeros((P, CK_N), np.float32)

    def put(name, v):
        a, n = CK[name]
        ck[:, a:a + n] = np.asarray(v, np.float32).reshape(P, n)

    i = np.arange(P)
    up = (i[:, None] <= i[None, :])
    put("ident", np.eye(P))
    put("ones", np.ones((P, P)))
    put("tri_f", up)
    put("tri_b", up.T)
    put("neg_f", np.where(up, 0.0, -1e30))
    put("neg_b", np.where(up.T, 0.0, -1e30))
    lo = np.zeros((P, LEVELS, P))
    for lev in range(LEVELS):
        b = 1 << lev
        same = (i[:, None] // (2 * b)) == (i[None, :] // (2 * b))
        lo[:, lev] = same & ((i[:, None] % (2 * b)) >= b) & ((i[None, :] % (2 * b)) < b)
    put("mask_lo", lo)
    put("mask_up", lo.transpose(2, 1, 0))
    put("iota64", np.tile(np.arange(P) % CAP_S, (P, 1)))
    put("iota32", np.tile(np.arange(P) % 32, (P, 1)))
    put("eps", np.tile([1e-5, 128e-6, 1e-6, 0.0], (P, 1)))
    off = np.concatenate([np.abs(np.arange(l) - l // 2) / (l // 2) for l in (SEQ_S, SEQ_C)])
    put("offset", -off.reshape(NT, P).T)
    feats = np.zeros((P, FEATS_N), np.float32)
    feats[:HY_EMB, 0:SEQ_S] = filter_features(SEQ_S)
    feats[:HY_EMB, SEQ_S:TOK] = filter_features(SEQ_C)
    deltas = np.abs(np.linspace(math.log(1e-2) / 1.5, math.log(1e-2) / 0.3, HYW, dtype=np.float32))
    feats[:, TOK:] = deltas[None, :]

    def dft(l, nf):
        period = 2 * nf
        ang = 2 * np.pi * ((np.arange(nf) + 0.5)[None, :] * np.arange(l)[:, None] % period) / period
        fwd = np.stack([np.cos(ang), np.sin(ang)], 1)
        out = np.arange(l // 2, l // 2 + l)
        ang = 2 * np.pi * ((np.arange(nf) + 0.5)[:, None] * out[None, :] % (2 * period)) / period
        inv = np.stack([np.cos(ang), np.sin(ang)], 1) * (2.0 / period)
        return fwd, inv

    fs, is_ = dft(SEQ_S, FREQ_S)
    fc, ic = dft(SEQ_C, FREQ_C)
    dft_f = np.zeros((P, 4096), np.float32)
    dft_f[:, 0:ST * 2 * FREQ_S] = fs.reshape(ST, P, 2 * FREQ_S).transpose(1, 0, 2).reshape(P, -1)
    dft_f[:, ST * 2 * FREQ_S:ST * 2 * FREQ_S + 2 * FREQ_C] = fc.reshape(P, -1)
    dft_i = np.zeros((P, 4096), np.float32)
    dft_i[:, 0:FT * 2 * SEQ_S] = is_.reshape(FT, P, 2, SEQ_S).transpose(1, 0, 2, 3).reshape(P, -1)
    dft_i[0:FREQ_C, FT * 2 * SEQ_S:FT * 2 * SEQ_S + 2 * SEQ_C] = ic.reshape(FREQ_C, -1)
    quarter = D // 4
    omega = (1.0 / (10000.0 ** (np.arange(quarter, dtype=np.float32) / np.float32(quarter)))).astype(np.float32)

    def enc(n):
        ang = np.arange(n, dtype=np.float32)[:, None] * omega[None, :]
        return np.concatenate([np.sin(ang), np.cos(ang)], -1).astype(np.float32)

    rows = enc(SEQ_S // GRID_W)
    cols = enc(GRID_W)
    token = np.arange(SEQ_S).reshape(ST, P)
    return {"const_ck": ck, "const_feats": feats, "const_dft_f": dft_f, "const_dft_i": dft_i,
            "pos_row": rows[token // GRID_W].transpose(1, 0, 2), "pos_col": cols[np.arange(P) % GRID_W]}


MAGIC = 1.5 * 2.0 ** 23
TWO_PI = (6.28125, 0.0019350051879882812, 3.019916050e-07)
PI_BELOW = 3.1415925


def build(nc, T, O):
    ctx = ExitStack()
    with ctx:
        def sb(name, cols):
            return ctx.enter_context(nc.sbuf_tensor(name, [P, cols], F32))

        sems = {}

        def sem(name):
            if name not in sems:
                sems[name] = ctx.enter_context(nc.semaphore(name))
            return sems[name]

        SLOT = KB * 512
        ring = sb("ring", 4 * SLOT)
        hbuf = sb("hbuf", NT * D)
        front = sb("front", 23040)
        ck = sb("ck", CK_N)
        pk = sb("pk", PK_N)
        modT = sb("modT", 96)
        misc = sb("misc", 2700)
        dec = sb("dec", 13 * 40)
        stats = sb("stats", NT * 12 + NT * 2 + NT)
        bank = [ctx.enter_context(nc.psum_tensor(f"bank{i}", [P, 512], F32)) for i in range(8)]

        def C(name):
            a, n = CK[name]
            return ck[:, a:a + n]

        def K(name):
            a, n = PK[name]
            return pk[:, a:a + n]

        def reg(a, n):
            return front[:, a:a + n]

        ident, ones = C("ident"), C("ones")
        eps_ln, eps_q, eps_k = (C("eps")[:, i:i + 1] for i in range(3))
        bn = stats[:, 0:NT * 12].rearrange("p (t s) -> p t s", t=NT)
        mv = stats[:, NT * 12:NT * 14].rearrange("p (t s) -> p t s", t=NT)
        rstd = stats[:, NT * 14:NT * 15]

        W0 = 12800
        feats = misc[:, 0:FEATS_N]
        hid = [misc[0:64, 1152 + TOK * i:1152 + TOK * (i + 1)] for i in range(2)]
        sin_arg, sin_n = reg(2560, TOK)[0:64], reg(2560 + TOK, TOK)[0:64]
        filt = reg(0, NT * 512).rearrange("p (t c) -> p t c", t=NT)
        absf = reg(2560, NT * 512).rearrange("p (t c) -> p t c", t=NT)
        filtnorm = reg(2560, 1024).rearrange("p (j c) -> p j c", j=2)
        fspec = reg(W0 + 512, 4096).rearrange("p (j c) -> p j c", j=8)
        uspec = reg(W0 + 4608, 4096).rearrange("p (j c) -> p j c", j=8)
        ptmp = reg(W0 + 8704, 1024).rearrange("p (j c) -> p j c", j=2)
        xn = reg(W0 + 5120, 5120).rearrange("p (t d) -> p t d", t=NT)
        posc = reg(W0 + 4608, 512)
        posr = xn.rearrange("p t d -> p (t d)")[:, 0:2048].rearrange("p (t c) -> p t c", t=ST)
        cond32 = misc[:, 2432:2688].rearrange("p (k c) -> p k c", k=KB)
        modrow = misc[:, 1152:1664]
        uT = reg(0, 5120).rearrange("p (k t) -> p k t", k=KB)
        R = [reg(5120 + 2560 * i, 2560).rearrange("p (b t) -> p b t", b=4) for i in range(3)]
        x1T, uuT, x0T = R
        ybT = x0T
        uuTok = reg(5120, 2560).rearrange("p (t c) -> p t c", t=NT)
        h = hbuf[:, :].rearrange("p (t d) -> p t d", t=NT)
        kT = R[0]
        vtok = reg(7680, 2560).rearrange("p (t c) -> p t c", t=NT)
        vT = hbuf[:, 0:2560].rearrange("p (b t) -> p b t", b=4)
        qT = hbuf[:, 2560:5120].rearrange("p (b t) -> p b t", b=4)
        oT = vT
        barow = misc[:, 0:TOK]
        sq = [misc[:, TOK * (1 + i):TOK * (2 + i)] for i in range(2)]
        rn = [reg(W0 + 512 + TOK * i, TOK) for i in range(2)]

        def field(i, n=40):
            return dec[:, 40 * i:40 * i + n]

        (d_tmp, d_beta, d_negbeta, d_xa, d_neg, d_relu, d_g, d_gc, d_tot, d_negegc, d_edk, d_egl, d_expa) = (
            field(i) for i in range(13))

        def dw(r, i):
            return reg(W0 + 4608 * r + 512 * i, 512).rearrange("p (h c) -> p h c", h=HEADS)

        dD, dLnT, dAT, dKG, dKD, dQG, dM, dU, dVN = ([dw(r, i) for r in range(2)] for i in range(9))
        dW, dWT = dD, dLnT
        state = [reg(W0 + 9216 + 512 * r, 512).rearrange("p (h v) -> p h v", h=HEADS) for r in range(2)]
        zT, oG = R[0], R[1]
        sig = reg(W0, 5120).rearrange("p (b t) -> p b t", b=8)
        mixedT = reg(W0 + 5120, 5120).rearrange("p (b t) -> p b t", b=KB)
        uptmp = misc[:, 0:TOK]
        diag = misc[:, 0:2048].rearrange("p (c k f) -> p c k f", c=2, k=KB)
        grow = reg(W0, 2048).rearrange("p (c d) -> p c d", c=2)
        lnrow = reg(W0 + 2048, 2048).rearrange("p (j d) -> p j d", j=2)
        otmp = reg(10240, 2048).rearrange("p (j d) -> p j d", j=2)
        xn2 = reg(0, 5120).rearrange("p (t d) -> p t d", t=NT)
        u2T = reg(5120, 5120).rearrange("p (k t) -> p k t", k=KB)
        yacc = reg(13312, 5120).rearrange("p (t d) -> p t d", t=NT)
        rrow = misc[0:16, 0:TOK]
        mask = misc[0:16, TOK:2 * TOK]
        count = misc[0:16, 2 * TOK:3 * TOK]
        top8 = misc[0:16, 3 * TOK:3 * TOK + 8]
        probs = dec[:, 0:85].rearrange("p (t e) -> p t e", t=NT)
        slots = dec[:, 85:170].rearrange("p (t e) -> p t e", t=NT)
        rmax, rsum = dec[:, 170:175], dec[:, 175:180]
        EW = 18432

        def ew(a, n, groups=0):
            v = reg(EW + a, n)
            return v.rearrange("p (g c) -> p g c", g=groups) if groups else v

        xs, xsc = ew(0, 512), ew(512, 256)
        xsT, xcT = ew(768, 512, 8), ew(1280, 256, 8)
        sil, silc = ew(1536, 512), ew(2048, 256)
        hd, hdc = ew(2304, 512), ew(2816, 256)
        hdT, hdcT = ew(3072, 512, 8), ew(3584, 256, 8)
        ys, ysc = ew(3840, 512), ew(4352, 256)
        CT = misc[:, 0:512].rearrange("p (t c) -> p t c", t=ST)
        CTc = misc[:, 512:640]
        GA = misc[:, 640:1152].rearrange("p (t c) -> p t c", t=ST)
        GAc = misc[:, 1152:1280]
        Gs = misc[:, 1280:1536].rearrange("p (t c) -> p t c", t=ST)
        Gc = misc[:, 1536:1568]
        g2row = ring[:, 0:2048].rearrange("p (c d) -> p c d", c=2)
        ln2row = ring[:, SLOT:SLOT + 2048].rearrange("p (j d) -> p j d", j=2)

        h_spill = nc.dram_tensor("h_spill", [P, NT * D], F32, kind="Internal").ap()

        def slot(s):
            return ring[:, s * SLOT:(s + 1) * SLOT] if s < 4 else reg(5120 + (s - 4) * SLOT, SLOT)

        def wslot(s, k=KB):
            return slot(s).rearrange("p (k n) -> p k n", k=k)

        slot_full = [sem(f"slot_full{i}") for i in range(6)]
        w_in = T["w_in"].rearrange("(k p) n -> p k n", p=P)
        w_mod = T["w_mod"].rearrange("(k p) n -> p k n", p=P)
        w_out = T["w_out"].rearrange("(k p) n -> p k n", p=P)

        def cols(w, c):
            return w[:, :, c:c + 512]

        chunks = [("dftF0", 0, T["const_dft_f"], "spec_mm", 4)]
        chunks += [(f"mod{n}", (n + 1) % 6, cols(w_mod, 512 * n), "mod_mm", n // 4 + 1) for n in range(12)]
        chunks += [("hyx1", 1, cols(w_in, COL_HY + 512), "proj_mm", 4), ("hyv", 2, cols(w_in, COL_HY + 1024), "proj_mm", 8),
                   ("hyx0", 3, cols(w_in, COL_HY), "proj_mm", 12), ("dftF1", 0, T["const_dft_f"], "spec_mm", 8),
                   ("q", 1, cols(w_in, COL_Q), "proj_mm", 16), ("dftI", 2, T["const_dft_i"], "inv_mm", 4),
                   ("k", 3, cols(w_in, COL_K), "proj_mm", 20), ("v", 0, cols(w_in, COL_V), "proj_mm", 24),
                   ("z", 1, cols(w_in, COL_Z), "proj_mm", 28), ("ga0", 0, cols(w_in, COL_G), "proj_mm", 32),
                   ("upa", 2, T["w_up_a"].rearrange("(k p) n -> p k n", p=P), "up_mm", 8),
                   ("upb", 3, T["w_up_b"].rearrange("(k p) n -> p k n", p=P), "up_mm", 8),
                   ("gb0", 1, cols(w_in, COL_G + 1024), "proj_mm", 36),
                   ("ga1", 0, cols(w_in, COL_G + 512), "proj_mm", 40), ("gb1", 1, cols(w_in, COL_G + 1536), "proj_mm", 44),
                   ("out0", 2, cols(w_out, 0), "out_mm", 10), ("out1", 3, cols(w_out, 512), "out_mm", 10)]
        CH, last_use, fills = {}, [None] * 6, [0] * 6
        loads = []
        for name, s, src, used, value in chunks:
            loads.append((s, src, last_use[s]))
            fills[s] += 1
            CH[name] = (s, 16 * fills[s])
            last_use[s] = (used, value)

        CONV = 24
        rows_of = (SEQ_S, FREQ_C)

        block = ctx.enter_context(nc.Block())

        @block.sync
        def _(sp):
            for s, src, before in loads:
                if before:
                    sp.wait_ge(sem(before[0]), before[1])
                dst = slot(s)
                if src.shape[-1] != SLOT:
                    dst = wslot(s, src.shape[1])
                sp.dma_start(dst, src).then_inc(slot_full[s], 16)
            w_e = [T[w].rearrange("e (k p) n -> p (e k) n", p=P) for w in ("w_e_gate", "w_e_up", "w_e_down")]

            def load(e, s):
                src = w_e[s // 2][:, bass.ds(e * KB, KB), 512 * (s % 2):512 * (s % 2) + 512]
                sp.dma_start(wslot(s), src).then_inc(slot_full[s], 16)

            for s in range(6):
                sp.wait_ge(sem(last_use[s][0]), last_use[s][1])
                if s == 4:
                    sp.wait_ge(sem("router_mm"), 1)
                load(0, s)
            with sp.Fori(1, E) as e:
                for s in range(6):
                    if s < 4:
                        sp.wait_ge(sem("gu_mm"), e * 2 - (1 if s < 2 else 0))
                    else:
                        sp.wait_ge(sem("down_mm"), e)
                    load(e, s)

        def spread_gate(pe, mm, which):
            for c in range(2):
                pe.wait_ge(sem("diag"), 16 * which + KB * (c + 1))
                for k in range(KB):
                    i = mm(bank[4 + 2 * c + k // 4][:, P * (k % 4):P * (k % 4) + P], ones, diag[:, c, k, :])
                i.then_inc(sem("spread_mm"), 1)

        def delta_pe(pe, mm):
            tri = (C("tri_f"), C("tri_b"))
            for p in range(NT):
                def dve(r, step):
                    pe.wait_ge(sem(f"dn_dve{r}"), DVE_N * p + DVE[step])

                def act(r, step):
                    pe.wait_ge(sem(f"dn_act{r}"), ACT_N * p + ACTS[step])

                def heads(r, b, f):
                    for hh in range(HEADS):
                        i = f(hh, bank[4 * r + b][:, P * hh:P * hh + P])
                    return i

                def cols_of(r, src, hh):
                    return src[:, hh, P * TILE[r][p]:P * TILE[r][p] + P]

                for r in range(2):
                    gcol = d_g.rearrange("p (t x) -> p t x", t=NT)[:, TILE[r][p], :]
                    if p:
                        pe.wait_ge(sem(f"dn_dve{r}"), DVE_N * p)
                    heads(r, 3, lambda hh, o: mm(o, gcol[:, 4 * r + hh:4 * r + hh + 1].to_broadcast([P, P]), tri[r])) \
                        .then_inc(sem(f"dn_pe{r}"), 1)
                    heads(r, 0, lambda hh, o: mm(o, cols_of(r, kT, hh), cols_of(r, kT, hh))).then_inc(sem(f"dn_pe{r}"), 1)
                    heads(r, 1, lambda hh, o: mm(o, cols_of(r, kT, hh), cols_of(r, qT, hh))).then_inc(sem(f"dn_pe{r}"), 1)
                    heads(r, 2, lambda hh, o: pe.transpose(o, cols_of(r, kT, hh), ident)).then_inc(sem(f"dn_pe{r}"), 1)
                for r in range(2):
                    dve(r, "LT")
                    heads(r, 0, lambda hh, o: pe.transpose(o, dLnT[r][:, hh, :], ident)).then_inc(sem(f"dn_pe{r}"), 1)
                for lev in range(1, LEVELS):
                    for r in range(2):
                        dve(r, f"P{lev - 1}")
                        heads(r, 0, lambda hh, o: mm(o, dLnT[r][:, hh, :], dM[r][:, hh, :])).then_inc(sem(f"dn_pe{r}"), 1)
                    for r in range(2):
                        act(r, f"W{lev}")
                        if lev < LEVELS - 1:
                            heads(r, 1, lambda hh, o: mm(o, dU[r][:, hh, :], dW[r][:, hh, :]))
                        heads(r, 2, lambda hh, o: mm(o, dW[r][:, hh, :], dU[r][:, hh, :])).then_inc(sem(f"dn_pe{r}"), 1)
                for r in range(2):
                    dve(r, f"P{LEVELS - 1}")
                    act(r, "KD")
                    heads(r, 3, lambda hh, o: mm(o, dKG[r][:, hh, :], dU[r][:, hh, :])).then_inc(sem(f"dn_pe{r}"), 1)
                for r in range(2):
                    act(r, "WT")
                    if p == 0:
                        pe.wait_ge(sem("state_in"), 32)
                    for hh in range(HEADS):
                        o = bank[4 * r][:, P * hh:P * hh + P]
                        mm(o, dU[r][:, hh, :], vtok[:, TILE[r][p], P * hh:P * hh + P], 0, 2)
                        i = mm(o, dWT[r][:, hh, :], state[r][:, hh, :], 1, 2)
                    i.then_inc(sem(f"dn_pe{r}"), 1)
                for r in range(2):
                    dve(r, "VN")
                    for hh in range(HEADS):
                        o = bank[4 * r + 1][:, P * hh:P * hh + P]
                        mm(o, state[r][:, hh, :], dQG[r][:, hh, :], 0, 2)
                        mm(o, dVN[r][:, hh, :], dAT[r][:, hh, :], 1, 2)
                    heads(r, 2, lambda hh, o: mm(o, dKD[r][:, hh, :], dVN[r][:, hh, :])).then_inc(sem(f"dn_pe{r}"), 1)

        @block.tensor
        def _(pe):
            def mm(out, lhsT, rhs, k=0, n=1):
                return pe.matmul(out, lhsT, rhs, start=(k == 0), stop=(k == n - 1))

            def full(name):
                pe.wait_ge(slot_full[CH[name][0]], CH[name][1])

            def spectrum(table, src, read, per_output):
                for j in range(FT + 1):
                    A, B = bank[4 + 2 * (j % 2)], bank[5 + 2 * (j % 2)]
                    if j >= 2:
                        pe.wait_ge(sem(read), per_output * (j - 1))
                    for out, cs in ((A, 0), (B, 1)):
                        if j < FT:
                            for t in range(ST):
                                at = 2 * FREQ_S * t + FREQ_S * cs + P * j
                                i = mm(out[:, :], table[:, at:at + P], src[:, t, :], t, ST)
                        else:
                            at = 2 * FREQ_S * ST + FREQ_C * cs
                            i = mm(out[0:FREQ_C, :], table[:, at:at + FREQ_C], src[:, ST, :])
                    i.then_inc(sem("spec_mm"), 1)

            def transpose_tokens(src, ready, read):
                for k in range(KB):
                    if k >= 2:
                        pe.wait_ge(sem(read), 2 * (k - 1))
                    for t in range(ST):
                        pe.transpose(bank[2 + k % 2][:, P * t:P * t + P], src[:, t, P * k:P * k + P], ident)
                    pe.transpose(bank[k % 2][:, 0:P], src[:, ST, P * k:P * k + P], ident).then_inc(sem(ready), 1)

            pe.wait_ge(sem("loaded"), 48)
            for layer, (w, rows) in enumerate((("hy_w1", HY_EMB), ("hy_w2", 64))):
                rhs = feats if layer == 0 else hid[0]
                if layer:
                    pe.wait_ge(sem("hid"), 1)
                mm(bank[2 * layer][0:64, :], K(w)[0:rows, :], rhs[0:rows, 0:SEQ_S])
                mm(bank[2 * layer + 1][0:64, 0:SEQ_C], K(w)[0:rows, :], rhs[0:rows, SEQ_S:TOK]).then_inc(sem("hid_mm"), 1)
            pe.wait_ge(sem("hid"), 2)
            for t in range(NT):
                mm(bank[4 + t if t < 4 else 0][:, :], hid[1][:, P * t:P * t + P], K("hy_w3")[0:64, :]).then_inc(sem("filt_mm"), 1)
            for t in range(NT):
                pe.wait_ge(sem("filt_abs"), t + 1)
                i = mm(bank[1 if t < ST else 2][:, :], ones, absf[:, t, :], t % ST, ST if t < ST else 1)
            i.then_inc(sem("filt_sum"), 1)
            full("dftF0")
            spectrum(slot(CH["dftF0"][0]), filt, "fspec", 2)

            pe.wait_ge(sem("cond"), 2)
            mod_cols = (3, 5, 8)
            for g in range(3):
                for j in range(4):
                    full(f"mod{4 * g + j}")
                if g == 0:
                    pe.wait_ge(sem("filtnorm"), 4)
                for k in range(KB):
                    for j in range(4):
                        i = mm(bank[g][32 * j:32 * j + 32, :], cond32[:, k, :], wslot(CH[f"mod{4 * g + j}"][0])[:, k, :], k, KB)
                i.then_inc(sem("mod_mm"), 1)
                pe.wait_ge(sem("mod_row"), g + 1)
                if g:
                    pe.wait_ge(sem("mod_col"), mod_cols[g - 1])
                else:
                    pe.wait_ge(sem("fspec"), 8)
                for i in range(4):
                    tr = pe.transpose(bank[7][:, P * i:P * i + P], modrow[:, P * i:P * i + P], ident)
                tr.then_inc(sem("mod_tr"), 1)
            pe.wait_ge(sem("xn"), NT)
            transpose_tokens(xn, "xnT_mm", "uT")

            done = [0]

            def project(name):
                s = CH[name][0]
                full(name)
                for b in range(4):
                    n = done[0]
                    if 2 <= n < CONV + 2:
                        pe.wait_ge(sem("conv"), 4 * (n - 1))
                    elif n >= CONV + 2:
                        pe.wait_ge(sem("zg"), 2 * (n - 1 - CONV))
                    for k in range(KB):
                        mm(bank[n % 2][:, :], wslot(s)[:, k, P * b:P * b + P], uT[:, k, 0:SEQ_S], k, KB)
                        i = mm(bank[2 + n % 2][:, 0:SEQ_C], wslot(s)[:, k, P * b:P * b + P], uT[:, k, SEQ_S:TOK], k, KB)
                    i.then_inc(sem("proj_mm"), 1)
                    done[0] += 1

            pe.wait_ge(sem("uT"), 2 * KB)
            project("hyx1")
            project("hyv")
            project("hyx0")
            pe.wait_ge(sem("uu"), 4)
            for t in range(NT):
                if t >= 2:
                    pe.wait_ge(sem("uutok"), t - 1)
                for cb in range(4):
                    i = pe.transpose(bank[4 + t % 2][:, P * cb:P * cb + P], uuT[:, cb, P * t:P * t + P], ident)
                i.then_inc(sem("uutok_mm"), 1)
            project("q")
            pe.wait_ge(sem("uutok"), NT)
            full("dftF1")
            spectrum(slot(CH["dftF1"][0]), uuTok, "product", 6)
            project("k")
            full("dftI")
            inv = slot(CH["dftI"][0])
            pe.wait_ge(sem("product"), 6 * (FT + 1))
            for cb in range(4):
                A, B = bank[4 + 2 * (cb % 2)], bank[5 + 2 * (cb % 2)]
                if cb >= 2:
                    pe.wait_ge(sem("yb"), 3 * (cb - 1))
                for j in range(2 * FT):
                    mm(A[:, :], uspec[:, j, P * cb:P * cb + P], inv[:, 512 * j:512 * j + 512], j, 2 * FT)
                for j in range(2):
                    at = 2 * FT * 512 + SEQ_C * j
                    i = mm(B[:, 0:SEQ_C], uspec[0:FREQ_C, 2 * FT + j, P * cb:P * cb + P], inv[0:FREQ_C, at:at + SEQ_C], j, 2)
                i.then_inc(sem("inv_mm"), 1)
            project("v")

            pe.wait_ge(sem("yb"), 12)
            wba = K("w_ba").rearrange("p (k n) -> p k n", k=KB)
            for k in range(KB):
                mm(bank[4][0:16, :], wba[:, k, :], uT[:, k, 0:SEQ_S], k, KB)
                i = mm(bank[5][0:16, 0:SEQ_C], wba[:, k, :], uT[:, k, SEQ_S:TOK], k, KB)
            i.then_inc(sem("ba_mm"), 1)
            pe.wait_ge(sem("ba_row"), 2)
            for t in range(NT):
                i = pe.transpose(bank[6][:, 16 * t:16 * t + 16], barow[0:16, P * t:P * t + P], ident[0:16, 0:16])
            i.then_inc(sem("ba_tr"), 1)
            pe.wait_ge(sem("dec"), DEC_G)
            gv = d_g.rearrange("p (t x) -> p t x", t=NT)
            mm(bank[7][:, 0:20], C("tri_f"), gv[:, :, 0:4])
            mm(bank[7][:, 32:52], C("tri_b"), gv[:, :, 4:8])
            mm(bank[7][:, 64:104], ones, d_g).then_inc(sem("gc_mm"), 1)
            for n in range(8):
                pe.wait_ge(sem("sq"), n + 1)
                if n >= 2:
                    pe.wait_ge(sem("norm_root"), 2 * (n - 1))
                elif n == 0:
                    pe.wait_ge(sem("conv"), 4 * CONV)
                mm(bank[n % 2][:, :], ones, sq[n % 2][:, 0:SEQ_S])
                mm(bank[2 + n % 2][:, 0:SEQ_C], ones, sq[n % 2][:, SEQ_S:TOK]).then_inc(sem("norm_mm"), 1)
            pe.wait_ge(sem("qkv_act"), 12)
            for t in range(NT):
                if t >= 2:
                    pe.wait_ge(sem("vtok"), t - 1)
                for hd_ in range(HEADS):
                    i = pe.transpose(bank[4 + t % 2][:, P * hd_:P * hd_ + P], vT[:, hd_, P * t:P * t + P], ident)
                i.then_inc(sem("vtok_mm"), 1)
            pe.wait_ge(sem("vtok"), NT)
            pe.wait_ge(sem("dec"), DEC_ALL)
            pe.wait_ge(sem("qk_normal"), 16)
            delta_pe(pe, mm)

            pe.wait_ge(sem("dn_dve1"), DVE_N * NT)
            pe.wait_ge(sem("dn_dve0"), DVE_N * NT)
            project("z")
            pe.wait_ge(sem("dn_act1"), ACT_N * NT)
            for n in range(HEADS):
                pe.wait_ge(sem("osq"), n + 1)
                if n >= 2:
                    pe.wait_ge(sem("onorm_root"), 2 * (n - 1))
                mm(bank[4 + n % 2][:, :], ones, sq[n % 2][:, 0:SEQ_S])
                mm(bank[6 + n % 2][:, 0:SEQ_C], ones, sq[n % 2][:, SEQ_S:TOK]).then_inc(sem("onorm_mm"), 1)
            for half in range(2):
                if half:
                    pe.wait_ge(sem("mixed"), 20)
                project(f"ga{half}")
                project(f"gb{half}")
                if half == 0:
                    full("upa")
                    full("upb")
                    pe.wait_ge(sem("og"), 2 * HEADS)
                    pe.wait_ge(sem("onorm_root"), 2 * HEADS)
                for b in range(4):
                    n = 4 * half + b
                    if b == 1:
                        pe.wait_ge(sem("zg"), 2 * (12 + 8 * half))
                    if n >= 2:
                        pe.wait_ge(sem("mixed"), 5 * (n - 1))
                    banks = (4, 5, 6, 7) if n % 2 == 0 else (0, 2, 1, 3)
                    for w, src, A, B in (("upa", oG, banks[0], banks[1]), ("upb", ybT, banks[2], banks[3])):
                        for k in range(4):
                            lw = wslot(CH[w][0], 4)[:, k, P * n:P * n + P]
                            mm(bank[A][:, :], lw, src[:, k, 0:SEQ_S], k, 4)
                            i = mm(bank[B][:, 0:SEQ_C], lw, src[:, k, SEQ_S:TOK], k, 4)
                    i.then_inc(sem("up_mm"), 1)
            pe.wait_ge(sem("mixed"), 5 * KB)
            spread_gate(pe, mm, 0)
            pe.wait_ge(sem("gate_row"), 4)
            full("out0")
            full("out1")
            for t in range(NT):
                for c in range(2):
                    n = 2 * t + c
                    if n >= 4:
                        pe.wait_ge(sem("out_read"), n - 3)
                    for k in range(KB):
                        i = mm(bank[n % 4][:, :], mixedT[:, k, P * t:P * t + P], wslot(CH[f"out{c}"][0])[:, k, :], k, KB)
                    i.then_inc(sem("out_mm"), 1)
            pe.wait_ge(sem("xn2"), NT)
            transpose_tokens(xn2, "xn2T_mm", "u2T")
            pe.wait_ge(sem("u2T"), 2 * KB)
            wr = K("w_router").rearrange("p (k n) -> p k n", k=KB)
            for k in range(KB):
                mm(bank[4][0:16, :], wr[:, k, :], u2T[:, k, 0:SEQ_S], k, KB)
                i = mm(bank[5][0:16, 0:SEQ_C], wr[:, k, :], u2T[:, k, SEQ_S:TOK], k, KB)
            i.then_inc(sem("router_mm"), 1)
            pe.wait_ge(sem("logit_row"), 2)
            for t in range(NT):
                i = pe.transpose(bank[2][:, 16 * t:16 * t + 16], rrow[:, P * t:P * t + P], ident[0:16, 0:16])
            i.then_inc(sem("logit_tr"), 1)
            pe.wait_ge(sem("probs"), 1)
            for t in range(NT):
                i = pe.transpose(bank[6 + t // 4][0:16, P * (t % 4):P * (t % 4) + P], probs[:, t, 0:E], ident)
            i.then_inc(sem("prob_tr"), 1)
            pe.wait_ge(sem("slot_row"), 1)
            for t in range(NT):
                i = pe.transpose(bank[5][:, 16 * t:16 * t + 16], rrow[:, P * t:P * t + P], ident[0:16, 0:16])
            i.then_inc(sem("slot_tr"), 1)

            def gather(n):
                pe.wait_ge(sem("onehot"), 5 * n + 5)
                for t in range(ST):
                    for half in range(2):
                        mm(bank[3][64 * half:64 * half + 64, :], Gs[:, t, :], xn2[:, t, 512 * half:512 * half + 512], t, ST)
                for q in range(4):
                    i = mm(bank[4][32 * q:32 * q + 32, 0:256], Gc, xn2[:, ST, 256 * q:256 * q + 256])
                i.then_inc(sem("gather_mm"), 1)

            def gather_transpose(n):
                pe.wait_ge(sem("gathered"), 2 * n + 2)
                for j in range(4):
                    pe.transpose(bank[3][:, P * j:P * j + P], xs[:, P * j:P * j + P], ident)
                for j in range(2):
                    i = pe.transpose(bank[4][:, P * j:P * j + P], xsc[:, P * j:P * j + P], ident)
                i.then_inc(sem("xT_mm"), 1)

            pe.wait_ge(sem("slots"), 2)
            gather(0)
            gather_transpose(0)
            with pe.Fori(0, E) as e:
                pe.wait_ge(sem("xT"), e * 4 + 4)
                pe.wait_ge(sem("yadd"), e * 12 + 1)
                for which, out, outc in ((0, bank[0], bank[2][:, 0:256]), (1, bank[1], bank[5][:, 256:512])):
                    for half in range(2):
                        pe.wait_ge(slot_full[2 * which + half], e * 16 + (16 * fills[2 * which + half] + 16))
                    for k in range(KB):
                        for half in range(2):
                            mm(out[64 * half:64 * half + 64, :], xsT[:, k, :], wslot(2 * which + half)[:, k, :], k, KB)
                    for k in range(KB):
                        for q in range(4):
                            i = mm(outc[32 * q:32 * q + 32, :], xcT[:, k, :],
                                   wslot(2 * which + q // 2)[:, k, 256 * (q % 2):256 * (q % 2) + 256], k, KB)
                    i.then_inc(sem("gu_mm"), 1)
                gather(e + 1)
                pe.wait_ge(sem("weighted"), e * 5 + 5)
                for t in range(ST):
                    pe.transpose(bank[6][:, P * t:P * t + P], GA[:, t, :], ident)
                pe.wait_ge(sem("hid_e"), e * 2 + 2)
                for j in range(4):
                    pe.transpose(bank[5][:, P * j:P * j + P], hd[:, P * j:P * j + P], ident)
                for j in range(2):
                    i = pe.transpose(bank[7][:, P * j:P * j + P], hdc[:, P * j:P * j + P], ident)
                i.then_inc(sem("hidT_mm"), 1)
                pe.wait_ge(sem("gathered"), e * 2 + 4)
                pe.transpose(bank[4][:, 0:P], GAc, ident).then_inc(sem("ct_mm"), 1)
                pe.wait_ge(sem("hidT"), e * 2 + 2)
                for half in range(2):
                    pe.wait_ge(slot_full[4 + half], e * 16 + (16 * fills[4 + half] + 16))
                for k in range(KB):
                    for half in range(2):
                        mm(bank[7][64 * half:64 * half + 64, :], hdT[:, k, :], wslot(4 + half)[:, k, :], k, KB)
                for k in range(KB):
                    for q in range(4):
                        i = mm(bank[5][32 * q:32 * q + 32, 0:256], hdcT[:, k, :],
                               wslot(4 + q // 2)[:, k, 256 * (q % 2):256 * (q % 2) + 256], k, KB)
                i.then_inc(sem("down_mm"), 1)
                pe.wait_ge(sem("ct"), e * 2 + 2)
                gather_transpose(e + 1)
                pe.wait_ge(sem("ys"), e * 2 + 2)
                for t in range(ST):
                    if t >= 2:
                        pe.wait_ge(sem("yadd"), e * 12 + (1 + 2 * (t - 1)))
                    for half in range(2):
                        i = mm(bank[SCATTER_BANKS[t % 2][half]][:, :], CT[64 * half:64 * half + 64, t, :],
                               ys[64 * half:64 * half + 64, :])
                    i.then_inc(sem("scatter_mm"), 1)
                pe.wait_ge(sem("yadd"), e * 12 + 7)
                for q in range(4):
                    i = mm(bank[(2, 6, 5, 7)[q]][:, 0:256], CTc[32 * q:32 * q + 32, :], ysc[32 * q:32 * q + 32, :])
                i.then_inc(sem("scatter_mm"), 1)
            pe.wait_ge(sem("yadd"), 1 + 12 * E)
            spread_gate(pe, mm, 1)

        @block.scalar
        def _(act):
            A = nc.scalar.activation
            act.dma_start(ck[:, :], T["const_ck"]).then_inc(sem("loaded"), 16)
            act.dma_start(pk[:, :], T["packed"]).then_inc(sem("loaded"), 16)
            act.dma_start(feats, T["const_feats"]).then_inc(sem("loaded"), 16)
            act.dma_start(h[:, 0:ST, :], T["x_sample"].rearrange("(t p) d -> p t d", p=P)).then_inc(sem("x_in"), 16)
            act.dma_start(h[:, ST, :], T["x_prompt"]).then_inc(sem("x_in"), 16)
            act.dma_start(posc, T["pos_col"]).then_inc(sem("x_in"), 16)
            act.dma_start(posr, T["pos_row"]).then_inc(sem("x_in"), 16)
            act.wait_ge(sem("loaded"), 48)
            for t in range(NT):
                A(filt[:, t, :], feats[:, TOK:TOK + 512], ACT.Exp, scale=C("offset")[:, t:t + 1]).then_inc(sem("window"), 1)
            for n in range(2):
                act.wait_ge(sem("sin_arg"), 9 * (n + 1))
                A(hid[n], sin_arg, ACT.Sin).then_inc(sem("hid"), 1)
            act.wait_ge(sem("cond"), 1)
            A(cond32[:, :, 0:2], K("cond").rearrange("p (k c) -> p k c", k=KB), ACT.Silu).then_inc(sem("cond"), 1)
            for t in range(NT):
                act.wait_ge(sem("filt"), t + 1)
                A(absf[:, t, :], filt[:, t, :], ACT.Abs).then_inc(sem("filt_abs"), 1)
            act.wait_ge(sem("moments"), NT)
            A(rstd, mv[:, :, 1], ACT.Sqrt, bias=eps_ln).then_inc(sem("root"), 1)
            act.wait_ge(sem("h"), 2)
            act.dma_start(h_spill.rearrange("p (t d) -> p t d", t=NT), h).then_inc(sem("spilled"), 16)

            def modulate(dst, mm_done, out, sc, sh):
                for k in range(KB):
                    act.wait_ge(sem(mm_done), k + 1)
                    for c, (b, a, n) in enumerate(((2 + k % 2, 0, SEQ_S), (k % 2, SEQ_S, SEQ_C))):
                        A(dst[:, k, a:a + n], bank[b][:, 0:n], ACT.Identity, bias=modT[:, 48 * c + sh + k:48 * c + sh + k + 1],
                          scale=modT[:, 48 * c + sc + k:48 * c + sc + k + 1]).then_inc(sem(out), 1)

            act.wait_ge(sem("mod_col"), 8)
            modulate(uT, "xnT_mm", "uT", 8, 0)

            conv_dst = [x1T] * 4 + [uuT] * 4 + [x0T] * 4 + [qT] * 4 + [kT] * 4 + [vT] * 4

            def tap(n):
                act.wait_ge(sem("proj_mm"), n + 1)
                if n == 12:
                    act.wait_ge(sem("spilled"), 16)
                if n < 12:
                    w = K("conv_b").rearrange("p (b j) -> p b j", j=3)[:, HY_BLOCK[n], 1:2]
                    bias = K("conv_bb")[:, HY_BLOCK[n]:HY_BLOCK[n] + 1]
                else:
                    w, bias = K("conv_a").rearrange("p (b j) -> p b j", j=3)[:, n - 12, 1:2], 0.0
                d = conv_dst[n][:, n % 4, :]
                A(d[:, 0:SEQ_S], bank[n % 2][:, :], ACT.Identity, bias=bias, scale=w).then_inc(sem("tap"), 1)
                A(d[:, SEQ_S:TOK], bank[2 + n % 2][:, 0:SEQ_C], ACT.Identity, bias=bias, scale=w).then_inc(sem("tap"), 1)

            def silu(n):
                act.wait_ge(sem("conv"), 4 * (n + 1))
                d = conv_dst[n][:, n % 4, :]
                A(d, d, ACT.Silu).then_inc(sem("qkv_act"), 1)

            for n in range(12):
                tap(n)
            for t in range(NT):
                act.wait_ge(sem("uutok_mm"), t + 1)
                A(uuTok[:, t, :], bank[4 + t % 2][:, :], ACT.Copy).then_inc(sem("uutok"), 1)
            for n in range(12, CONV):
                tap(n)
                if n > 12:
                    silu(n - 1)
            silu(CONV - 1)
            b6 = bank[6][:, 0:80].rearrange("p (t x) -> p t x", t=NT)
            act.wait_ge(sem("ba_tr"), 1)
            act.wait_ge(sem("dec"), 1)
            A(d_tmp.rearrange("p (t x) -> p t x", t=NT), b6[:, :, 0:8], ACT.Exp, scale=-1.0).then_inc(sem("dec_act"), 1)
            A(d_expa[:, 0:8], K("a_log"), ACT.Exp).then_inc(sem("dec_act"), 1)
            act.wait_ge(sem("dec"), DEC_NEG)
            A(d_neg, d_neg, ACT.Exp).then_inc(sem("dec_act"), 1)
            act.wait_ge(sem("dec_act"), 3)
            A(d_neg, d_neg, ACT.Ln, bias=1.0).then_inc(sem("dec_act"), 1)
            act.wait_ge(sem("dec"), DEC_GC)
            A(d_negegc, d_gc, ACT.Exp).then_inc(sem("dec_act"), 1)
            A(d_edk, d_edk, ACT.Exp).then_inc(sem("dec_act"), 1)
            A(d_egl, d_tot, ACT.Exp).then_inc(sem("dec_act"), 1)
            for n in range(9):
                if n < 8:
                    src = (qT if n < 4 else kT)[:, n % 4, :]
                    if n >= 2:
                        act.wait_ge(sem("norm_mm"), n - 1)
                    else:
                        act.wait_ge(sem("qkv_act"), 12)
                    A(sq[n % 2], src, ACT.Square).then_inc(sem("sq"), 1)
                if n >= 1:
                    m = n - 1
                    act.wait_ge(sem("norm_mm"), m + 1)
                    if m >= 2:
                        act.wait_ge(sem("qk_normal"), 2 * (m - 1))
                    scale, bias = (float(P), eps_q) if m < 4 else (1.0, eps_k)
                    A(rn[m % 2][:, 0:SEQ_S], bank[m % 2][:, :], ACT.Sqrt, bias=bias, scale=scale).then_inc(sem("norm_root"), 1)
                    A(rn[m % 2][:, SEQ_S:TOK], bank[2 + m % 2][:, 0:SEQ_C], ACT.Sqrt, bias=bias, scale=scale).then_inc(sem("norm_root"), 1)
            for t in range(NT):
                act.wait_ge(sem("vtok_mm"), t + 1)
                A(vtok[:, t, :], bank[4 + t % 2][:, :], ACT.Copy).then_inc(sem("vtok"), 1)

            for p in range(NT):
                def pe_(r, step):
                    act.wait_ge(sem(f"dn_pe{r}"), PE_N * p + PES[step])

                def dve_(r, step):
                    act.wait_ge(sem(f"dn_dve{r}"), DVE_N * p + DVE[step])

                def bank4(r, b):
                    return bank[4 * r + b][:, :].rearrange("p (h c) -> p h c", h=HEADS)

                if p == 0:
                    act.wait_ge(sem("qk_normal"), 16)
                    act.wait_ge(sem("inv_mm"), 4)
                    for r, name in enumerate(("state_delta_fwd", "state_delta_bwd")):
                        act.dma_start(state[r], T[name].rearrange("h k v -> k h v")).then_inc(sem("state_in"), 16)
                for r in range(2):
                    pe_(r, "R")
                    A(dQG[r], bank4(r, 3), ACT.Exp).then_inc(sem(f"dn_act{r}"), 1)
                for r in range(2):
                    dve_(r, "E")
                    A(dD[r], dD[r], ACT.Exp).then_inc(sem(f"dn_act{r}"), 1)
                for r in range(2):
                    pe_(r, "KT")
                    for hh in range(HEADS):
                        x = 8 * TILE[r][p] + 4 * r + hh
                        A(dKG[r][:, hh, :], bank[4 * r + 2][:, P * hh:P * hh + P], ACT.Copy, scale=d_negegc[:, x:x + 1]) \
                            .then_inc(sem(f"dn_act{r}"), 1)
                    for hh in range(HEADS):
                        x = 8 * TILE[r][p] + 4 * r + hh
                        A(dKD[r][:, hh, :], bank[4 * r + 2][:, P * hh:P * hh + P], ACT.Copy, scale=d_edk[:, x:x + 1]) \
                            .then_inc(sem(f"dn_act{r}"), 1)
                for lev in range(1, LEVELS):
                    for r in range(2):
                        pe_(r, f"W{lev}")
                        A(dW[r], bank4(r, 0), ACT.Copy).then_inc(sem(f"dn_act{r}"), 1)
                for r in range(2):
                    pe_(r, "WT")
                    A(dWT[r], bank4(r, 3), ACT.Copy).then_inc(sem(f"dn_act{r}"), 1)
                if p == NT - 1:
                    for r in range(2):
                        dve_(r, "ST")
                        act.dma_start(O[2 + r].rearrange("h k v -> k h v"), state[r]).then_inc(sem("out_done"), 16)

            def gate(n, f, dst):
                act.wait_ge(sem("proj_mm"), n + 1)
                A(dst[:, 0:SEQ_S], bank[n % 2][:, :], f).then_inc(sem("zg"), 1)
                A(dst[:, SEQ_S:TOK], bank[2 + n % 2][:, 0:SEQ_C], f).then_inc(sem("zg"), 1)

            for n in range(4):
                gate(CONV + n, ACT.Silu, zT[:, n, :])
            act.wait_ge(sem("out_done"), 32)
            for n in range(HEADS + 1):
                if n < HEADS:
                    if n >= 2:
                        act.wait_ge(sem("onorm_mm"), n - 1)
                    A(sq[n % 2], oT[:, n, :], ACT.Square).then_inc(sem("osq"), 1)
                if n >= 1:
                    m = n - 1
                    act.wait_ge(sem("onorm_mm"), m + 1)
                    if m >= 2:
                        act.wait_ge(sem("og"), 2 * (m - 1))
                    A(rn[m % 2][:, 0:SEQ_S], bank[4 + m % 2][:, :], ACT.Sqrt, bias=eps_k, scale=1.0 / P).then_inc(sem("onorm_root"), 1)
                    A(rn[m % 2][:, SEQ_S:TOK], bank[6 + m % 2][:, 0:SEQ_C], ACT.Sqrt, bias=eps_k, scale=1.0 / P).then_inc(sem("onorm_root"), 1)
            act.wait_ge(sem("og"), 2 * HEADS)
            act.dma_start(h, h_spill.rearrange("p (t d) -> p t d", t=NT)).then_inc(sem("h_back"), 16)
            for half in range(2):
                for b in range(8):
                    gate(CONV + 4 + 8 * half + b, ACT.Sigmoid, sig[:, b, :])
            act.wait_ge(sem("mixed"), 5 * KB)
            for j, w in enumerate(("ln1_g", "ln1_b")):
                act.dma_start(lnrow[:, j, :], T[w].to_broadcast([P, D])).then_inc(sem("ln1_in"), 16)
            for t in range(NT):
                for j in range(2):
                    act.wait_ge(sem("moments1"), 2 * t + j + 1)
                    A(rstd[:, t:t + 1], mv[:, t, 1:2], ACT.Sqrt, bias=eps_ln).then_inc(sem("root1"), 1)
            modulate(u2T, "xn2T_mm", "u2T", 32, 24)
            act.wait_ge(sem("logits"), 3)
            lg = probs[:, :, 0:E]
            A(lg, lg, ACT.Exp).then_inc(sem("exp_logits"), 1)

            def copy_gathered(n):
                act.wait_ge(sem("gather_mm"), n + 1)
                A(xs, bank[3][:, :], ACT.Copy).then_inc(sem("gathered"), 1)
                A(xsc, bank[4][:, 0:256], ACT.Copy).then_inc(sem("gathered"), 1)

            def by_block(b, width, n):
                return bank[b][:, 0:P * n].rearrange("p (j h s) -> p h j s", j=n, s=width)

            copy_gathered(0)
            with act.Fori(0, E) as e:
                act.wait_ge(sem("gu_mm"), e * 2 + 1)
                A(sil, bank[0][:, :], ACT.Silu).then_inc(sem("sil"), 1)
                A(silc, bank[2][:, 0:256], ACT.Silu).then_inc(sem("sil"), 1)
                copy_gathered(e + 1)
                act.wait_ge(sem("hidT_mm"), e + 1)
                A(hdT.rearrange("p (h j) s -> p h j s", h=2), by_block(5, 64, 4), ACT.Copy).then_inc(sem("hidT"), 1)
                A(hdcT.rearrange("p (h j) s -> p h j s", h=4), by_block(7, 32, 2), ACT.Copy).then_inc(sem("hidT"), 1)
                act.wait_ge(sem("ct_mm"), e + 1)
                A(CT, bank[6][:, :].rearrange("p (t c) -> p t c", t=ST), ACT.Copy).then_inc(sem("ct"), 1)
                A(CTc, bank[4][:, 0:P], ACT.Copy).then_inc(sem("ct"), 1)
                act.wait_ge(sem("down_mm"), e + 1)
                A(ys, bank[7][:, :], ACT.Copy).then_inc(sem("ys"), 1)
                A(ysc, bank[5][:, 0:256], ACT.Copy).then_inc(sem("ys"), 1)
            for j, w in enumerate(("ln2_g", "ln2_b")):
                act.dma_start(ln2row[:, j, :], T[w].to_broadcast([P, D])).then_inc(sem("ln2_in"), 16)
            for t in range(NT):
                act.wait_ge(sem("moments2"), t + 1)
                A(rstd[:, t:t + 1], mv[:, t, 1:2], ACT.Sqrt, bias=eps_ln).then_inc(sem("root2"), 1)
                act.wait_ge(sem("y"), t + 1)
                act.dma_start(O[1][P * t:P * t + P, :] if t < ST else O[0], h[:, t, :]).then_inc(sem("out_done"), 16)
            act.wait_ge(sem("out_done"), 16 * (2 + NT))

        @block.vector
        def _(dve):
            V = nc.vector

            class Stage:
                def __init__(self, name):
                    self.sem, self.n = sem(name), 0

                def add(self, ins):
                    ins.then_inc(self.sem, 1)
                    self.n += 1

                def settle(self):
                    dve.wait_ge(self.sem, self.n)

            dve.wait_ge(sem("loaded"), 48)
            V.memset(misc[:, 2432:2688], 0.0).then_inc(sem("cond"), 1)
            s = Stage("sin_arg")
            for layer in range(2):
                dve.wait_ge(sem("hid_mm"), layer + 1)
                if layer:
                    dve.wait_ge(sem("hid"), 1)
                for b, a, n in ((2 * layer, 0, SEQ_S), (2 * layer + 1, SEQ_S, SEQ_C)):
                    s.add(V.tensor_scalar(sin_arg[:, a:a + n], bank[b][0:64, 0:n], K("hy_b1" if layer == 0 else "hy_b2")[0:64, :],
                                          K("hy_freq")[0:64, :], ALU.add, ALU.mult))
                s.settle()
                s.add(V.tensor_scalar(sin_n, sin_arg, 1.0 / (2.0 * math.pi), MAGIC, ALU.mult, ALU.add))
                s.settle()
                s.add(V.tensor_scalar(sin_n, sin_n, -MAGIC, None, ALU.add))
                for part in TWO_PI:
                    s.settle()
                    s.add(V.scalar_tensor_tensor(sin_arg, sin_n, -part, sin_arg, ALU.mult, ALU.add))
                s.settle()
                s.add(V.tensor_scalar(sin_arg, sin_arg, PI_BELOW, -PI_BELOW, ALU.min, ALU.max))
                s.settle()
                s.add(V.engine_nop())
            s = Stage("filt")
            dve.wait_ge(sem("window"), NT)
            for t in range(NT):
                dve.wait_ge(sem("filt_mm"), t + 1)
                s.add(V.tensor_tensor(filt[:, t, :], bank[4 + t if t < 4 else 0][:, :], filt[:, t, :], ALU.mult))
            dve.wait_ge(sem("filt_sum"), 1)
            s = Stage("filtnorm")
            for j in range(2):
                s.add(V.tensor_scalar(filtnorm[:, j, :], bank[1 + j][:, :], 1e-6, None, ALU.add))
            s.settle()
            for j in range(2):
                s.add(V.reciprocal(filtnorm[:, j, :], filtnorm[:, j, :]))
            hs = Stage("h")
            dve.wait_ge(sem("x_in"), 64)
            hs.add(V.tensor_tensor(h[:, 0:ST, 0:512], h[:, 0:ST, 0:512], posr, ALU.add))
            hs.add(V.tensor_tensor(h[:, 0:ST, 512:D], h[:, 0:ST, 512:D], posc.unsqueeze(1).to_broadcast([P, ST, 512]), ALU.add))
            hs.settle()
            bs, ms = Stage("bn"), Stage("moments")

            def moments(t, src, stage):
                for j in range(2):
                    bs.add(V.bn_stats(bn[:, t, 6 * j:6 * j + 6], src[:, 512 * j:512 * j + 512]))
                bs.settle()
                stage.add(V.bn_aggr(mv[:, t, :], bn[:, t, :]))

            for t in range(NT):
                moments(t, h[:, t, :], ms)
            rs, xs_ = Stage("rstd"), Stage("xn")
            dve.wait_ge(sem("root"), 1)
            rs.add(V.reciprocal(rstd, rstd))
            rs.settle()
            for t in range(NT):
                xs_.add(V.tensor_scalar(xn[:, t, :], h[:, t, :], mv[:, t, 0:1], rstd[:, t:t + 1], ALU.subtract, ALU.mult))
            s = Stage("fspec")
            dve.wait_ge(sem("filtnorm"), 4)
            for j in range(FT + 1):
                dve.wait_ge(sem("spec_mm"), j + 1)
                r = P if j < FT else FREQ_C
                for cs in range(2):
                    s.add(V.tensor_tensor(fspec[0:r, 2 * j + cs, :], bank[4 + 2 * (j % 2) + cs][0:r, :],
                                          filtnorm[0:r, j // FT, :], ALU.mult))
            ms2 = Stage("mod_col")
            for g in range(3):
                dve.wait_ge(sem("mod_mm"), g + 1)
                V.tensor_copy(modrow, bank[g][:, :]).then_inc(sem("mod_row"), 1)
                dve.wait_ge(sem("mod_tr"), g + 1)
                src = bank[7][:, :].rearrange("p (i j x) -> p j i x", i=4, j=4)
                for c in range(2):
                    ms2.add(V.tensor_tensor(modT[:, 48 * c + 16 * g:48 * c + 16 * g + 16].rearrange("p (j i) -> p j i", j=4),
                                            src[:, :, :, c],
                                            K("b_mod")[:, 16 * g:16 * g + 16].rearrange("p (j i) -> p j i", j=4), ALU.add))
                if g != 1:
                    ms2.settle()
                    b = 8 if g == 0 else 32
                    v = modT[:, :].rearrange("p (c b) -> p c b", c=2)[:, :, b:b + 8]
                    ms2.add(V.tensor_scalar(v, v, 1.0, None, ALU.add))
            cs_ = Stage("conv")
            conv_dst = [x1T] * 4 + [uuT] * 4 + [x0T] * 4 + [qT] * 4 + [kT] * 4 + [vT] * 4

            def conv(n):
                dve.wait_ge(sem("tap"), 2 * (n + 1))
                w = K("conv_b" if n < 12 else "conv_a").rearrange("p (b j) -> p b j", j=3)[:, HY_BLOCK[n] if n < 12 else n - 12, :]
                d = conv_dst[n][:, n % 4, :]
                for tap_, shift in ((0, 1), (2, -1)):
                    if tap_:
                        cs_.settle()
                    for b, a, l in ((n % 2, 0, SEQ_S), (2 + n % 2, SEQ_S, SEQ_C)):
                        o = (1, l) if shift == 1 else (0, l - 1)
                        out = d[:, a + o[0]:a + o[1]]
                        cs_.add(V.scalar_tensor_tensor(out, bank[b][:, o[0] - shift:o[1] - shift], w[:, tap_:tap_ + 1], out,
                                                       ALU.mult, ALU.add))

            us = Stage("uu")
            for n in range(12):
                conv(n)
                if 4 <= n < 8:
                    cs_.settle()
                    us.add(V.tensor_tensor(uuT[:, n - 4, :], x1T[:, n - 4, :], uuT[:, n - 4, :], ALU.mult))
            for n in range(12, 16):
                conv(n)
            s = Stage("product")
            for j in range(FT + 1):
                dve.wait_ge(sem("spec_mm"), FT + 1 + j + 1)
                r = P if j < FT else FREQ_C
                a, b = (bank[4 + 2 * (j % 2) + cs][0:r, :] for cs in range(2))
                fc, fs = (fspec[0:r, 2 * j + cs, :] for cs in range(2))
                s.add(V.tensor_tensor(uspec[0:r, 2 * j, :], a, fc, ALU.mult))
                s.add(V.tensor_tensor(ptmp[0:r, 0, :], b, fs, ALU.mult))
                s.add(V.tensor_tensor(uspec[0:r, 2 * j + 1, :], a, fs, ALU.mult))
                s.add(V.tensor_tensor(ptmp[0:r, 1, :], b, fc, ALU.mult))
                s.settle()
                s.add(V.tensor_tensor(uspec[0:r, 2 * j, :], uspec[0:r, 2 * j, :], ptmp[0:r, 0, :], ALU.subtract))
                s.add(V.tensor_tensor(uspec[0:r, 2 * j + 1, :], uspec[0:r, 2 * j + 1, :], ptmp[0:r, 1, :], ALU.add))
                s.settle()
            for n in range(16, 20):
                conv(n)
            s = Stage("yb")
            for cb in range(4):
                dve.wait_ge(sem("inv_mm"), cb + 1)
                for b, a, l in ((4 + 2 * (cb % 2), 0, SEQ_S), (5 + 2 * (cb % 2), SEQ_S, SEQ_C)):
                    s.add(V.scalar_tensor_tensor(uuT[:, cb, a:a + l], uuT[:, cb, a:a + l], K("skip")[:, cb:cb + 1],
                                                 bank[b][:, 0:l], ALU.mult, ALU.add))
                s.settle()
                s.add(V.tensor_tensor(x0T[:, cb, :], x0T[:, cb, :], uuT[:, cb, :], ALU.mult))
            for n in range(20, CONV):
                conv(n)
            dve.wait_ge(sem("ba_mm"), 1)
            V.tensor_copy(barow[0:16, 0:SEQ_S], bank[4][0:16, :]).then_inc(sem("ba_row"), 1)
            V.tensor_copy(barow[0:16, SEQ_S:TOK], bank[5][0:16, 0:SEQ_C]).then_inc(sem("ba_row"), 1)
            s = Stage("dec")

            def tx(v):
                return v.rearrange("p (t x) -> p t x", t=NT)

            dve.wait_ge(sem("ba_tr"), 1)
            s.add(V.tensor_tensor(tx(d_xa), bank[6][:, 0:80].rearrange("p (t x) -> p t x", t=NT)[:, :, 8:16],
                                  K("dt_bias").unsqueeze(1).to_broadcast([P, NT, 8]), ALU.add))
            s.settle()
            s.add(V.tensor_scalar(d_relu, d_xa, 0.0, None, ALU.max))
            s.add(V.tensor_scalar(d_neg, d_xa, -1.0, None, ALU.mult))
            s.settle()
            s.add(V.tensor_tensor(d_neg, d_neg, d_xa, ALU.min))
            dve.wait_ge(sem("dec_act"), 2)
            s.add(V.tensor_scalar(d_tmp, d_tmp, 1.0, None, ALU.add))
            s.settle()
            s.add(V.reciprocal(d_beta, d_tmp))
            s.settle()
            s.add(V.tensor_scalar(d_negbeta, d_beta, -1.0, None, ALU.mult))
            dve.wait_ge(sem("dec_act"), 4)
            s.add(V.tensor_tensor(d_relu, d_relu, d_neg, ALU.add))
            s.settle()
            s.add(V.scalar_tensor_tensor(tx(d_g), tx(d_relu), -1.0, d_expa[:, 0:8].unsqueeze(1).to_broadcast([P, NT, 8]),
                                         ALU.mult, ALU.mult))
            dve.wait_ge(sem("gc_mm"), 1)
            s.add(V.tensor_copy(tx(d_gc)[:, :, 0:4], bank[7][:, 0:20].rearrange("p (t x) -> p t x", t=NT)))
            s.add(V.tensor_copy(tx(d_gc)[:, :, 4:8], bank[7][:, 32:52].rearrange("p (t x) -> p t x", t=NT)))
            s.add(V.tensor_copy(d_tot, bank[7][:, 64:104]))
            s.settle()
            s.add(V.tensor_tensor(d_edk, d_tot, d_gc, ALU.subtract))
            dve.wait_ge(sem("dec_act"), 7)
            s.add(V.tensor_scalar(d_negegc, d_negegc, -1.0, None, ALU.mult))
            s = Stage("qk_normal")
            rs = Stage("rn")
            for n in range(8):
                dve.wait_ge(sem("norm_root"), 2 * (n + 1))
                rs.add(V.reciprocal(rn[n % 2], rn[n % 2]))
                rs.settle()
                d = (qT if n < 4 else kT)[:, n % 4, :]
                s.add(V.tensor_tensor(d, d, rn[n % 2], ALU.mult))
                s.add(V.engine_nop())

            neg = (C("neg_f"), C("neg_b"))
            masks = tuple(C(m).bitcast(U32).rearrange("p (l c) -> p l c", l=LEVELS) for m in ("mask_lo", "mask_up"))
            ds = [Stage("dn_dve0"), Stage("dn_dve1")]
            first = [True] * NT
            for p in range(NT):
                def pe_(r, step):
                    dve.wait_ge(sem(f"dn_pe{r}"), PE_N * p + PES[step])

                def act_(r, step):
                    dve.wait_ge(sem(f"dn_act{r}"), ACT_N * p + ACTS[step])

                def bank4(r, b):
                    return bank[4 * r + b][:, :].rearrange("p (h c) -> p h c", h=HEADS)

                def x(r, hh):
                    return 8 * TILE[r][p] + 4 * r + hh

                def blend(r, lev, which, data):
                    m = masks[(r + which) % 2][:, lev, :].unsqueeze(1).to_broadcast([P, HEADS, P])
                    return V.copy_predicated((dM, dU)[which][r], m, data)

                for r in range(2):
                    act_(r, "EG")
                    for hh in range(HEADS):
                        ds[r].add(V.scalar_tensor_tensor(dD[r][:, hh, :], bank[4 * r + 3][:, P * hh:P * hh + P],
                                                         d_gc[:, x(r, hh):x(r, hh) + 1], neg[r], ALU.subtract, ALU.add))
                for r in range(2):
                    for w in (dM, dU):
                        ds[r].add(V.tensor_copy(w[r], ident.unsqueeze(1).to_broadcast([P, HEADS, P])))
                    act_(r, "D")
                    pe_(r, "KK")
                    for hh in range(HEADS):
                        ds[r].add(V.scalar_tensor_tensor(dLnT[r][:, hh, :], bank[4 * r][:, P * hh:P * hh + P],
                                                         d_negbeta[:, x(r, hh):x(r, hh) + 1], dD[r][:, hh, :], ALU.mult, ALU.mult))
                for r in range(2):
                    pe_(r, "QK")
                    ds[r].add(V.tensor_tensor(dAT[r], bank4(r, 1), dD[r], ALU.mult))
                    t = TILE[r][p]
                    ds[r].add(V.tensor_tensor(dQG[r], qT[:, :, P * t:P * t + P], dQG[r], ALU.mult))
                for r in range(2):
                    ds[r].settle()
                    ds[r].add(blend(r, 0, 1, dLnT[r]))
                    pe_(r, "LN")
                    ds[r].add(blend(r, 0, 0, bank4(r, 0)))
                for lev in range(1, LEVELS):
                    for r in range(2):
                        pe_(r, f"MU{lev}")
                        ds[r].settle()
                        if lev < LEVELS - 1:
                            ds[r].add(blend(r, lev, 0, bank4(r, 1)))
                        ds[r].add(blend(r, lev, 1, bank4(r, 2)))
                for r in range(2):
                    pe_(r, "V")
                    for hh in range(HEADS):
                        ds[r].add(V.tensor_scalar(dVN[r][:, hh, :], bank[4 * r][:, P * hh:P * hh + P],
                                                  d_beta[:, x(r, hh):x(r, hh) + 1], None, ALU.mult))
                for r in range(2):
                    pe_(r, "OS")
                    t = TILE[r][p]
                    o = oT[:, :, P * t:P * t + P]
                    if r:
                        dve.wait_ge(sem("dn_dve0"), ds[0].n)
                    else:
                        dve.wait_ge(sem("dn_dve1"), ds[1].n)
                    if first[t]:
                        ds[r].add(V.tensor_copy(o, bank4(r, 1)))
                        first[t] = False
                    else:
                        ds[r].add(V.tensor_tensor(o, bank4(r, 1), o, ALU.add))
                    if p == ST - 1:
                        ds[r].add(V.memset(state[r], 0.0))
                        for _i in range(3):
                            ds[r].add(V.engine_nop())
                    else:
                        if p == 0:
                            dve.wait_ge(sem("state_in"), 32)
                        for hh in range(HEADS):
                            ds[r].add(V.scalar_tensor_tensor(state[r][:, hh, :], state[r][:, hh, :], d_egl[:, x(r, hh):x(r, hh) + 1],
                                                             bank[4 * r + 2][:, P * hh:P * hh + P], ALU.mult, ALU.add))
                    assert ds[r].n == DVE_N * (p + 1), (ds[r].n, DVE_N)

            s = Stage("og")
            rs2 = rs
            dve.wait_ge(sem("zg"), 8)
            for n in range(HEADS):
                dve.wait_ge(sem("onorm_root"), 2 * (n + 1))
                rs2.add(V.reciprocal(rn[n % 2], rn[n % 2]))
                rs2.settle()
                s.add(V.scalar_tensor_tensor(oG[:, n, :], oT[:, n, :], K("gnorm"), rn[n % 2], ALU.mult, ALU.mult))
                s.settle()
                s.add(V.tensor_tensor(oG[:, n, :], oG[:, n, :], zT[:, n, :], ALU.mult))
            s = Stage("mixed")
            for n in range(KB):
                dve.wait_ge(sem("zg"), 2 * (12 + 8 * (n // 4)))
                dve.wait_ge(sem("up_mm"), n + 1)
                banks = (4, 5, 6, 7) if n % 2 == 0 else (0, 2, 1, 3)
                if n:
                    s.settle()
                s.add(V.tensor_tensor(mixedT[:, n, 0:SEQ_S], bank[banks[0]][:, :], sig[:, n % 4, 0:SEQ_S], ALU.mult))
                s.add(V.tensor_tensor(mixedT[:, n, SEQ_S:TOK], bank[banks[1]][:, 0:SEQ_C], sig[:, n % 4, SEQ_S:TOK], ALU.mult))
                s.add(V.tensor_tensor(uptmp[:, 0:SEQ_S], bank[banks[2]][:, :], sig[:, 4 + n % 4, 0:SEQ_S], ALU.mult))
                s.add(V.tensor_tensor(uptmp[:, SEQ_S:TOK], bank[banks[3]][:, 0:SEQ_C], sig[:, 4 + n % 4, SEQ_S:TOK], ALU.mult))
                s.settle()
                s.add(V.tensor_tensor(mixedT[:, n, :], mixedT[:, n, :], uptmp, ALU.add))
            s.settle()
            dg = Stage("diag")

            def spread(which, rows):
                for c in range(2):
                    for k in range(KB):
                        b = 48 * c + (16, 40)[which] + k
                        dg.add(V.tensor_scalar(diag[:, c, k, :], ident, modT[:, b:b + 1], None, ALU.mult))
                for c in range(2):
                    dve.wait_ge(sem("spread_mm"), 2 * which + c + 1)
                    for j in range(2):
                        V.tensor_copy(rows[:, c, 512 * j:512 * j + 512], bank[4 + 2 * c + j][:, :]).then_inc(sem("gate_row"), 1)
                dve.wait_ge(sem("gate_row"), 4 * which + 4)

            spread(0, grow)
            dve.wait_ge(sem("h_back"), 16)
            s = Stage("resid1")
            m1, orr, x2 = Stage("moments1"), Stage("out_read"), Stage("xn2")

            def norm(t, src, dst, stage, root, nroot, out):
                moments(t, src, stage)
                dve.wait_ge(sem(root), nroot)
                rs.add(V.reciprocal(rstd[:, t:t + 1], rstd[:, t:t + 1]))
                rs.settle()
                out.add(V.tensor_scalar(dst, src, mv[:, t, 0:1], rstd[:, t:t + 1], ALU.subtract, ALU.mult))

            for t in range(NT):
                c = 0 if t < ST else 1
                for j in range(2):
                    dve.wait_ge(sem("out_mm"), 2 * t + j + 1)
                    orr.add(V.tensor_tensor(otmp[:, t % 2, 512 * j:512 * j + 512], bank[(2 * t + j) % 4][:, :],
                                            grow[:, c, 512 * j:512 * j + 512], ALU.mult))
                orr.settle()
                s.add(V.scalar_tensor_tensor(h[:, t, :], h[:, t, :], ALPHA, otmp[:, t % 2, :], ALU.mult, ALU.add))
                s.settle()
                norm(t, h[:, t, :], h[:, t, :], m1, "root1", 2 * t + 1, s)
                s.settle()
                dve.wait_ge(sem("ln1_in"), 32)
                s.add(V.tensor_tensor(h[:, t, :], h[:, t, :], lnrow[:, 0, :], ALU.mult))
                s.settle()
                s.add(V.tensor_tensor(h[:, t, :], h[:, t, :], lnrow[:, 1, :], ALU.add))
                s.settle()
                norm(t, h[:, t, :], xn2[:, t, :], m1, "root1", 2 * t + 2, x2)
            x2.settle()
            dve.wait_ge(sem("router_mm"), 1)
            V.tensor_copy(rrow[:, 0:SEQ_S], bank[4][0:16, :]).then_inc(sem("logit_row"), 1)
            V.tensor_copy(rrow[:, SEQ_S:TOK], bank[5][0:16, 0:SEQ_C]).then_inc(sem("logit_row"), 1)
            dve.wait_ge(sem("logit_tr"), 1)
            s = Stage("logits")
            b2 = bank[2][:, 0:80].rearrange("p (t e) -> p t e", t=NT)
            s.add(V.tensor_reduce(rmax, b2, AX, ALU.max))
            s.settle()
            s.add(V.tensor_tensor(probs[:, :, 0:E], b2, rmax.unsqueeze(2).to_broadcast([P, NT, E]), ALU.subtract))
            s.add(V.memset(probs[:, :, E:E + 1], 0.0))
            dve.wait_ge(sem("exp_logits"), 1)
            s.add(V.tensor_reduce(rsum, probs[:, :, 0:E], AX, ALU.add))
            s.settle()
            s.add(V.reciprocal(rsum, rsum))
            s.settle()
            V.tensor_tensor(probs[:, :, 0:E], probs[:, :, 0:E], rsum.unsqueeze(2).to_broadcast([P, NT, E]), ALU.mult) \
                .then_inc(sem("probs"), 1)
            s = Stage("topk")
            dve.wait_ge(sem("prob_tr"), 1)
            s.add(V.tensor_copy(rrow[:, 0:SEQ_S], bank[6][0:16, :]))
            s.add(V.tensor_copy(rrow[:, SEQ_S:TOK], bank[7][0:16, 0:SEQ_C]))
            s.settle()
            for a, l, rounds in ((0, SEQ_S, CAP_S // 8), (SEQ_S, SEQ_C, CAP_C // 8)):
                for _r in range(rounds):
                    s.add(V.max(top8, rrow[:, a:a + l]))
                    s.settle()
                    s.add(V.match_replace(rrow[:, a:a + l], top8, rrow[:, a:a + l], -1.0))
                    s.settle()
            s.add(V.tensor_scalar(mask, rrow, 0.0, None, ALU.is_lt))
            s.settle()
            for a, l in ((0, SEQ_S), (SEQ_S, SEQ_C)):
                s.add(V.tensor_tensor_scan(count[:, a:a + l], mask[:, a:a + l], mask[:, a:a + l], 0.0, ALU.add, ALU.max))
            s.settle()
            s.add(V.tensor_tensor(count, count, mask, ALU.mult))
            s.settle()
            V.tensor_scalar(rrow, count, -1.0, None, ALU.add).then_inc(sem("slot_row"), 1)
            dve.wait_ge(sem("slot_tr"), 1)
            V.tensor_copy(slots[:, :, 0:E], bank[5][:, 0:80].rearrange("p (t e) -> p t e", t=NT)).then_inc(sem("slots"), 1)
            V.memset(slots[:, :, E:E + 1], -1.0).then_inc(sem("slots"), 1)
            V.memset(yacc, 0.0).then_inc(sem("yadd"), 1)
            dve.wait_ge(sem("slots"), 2)

            def col(v, t, n):
                return v[:, t, bass.ds(n, 1)]

            def onehot(n):
                for t in range(ST):
                    V.tensor_scalar(Gs[:, t, :], C("iota64")[:, 0:CAP_S], col(slots, t, n), None, ALU.is_equal).then_inc(sem("onehot"), 1)
                V.tensor_scalar(Gc, C("iota32")[:, 0:32], col(slots, ST, n), None, ALU.is_equal).then_inc(sem("onehot"), 1)

            def xT(n):
                dve.wait_ge(sem("xT_mm"), n + 1)
                for stage, op in ((0, ALU.mult), (1, ALU.add)):
                    if stage:
                        dve.wait_ge(sem("xT"), n * 4 + 2)
                    for c, (dst, b, blocks, width, halves) in enumerate(((xsT, 3, 4, CAP_S, 2), (xcT, 4, 2, 32, 4))):
                        src = dst if stage else bank[b][:, 0:P * blocks].rearrange("p (j h s) -> p h j s", j=blocks, s=width)
                        if stage:
                            src = src.rearrange("p (h j) s -> p h j s", h=halves)
                        m = modT[:, 48 * c + (24 if stage else 32):48 * c + (32 if stage else 40)]
                        m = m.rearrange("p (h j) -> p h j", h=halves).unsqueeze(3).to_broadcast([P, halves, blocks, width])
                        V.tensor_tensor(dst.rearrange("p (h j) s -> p h j s", h=halves), src, m, op).then_inc(sem("xT"), 1)

            onehot(0)
            xT(0)
            with dve.Fori(0, E) as e:
                dve.wait_ge(sem("gather_mm"), e + 1)
                dve.wait_ge(sem("onehot"), e * 5 + 5)
                onehot(e + 1)
                for t in range(ST):
                    V.tensor_scalar(GA[:, t, :], C("iota64"), col(slots, t, e), col(probs, t, e), ALU.is_equal, ALU.mult) \
                        .then_inc(sem("weighted"), 1)
                V.tensor_scalar(GAc, C("iota32"), col(slots, ST, e), col(probs, ST, e), ALU.is_equal, ALU.mult) \
                    .then_inc(sem("weighted"), 1)
                dve.wait_ge(sem("sil"), e * 2 + 2)
                dve.wait_ge(sem("gu_mm"), e * 2 + 2)
                V.tensor_tensor(hd, bank[1][:, :], sil, ALU.mult).then_inc(sem("hid_e"), 1)
                V.tensor_tensor(hdc, bank[5][:, 256:512], silc, ALU.mult).then_inc(sem("hid_e"), 1)
                xT(e + 1)
                dve.wait_ge(sem("yadd"), e * 12 + 1)
                for t in range(ST):
                    dve.wait_ge(sem("scatter_mm"), e * 5 + (t + 1))
                    for half in range(2):
                        y = yacc[:, t, 512 * half:512 * half + 512]
                        V.tensor_tensor(y, bank[SCATTER_BANKS[t % 2][half]][:, :], y, ALU.add).then_inc(sem("yadd"), 1)
                dve.wait_ge(sem("scatter_mm"), e * 5 + 5)
                for q in range(4):
                    y = yacc[:, ST, 256 * q:256 * q + 256]
                    V.tensor_tensor(y, bank[(2, 6, 5, 7)[q]][:, 0:256], y, ALU.add).then_inc(sem("yadd"), 1)
            dve.wait_ge(sem("yadd"), 12 * E + 1)
            spread(1, g2row)
            s = Stage("resid2")
            m2 = Stage("moments2")
            for t in range(NT):
                c = 0 if t < ST else 1
                s.add(V.tensor_tensor(yacc[:, t, :], yacc[:, t, :], g2row[:, c, :], ALU.mult))
                s.settle()
                s.add(V.scalar_tensor_tensor(h[:, t, :], h[:, t, :], ALPHA, yacc[:, t, :], ALU.mult, ALU.add))
                s.settle()
                norm(t, h[:, t, :], h[:, t, :], m2, "root2", t + 1, s)
                s.settle()
                dve.wait_ge(sem("ln2_in"), 32)
                s.add(V.tensor_tensor(h[:, t, :], h[:, t, :], ln2row[:, 0, :], ALU.mult))
                s.settle()
                V.tensor_tensor(h[:, t, :], h[:, t, :], ln2row[:, 1, :], ALU.add).then_inc(sem("y"), 1)


def steps(*named):
    out, n = {}, 0
    for name, k in named:
        n += k
        out[name] = n
    return out, n


PES, PE_N = steps(("R", 1), ("KK", 1), ("QK", 1), ("KT", 1), ("LN", 1),
                  *[s for lev in range(1, LEVELS) for s in ((f"W{lev}", 1), (f"MU{lev}", 1))], ("WT", 1), ("V", 1), ("OS", 1))
ACTS, ACT_N = steps(("EG", 1), ("D", 1), ("KG", 4), ("KD", 4), *[(f"W{lev}", 1) for lev in range(1, LEVELS)], ("WT", 1))
DVE, DVE_N = steps(("E", 4), ("LT", 6), ("AT", 1), ("QG", 1), ("P0", 2),
                   *[(f"P{lev}", 2 if lev < LEVELS - 1 else 1) for lev in range(1, LEVELS)], ("VN", 4), ("O", 1), ("ST", 4))
TILE = ((0, 1, 2, 3, 4), (3, 2, 1, 0, 4))
DEC_NEG, DEC_G, DEC_GC, DEC_ALL = 4, 9, 13, 14
HY_BLOCK = (4, 5, 6, 7, 8, 9, 10, 11, 0, 1, 2, 3)
SCATTER_BANKS = ((2, 6), (0, 1))

_INS = ["w_mod", "w_in", "w_up_a", "w_up_b", "w_out", "w_e_gate", "w_e_up", "w_e_down"]


def kernel(**inputs):
    import concourse.bacc as _bacc
    from concourse.bass_utils import run_bass_kernel_spmd as _run

    nc = _bacc.Bacc("TRN2", target_bir_lowering=False, num_devices=1)
    arr = {k: np.ascontiguousarray(v) for k, v in inputs.items()}
    arrays = {k: arr[k][0] for k in _INS + ["x_prompt", "x_sample"]}
    for k in ("state_delta_fwd", "state_delta_bwd"):
        arrays[k] = arr[k][0, 0]
    for k in ("ln1_g", "ln1_b", "ln2_g", "ln2_b"):
        arrays[k] = arr[k]
    pk = np.zeros((P, PK_N), np.float32)

    def put(name, v):
        a, n = PK[name]
        v = v.reshape(v.shape[0], -1)
        pk[0:v.shape[0], a:a + v.shape[1]] = v

    def blocks(v, n):
        return v.reshape(n, P, -1).transpose(1, 0, 2)

    put("cond", blocks(np.stack([arr["c"][0], arr["c_ctx"]], 1), KB))
    put("b_mod", blocks(arr["b_mod"][0], 48))
    put("conv_a", blocks(arr["conv_a_w"][0].T, 12))
    put("conv_b", blocks(arr["conv_b_w"][0].T, 12))
    put("conv_bb", blocks(arr["conv_b_b"][0], 12))
    put("skip", blocks(arr["hy_bias"][0], 4))
    put("gnorm", arr["gnorm_w"][0])
    put("a_log", np.tile(arr["a_log"].reshape(1, 8), (P, 1)))
    put("dt_bias", np.tile(arr["dt_bias"].reshape(1, 8), (P, 1)))
    put("hy_b1", arr["hy_b1"][0])
    put("hy_b2", arr["hy_b2"][0])
    put("hy_freq", arr["hy_freq"][0])
    put("w_router", blocks(arr["w_router"][0], KB))
    put("w_ba", blocks(arr["w_in"][0][:, COL_BA:COL_BA + 16], KB))
    put("hy_w1", arr["hy_w1"][0])
    put("hy_w2", arr["hy_w2"][0])
    put("hy_w3", arr["hy_w3"][0])
    arrays["packed"] = pk
    arrays.update(constants())
    arrays = {k: np.ascontiguousarray(v) for k, v in arrays.items()}
    T = {k: nc.dram_tensor(k + "_dram", v.shape, F32, kind="ExternalInput").ap() for k, v in arrays.items()}
    shapes = {"y_prompt": (1, SEQ_C, D), "y_sample": (1, SEQ_S, D), "state_fwd": (1, 1, HEADS, P, P), "state_bwd": (1, 1, HEADS, P, P)}
    outs = {k: nc.dram_tensor(k + "_out", s, F32, kind="ExternalOutput").ap() for k, s in shapes.items()}
    O = [outs["y_prompt"][0], outs["y_sample"][0], outs["state_fwd"][0, 0], outs["state_bwd"][0, 0]]
    build(nc, T, O)
    r = _run(nc, [{k + "_dram": v for k, v in arrays.items()}], core_ids=[0])
    return tuple(r.results[0][k + "_out"] for k in shapes)
```

```python
from contextlib import ExitStack
import math

import numpy as np
import concourse.bass as bass
from concourse import mybir

F32 = mybir.dt.float32
U32 = mybir.dt.uint32
ALU = mybir.AluOpType
ACT = mybir.ActivationFunctionType
AX = mybir.AxisListType.X

P = 128
D = 1024
KB = D // P
SEQ_S, SEQ_C = 512, 128
TOK = SEQ_S + SEQ_C
NT = TOK // P
ST = SEQ_S // P
HEADS = 4
E = 16
CAP_S, CAP_C = 2 * SEQ_S // E, 2 * SEQ_C // E
ALPHA = 2.0 ** 0.25
HYW = 512
HY_EMB = 33
FREQ_S, FREQ_C = 3 * SEQ_S // 4, 3 * SEQ_C // 4
FT = FREQ_S // P
N_IN = 5648
COL_Q, COL_K, COL_V, COL_Z, COL_BA, COL_HY, COL_G = 0, 512, 1024, 1536, 2048, 2064, 3600
LEVELS = 7
GRID_W = 64

PK = {}
_at = 0
for _name, _n in (("cond", KB * 2), ("b_mod", 48), ("conv_a", 36), ("conv_b", 36), ("conv_bb", 12), ("skip", 4),
                  ("gnorm", 1), ("a_log", 8), ("dt_bias", 8), ("hy_b1", 1), ("hy_b2", 1), ("hy_freq", 1),
                  ("w_router", KB * E), ("w_ba", KB * 16), ("hy_w1", 64), ("hy_w2", 64), ("hy_w3", HYW)):
    PK[_name] = (_at, _n)
    _at += _n
PK_N = _at

CK = {}
_at = 0
for _name, _n in (("ident", P), ("ones", P), ("eps", 4), ("offset", NT), ("iota", CAP_S), ("tri_f", P), ("tri_b", P),
                  ("neg_f", P), ("neg_b", P), ("mask_lo", LEVELS * P), ("mask_up", LEVELS * P)):
    CK[_name] = (_at, _n)
    _at += _n
CK_FIRST = CK["tri_f"][0]
CK_N = _at
FEATS_N = TOK + HYW


def filter_features(l):
    f = np.float32
    t = np.linspace(0.0, 1.0, l, dtype=f)[:, None]
    bands = (HY_EMB - 1) // 2
    w = (f(2.0 * math.pi) * np.arange(l, dtype=f) / f(l))[:, None].astype(f)
    ang = (w * np.linspace(1e-4, bands - 1, bands, dtype=f)[None, :]).astype(f)
    return np.concatenate([t, np.cos(ang), -np.sin(ang)], -1).astype(f).T


def constants():
    ck = np.zeros((P, CK_N), np.float32)

    def put(name, v):
        a, n = CK[name]
        ck[:, a:a + n] = np.asarray(v, np.float32).reshape(P, n)

    i = np.arange(P)
    up = (i[:, None] <= i[None, :])
    put("ident", np.eye(P))
    put("ones", np.ones((P, P)))
    put("tri_f", up)
    put("tri_b", up.T)
    put("neg_f", np.where(up, 0.0, -1e30))
    put("neg_b", np.where(up.T, 0.0, -1e30))
    lo = np.zeros((P, LEVELS, P))
    for lev in range(LEVELS):
        b = 1 << lev
        same = (i[:, None] // (2 * b)) == (i[None, :] // (2 * b))
        lo[:, lev] = same & ((i[:, None] % (2 * b)) >= b) & ((i[None, :] % (2 * b)) < b)
    put("mask_lo", lo)
    put("mask_up", lo.transpose(2, 1, 0))
    put("iota", np.tile(np.arange(CAP_S), (P, 1)))
    put("eps", np.tile([1e-5, 128e-6, 1e-6, 0.0], (P, 1)))
    off = np.concatenate([np.abs(np.arange(l) - l // 2) / (l // 2) for l in (SEQ_S, SEQ_C)])
    put("offset", -off.reshape(NT, P).T)
    feats = np.zeros((P, FEATS_N), np.float32)
    feats[:HY_EMB, 0:SEQ_S] = filter_features(SEQ_S)
    feats[:HY_EMB, SEQ_S:TOK] = filter_features(SEQ_C)
    deltas = np.abs(np.linspace(math.log(1e-2) / 1.5, math.log(1e-2) / 0.3, HYW, dtype=np.float32))
    feats[:, TOK:] = deltas[None, :]

    def dft(l, nf):
        period = 2 * nf
        ang = 2 * np.pi * ((np.arange(nf) + 0.5)[None, :] * np.arange(l)[:, None] % period) / period
        fwd = np.stack([np.cos(ang), np.sin(ang)], 1)
        out = np.arange(l // 2, l // 2 + l)
        ang = 2 * np.pi * ((np.arange(nf) + 0.5)[:, None] * out[None, :] % (2 * period)) / period
        inv = np.stack([np.cos(ang), np.sin(ang)], 1) * (2.0 / period)
        return fwd, inv

    fs, is_ = dft(SEQ_S, FREQ_S)
    fc, ic = dft(SEQ_C, FREQ_C)
    dft_f = np.zeros((P, 4096), np.float32)
    dft_f[:, 0:ST * 2 * FREQ_S] = fs.reshape(ST, P, 2 * FREQ_S).transpose(1, 0, 2).reshape(P, -1)
    dft_f[:, ST * 2 * FREQ_S:ST * 2 * FREQ_S + 2 * FREQ_C] = fc.reshape(P, -1)
    dft_i = np.zeros((P, 4096), np.float32)
    dft_i[:, 0:FT * 2 * SEQ_S] = is_.reshape(FT, P, 2, SEQ_S).transpose(1, 0, 2, 3).reshape(P, -1)
    dft_i[0:FREQ_C, FT * 2 * SEQ_S:FT * 2 * SEQ_S + 2 * SEQ_C] = ic.reshape(FREQ_C, -1)
    quarter = D // 4
    omega = (1.0 / (10000.0 ** (np.arange(quarter, dtype=np.float32) / np.float32(quarter)))).astype(np.float32)

    def enc(n):
        ang = np.arange(n, dtype=np.float32)[:, None] * omega[None, :]
        return np.concatenate([np.sin(ang), np.cos(ang)], -1).astype(np.float32)

    rows = enc(SEQ_S // GRID_W)
    cols = enc(GRID_W)
    token = np.arange(SEQ_S).reshape(ST, P)
    return {"const_ck": ck, "const_feats": feats, "const_dft_f": dft_f, "const_dft_i": dft_i,
            "pos_row": rows[token // GRID_W].transpose(1, 0, 2), "pos_col": cols[np.arange(P) % GRID_W]}


MAGIC = 1.5 * 2.0 ** 23
TWO_PI = (6.28125, 0.0019350051879882812, 3.019916050e-07)
PI_BELOW = 3.1415925


def build(nc, T, O):
    ctx = ExitStack()
    with ctx:
        def sb(name, cols):
            return ctx.enter_context(nc.sbuf_tensor(name, [P, cols], F32))

        sems = {}

        def sem(name):
            if name not in sems:
                sems[name] = ctx.enter_context(nc.semaphore(name))
            return sems[name]

        SLOT = KB * 512
        ring = sb("ring", 4 * SLOT)
        hbuf = sb("hbuf", NT * D)
        front = sb("front", 23040)
        ck = sb("ck", CK_N)
        pk = sb("pk", PK_N)
        modT = sb("modT", 96)
        misc = sb("misc", 2700)
        dec = sb("dec", 13 * 40)
        stats = sb("stats", NT * 12 + NT * 2 + NT + 24)
        bank = [ctx.enter_context(nc.psum_tensor(f"bank{i}", [P, 512], F32)) for i in range(8)]

        def C(name):
            a, n = CK[name]
            return ck[:, a:a + n]

        def K(name):
            a, n = PK[name]
            return pk[:, a:a + n]

        def reg(a, n):
            return front[:, a:a + n]

        ident, ones = C("ident"), C("ones")
        eps_ln, eps_q, eps_k = (C("eps")[:, i:i + 1] for i in range(3))
        bn = stats[:, 0:NT * 12].rearrange("p (t s) -> p t s", t=NT)
        mv = stats[:, NT * 12:NT * 14].rearrange("p (t s) -> p t s", t=NT)
        rstd = stats[:, NT * 14:NT * 15]
        fnorm, fnorm_inv, skip_norm = (stats[:, NT * 15 + 8 * i:NT * 15 + 8 * i + 8] for i in range(3))

        W0 = 12800
        feats = misc[:, 0:FEATS_N]
        hid = [misc[0:64, 1152 + TOK * i:1152 + TOK * (i + 1)] for i in range(2)]
        sin_arg, sin_n = reg(2560, TOK)[0:64], reg(2560 + TOK, TOK)[0:64]
        filt = reg(0, NT * 512).rearrange("p (t c) -> p t c", t=NT)
        absf = reg(2560, NT * 512).rearrange("p (t c) -> p t c", t=NT)
        filtnorm = reg(2560, 1024).rearrange("p (j c) -> p j c", j=2)
        fspec = reg(W0 + 512, 4096).rearrange("p (j c) -> p j c", j=8)
        uspec = reg(W0 + 4608, 4096).rearrange("p (j c) -> p j c", j=8)
        ptmp = reg(W0 + 8704, 1024).rearrange("p (j c) -> p j c", j=2)
        xn = reg(W0 + 5120, 5120).rearrange("p (t d) -> p t d", t=NT)
        posc = reg(W0 + 4608, 512)
        posr = xn.rearrange("p t d -> p (t d)")[:, 0:2048].rearrange("p (t c) -> p t c", t=ST)
        cond32 = misc[:, 2432:2688].rearrange("p (k c) -> p k c", k=KB)
        modrow = misc[:, 1920:2432]
        uT = reg(0, 5120).rearrange("p (k t) -> p k t", k=KB)
        R = [reg(5120 + 2560 * i, 2560).rearrange("p (b t) -> p b t", b=4) for i in range(3)]
        x1T, uuT, x0T = R
        ybT = x0T
        uuTok = reg(5120, 2560).rearrange("p (t c) -> p t c", t=NT)
        h = hbuf[:, :].rearrange("p (t d) -> p t d", t=NT)
        kT = R[0]
        vtok = reg(7680, 2560).rearrange("p (t c) -> p t c", t=NT)
        vT = hbuf[:, 0:2560].rearrange("p (b t) -> p b t", b=4)
        qT = hbuf[:, 2560:5120].rearrange("p (b t) -> p b t", b=4)
        oT = vT
        barow = misc[:, 0:TOK]
        sq = [misc[:, TOK * (1 + i):TOK * (2 + i)] for i in range(2)]
        rn = [reg(W0 + 512 + TOK * i, TOK) for i in range(2)]

        def field(i, n=40):
            return dec[:, 40 * i:40 * i + n]

        (d_tmp, d_beta, d_negbeta, d_xa, d_neg, d_relu, d_g, d_gc, d_tot, d_negegc, d_edk, d_egl, d_expa) = (
            field(i) for i in range(13))

        def dw(r, i):
            return reg(W0 + 4608 * r + 512 * i, 512).rearrange("p (h c) -> p h c", h=HEADS)

        dD, dLnT, dAT, dKG, dKD, dQG, dM, dU, dVN = ([dw(r, i) for r in range(2)] for i in range(9))
        dW, dWT = dD, dLnT
        state = [reg(W0 + 9216 + 512 * r, 512).rearrange("p (h v) -> p h v", h=HEADS) for r in range(2)]
        zT, oG = R[0], R[1]
        sig = reg(W0, 5120).rearrange("p (b t) -> p b t", b=8)
        mixedT = reg(W0 + 5120, 5120).rearrange("p (b t) -> p b t", b=KB)
        uptmp = misc[:, 0:TOK]
        diag = misc[:, 0:2048].rearrange("p (c k f) -> p c k f", c=2, k=KB)
        grow = reg(W0, 2048).rearrange("p (c d) -> p c d", c=2)
        lnrow = reg(W0 + 2048, 2048).rearrange("p (j d) -> p j d", j=2)
        otmp = reg(10240, 2048).rearrange("p (j d) -> p j d", j=2)
        xn2 = reg(0, 5120).rearrange("p (t d) -> p t d", t=NT)
        u2T = reg(5120, 5120).rearrange("p (k t) -> p k t", k=KB)
        GA = reg(13312, ST * E * CAP_S).rearrange("p (t c) -> p t c", t=ST)
        GAc = reg(13312 + ST * E * CAP_S, E * CAP_C)
        EW = 18432
        diag2 = reg(EW, 2048).rearrange("p (c k f) -> p c k f", c=2, k=KB)
        rrow, mask, count = (reg(EW + 2048 + TOK * i, TOK)[0:16, :] for i in range(3))
        top8 = reg(EW + 2048 + 3 * TOK, 8)[0:16, :]
        g2row = misc[:, 640:2688].rearrange("p (c d) -> p c d", c=2)
        probs = dec[:, 0:85].rearrange("p (t e) -> p t e", t=NT)
        slots = dec[:, 85:170].rearrange("p (t e) -> p t e", t=NT)
        rmax, rsum = dec[:, 170:175], dec[:, 175:180]

        def ew(a, n, groups=0):
            v = reg(EW + a, n)
            return v.rearrange("p (g c) -> p g c", g=groups) if groups else v

        xs, xsc = ew(0, 512), ew(512, 256)
        xsT, xcT = ew(768, 512, 8), ew(1280, 256, 8)
        sil, silc = ew(1536, 512), ew(2048, 256)
        hd, hdc = ew(2304, 512), ew(2816, 256)
        hdT, hdcT = ew(3072, 512, 8), ew(3584, 256, 8)
        ys, ysc = ew(3840, 512), ew(4352, 256)
        Gs = misc[:, 0:256].rearrange("p (t c) -> p t c", t=ST)
        Gc = misc[:, 256:288]
        PAIRS = E * CAP_S // P
        ysAll = ring[:, 0:PAIRS * D].rearrange("p (j d) -> p j d", j=PAIRS)
        yscAll = ring[:, 2 * SLOT:2 * SLOT + 2 * D].rearrange("p (j d) -> p j d", j=2)
        ln2row = ring[:, 2 * SLOT + 2 * D:3 * SLOT].rearrange("p (j d) -> p j d", j=2)
        CT = ring[:, 3 * SLOT:4 * SLOT].rearrange("p (j t) -> p j t", j=PAIRS)
        CTc = reg(11264, 256).rearrange("p (j t) -> p j t", j=2)
        ytmp = reg(5120, 2048).rearrange("p (j d) -> p j d", j=2)

        ys_dram = nc.dram_tensor("ys_dram", [E * CAP_S, D], F32, kind="Internal").ap()
        ysc_dram = nc.dram_tensor("ysc_dram", [E * CAP_C, D], F32, kind="Internal").ap()
        h_spill = nc.dram_tensor("h_spill", [P, NT * D], F32, kind="Internal").ap()

        def slot(s):
            return ring[:, s * SLOT:(s + 1) * SLOT] if s < 4 else reg(5120 + (s - 4) * SLOT, SLOT)

        def wslot(s, k=KB):
            return slot(s).rearrange("p (k n) -> p k n", k=k)

        slot_full = [sem(f"slot_full{i}") for i in range(6)]
        w_in = T["w_in"].rearrange("(k p) n -> p k n", p=P)
        w_mod = T["w_mod"].rearrange("(k p) n -> p k n", p=P)
        w_out = T["w_out"].rearrange("(k p) n -> p k n", p=P)

        def cols(w, c):
            return w[:, :, c:c + 512]

        chunks = [("dftF0", 0, T["const_dft_f"], "spec_mm", 4)]
        chunks += [(f"mod{n}", (1, 2, 4, 5)[n], cols(w_mod, 512 * n), "mod_mm", 1) for n in range(4)]

        def mod(n, s):
            return (f"mod{n}", s, cols(w_mod, 512 * n), "mod_mm", n - 2)

        chunks += [("hyx1", 3, cols(w_in, COL_HY + 512), "proj_mm", 4), mod(4, 1), ("hyv", 2, cols(w_in, COL_HY + 1024), "proj_mm", 8),
                   mod(5, 0), ("hyx0", 1, cols(w_in, COL_HY), "proj_mm", 12), mod(6, 3), ("q", 2, cols(w_in, COL_Q), "proj_mm", 16),
                   mod(7, 0), ("dftF1", 1, T["const_dft_f"], "spec_mm", 8), ("k", 3, cols(w_in, COL_K), "proj_mm", 20),
                   mod(8, 2), ("dftI", 0, T["const_dft_i"], "inv_mm", 4), ("v", 1, cols(w_in, COL_V), "proj_mm", 24),
                   mod(9, 3), mod(10, 2), ("z", 0, cols(w_in, COL_Z), "proj_mm", 28), mod(11, 1),
                   ("ga0", 3, cols(w_in, COL_G), "proj_mm", 32), ("gb0", 1, cols(w_in, COL_G + 1024), "proj_mm", 36),
                   ("upa", 2, T["w_up_a"].rearrange("(k p) n -> p k n", p=P), "up_mm", 8),
                   ("upb", 0, T["w_up_b"].rearrange("(k p) n -> p k n", p=P), "up_mm", 8),
                   ("ga1", 3, cols(w_in, COL_G + 512), "proj_mm", 40), ("gb1", 1, cols(w_in, COL_G + 1536), "proj_mm", 44),
                   ("out0", 2, cols(w_out, 0), "out_mm", 10), ("out1", 0, cols(w_out, 512), "out_mm", 10)]
        CH, last_use, fills = {}, [None] * 6, [0] * 6
        loads = []
        for name, s, src, used, value in chunks:
            loads.append((s, src, last_use[s]))
            fills[s] += 1
            CH[name] = (s, 16 * fills[s])
            last_use[s] = (used, value)

        CONV = 24
        rows_of = (SEQ_S, FREQ_C)

        block = ctx.enter_context(nc.Block())

        @block.sync
        def _(sp):
            sp.dma_start(pk[:, :], T["packed"]).then_inc(sem("loaded"), 16)
            sp.dma_start(feats[0:HY_EMB, 0:TOK], T["const_feats"][0:HY_EMB, 0:TOK]).then_inc(sem("loaded"), 16)
            sp.dma_start(feats[:, TOK:], T["const_feats"][:, TOK:]).then_inc(sem("loaded"), 16)
            sp.dma_start(ck[:, 0:CK_FIRST], T["const_ck"][:, 0:CK_FIRST]).then_inc(sem("loaded"), 16)
            for n, (s, src, before) in enumerate(loads):
                if before:
                    sp.wait_ge(sem(before[0]), before[1])
                dst = slot(s)
                if src.shape[-1] != SLOT:
                    dst = wslot(s, src.shape[1])
                sp.dma_start(dst, src).then_inc(slot_full[s], 16)
                if n == 0:
                    sp.dma_start(h[:, 0:ST, :], T["x_sample"].rearrange("(t p) d -> p t d", p=P)).then_inc(sem("x_in"), 16)
                    sp.dma_start(h[:, ST, :], T["x_prompt"]).then_inc(sem("x_in"), 16)
                    sp.dma_start(posc, T["pos_col"]).then_inc(sem("x_in"), 16)
                    sp.dma_start(posr, T["pos_row"]).then_inc(sem("x_in"), 16)
                if n == 4:
                    sp.dma_start(ck[:, CK_FIRST:], T["const_ck"][:, CK_FIRST:]).then_inc(sem("loaded_delta"), 16)
            w_e = [T[w].rearrange("e (k p) n -> p (e k) n", p=P) for w in ("w_e_gate", "w_e_up", "w_e_down")]

            def load(e, s):
                src = w_e[s // 2][:, bass.ds(e * KB, KB), 512 * (s % 2):512 * (s % 2) + 512]
                sp.dma_start(wslot(s), src).then_inc(slot_full[s], 16)

            for s in range(6):
                sp.wait_ge(sem(last_use[s][0]), last_use[s][1])
                if s == 4:
                    sp.wait_ge(sem("router_mm"), 1)
                load(0, s)
            with sp.Fori(1, E) as e:
                for s in range(6):
                    if s < 4:
                        sp.wait_ge(sem("gu_mm"), e * 2 - (1 if s < 2 else 0))
                    else:
                        sp.wait_ge(sem("down_mm"), e)
                    load(e, s)
            sp.wait_ge(sem("gu_mm"), 2 * E)
            sp.dma_start(ln2row[:, 0, :], T["ln2_g"].to_broadcast([P, D])).then_inc(sem("ln2_in"), 16)
            sp.dma_start(ln2row[:, 1, :], T["ln2_b"].to_broadcast([P, D])).then_inc(sem("ln2_in"), 16)
            ys_rows = ys_dram.rearrange("(j p) d -> p j d", p=P)
            ysc_rows = ysc_dram.rearrange("(j p) d -> p j d", p=P)
            sp.wait_ge(sem("ys"), 2 * E - 1)
            sp.dma_start(ysAll[:, 0:PAIRS - 1, :], ys_rows[:, 0:PAIRS - 1, :]).then_inc(sem("ys_back"), 16)
            sp.dma_start(yscAll[:, 0, :], ysc_rows[:, 0, :]).then_inc(sem("ys_back"), 16)
            sp.wait_ge(sem("ys_out"), 96 * E + 1)
            sp.dma_start(ysAll[:, PAIRS - 1, :], ys_rows[:, PAIRS - 1, :]).then_inc(sem("ys_last"), 16)
            sp.dma_start(yscAll[:, 1, :], ysc_rows[:, 1, :]).then_inc(sem("ys_last"), 16)

        def spread_gate(pe, mm, which):
            for c in range(2):
                pe.wait_ge(sem("diag"), 16 * which + KB * (c + 1))
                for k in range(KB):
                    i = mm(bank[SPREAD_BANKS[which][2 * c + k // 4]][:, P * (k % 4):P * (k % 4) + P], ones,
                           (diag, diag2)[which][:, c, k, :])
                i.then_inc(sem("spread_mm"), 1)

        def delta_pe(pe, mm):
            tri = (C("tri_f"), C("tri_b"))
            for p in range(NT):
                def dve(r, step):
                    pe.wait_ge(sem(f"dn_dve{r}"), DVE_N * p + DVE[step])

                def act(r, step):
                    pe.wait_ge(sem(f"dn_act{r}"), ACT_N * p + ACTS[step])

                def heads(r, b, f):
                    for hh in range(HEADS):
                        i = f(hh, bank[4 * r + b][:, P * hh:P * hh + P])
                    return i

                def cols_of(r, src, hh):
                    return src[:, hh, P * TILE[r][p]:P * TILE[r][p] + P]

                for r in range(2):
                    gcol = d_g.rearrange("p (t x) -> p t x", t=NT)[:, TILE[r][p], :]
                    if p:
                        pe.wait_ge(sem(f"dn_dve{r}"), DVE_N * p)
                    heads(r, 3, lambda hh, o: mm(o, gcol[:, 4 * r + hh:4 * r + hh + 1].to_broadcast([P, P]), tri[r])) \
                        .then_inc(sem(f"dn_pe{r}"), 1)
                    heads(r, 0, lambda hh, o: mm(o, cols_of(r, kT, hh), cols_of(r, kT, hh))).then_inc(sem(f"dn_pe{r}"), 1)
                    heads(r, 1, lambda hh, o: mm(o, cols_of(r, kT, hh), cols_of(r, qT, hh))).then_inc(sem(f"dn_pe{r}"), 1)
                    heads(r, 2, lambda hh, o: pe.transpose(o, cols_of(r, kT, hh), ident)).then_inc(sem(f"dn_pe{r}"), 1)
                for r in range(2):
                    dve(r, "LT")
                    heads(r, 0, lambda hh, o: pe.transpose(o, dLnT[r][:, hh, :], ident)).then_inc(sem(f"dn_pe{r}"), 1)
                for lev in range(1, LEVELS):
                    for r in range(2):
                        dve(r, f"P{lev - 1}")
                        heads(r, 0, lambda hh, o: mm(o, dLnT[r][:, hh, :], dM[r][:, hh, :])).then_inc(sem(f"dn_pe{r}"), 1)
                    for r in range(2):
                        act(r, f"W{lev}")
                        if lev < LEVELS - 1:
                            heads(r, 1, lambda hh, o: mm(o, dU[r][:, hh, :], dW[r][:, hh, :]))
                        heads(r, 2, lambda hh, o: mm(o, dW[r][:, hh, :], dU[r][:, hh, :])).then_inc(sem(f"dn_pe{r}"), 1)
                for r in range(2):
                    dve(r, f"P{LEVELS - 1}")
                    act(r, "KD")
                    heads(r, 3, lambda hh, o: mm(o, dKG[r][:, hh, :], dU[r][:, hh, :])).then_inc(sem(f"dn_pe{r}"), 1)
                for r in range(2):
                    act(r, "WT")
                    if p == 0:
                        pe.wait_ge(sem("state_in"), 32)
                    for hh in range(HEADS):
                        o = bank[4 * r][:, P * hh:P * hh + P]
                        mm(o, dU[r][:, hh, :], vtok[:, TILE[r][p], P * hh:P * hh + P], 0, 2)
                        i = mm(o, dWT[r][:, hh, :], state[r][:, hh, :], 1, 2)
                    i.then_inc(sem(f"dn_pe{r}"), 1)
                for r in range(2):
                    dve(r, "VN")
                    for hh in range(HEADS):
                        o = bank[4 * r + 1][:, P * hh:P * hh + P]
                        mm(o, state[r][:, hh, :], dQG[r][:, hh, :], 0, 2)
                        mm(o, dVN[r][:, hh, :], dAT[r][:, hh, :], 1, 2)
                    heads(r, 2, lambda hh, o: mm(o, dKD[r][:, hh, :], dVN[r][:, hh, :])).then_inc(sem(f"dn_pe{r}"), 1)

        def by_block(b, a, width, n):
            return bank[b][:, a:a + P * n].rearrange("p (j h s) -> p h j s", j=n, s=width)

        @block.tensor
        def _(pe):
            def mm(out, lhsT, rhs, k=0, n=1):
                return pe.matmul(out, lhsT, rhs, start=(k == 0), stop=(k == n - 1))

            def full(name):
                pe.wait_ge(slot_full[CH[name][0]], CH[name][1])

            def spectrum(table, src, read, per_output):
                for j in range(FT + 1):
                    A, B = bank[4 + 2 * (j % 2)], bank[5 + 2 * (j % 2)]
                    if j >= 2:
                        pe.wait_ge(sem(read), per_output * (j - 1))
                    for out, cs in ((A, 0), (B, 1)):
                        if j < FT:
                            for t in range(ST):
                                at = 2 * FREQ_S * t + FREQ_S * cs + P * j
                                i = mm(out[:, :], table[:, at:at + P], src[:, t, :], t, ST)
                        else:
                            at = 2 * FREQ_S * ST + FREQ_C * cs
                            i = mm(out[0:FREQ_C, :], table[:, at:at + FREQ_C], src[:, ST, :])
                    i.then_inc(sem("spec_mm"), 1)

            def transpose_tokens(src, ready, read):
                for k in range(KB):
                    if k >= 2:
                        pe.wait_ge(sem(read), 2 * (k - 1))
                    for t in range(ST):
                        pe.transpose(bank[2 + k % 2][:, P * t:P * t + P], src[:, t, P * k:P * k + P], ident)
                    pe.transpose(bank[k % 2][:, 0:P], src[:, ST, P * k:P * k + P], ident).then_inc(sem(ready), 1)

            pe.wait_ge(sem("loaded"), 64)
            for layer, (w, rows) in enumerate((("hy_w1", HY_EMB), ("hy_w2", 64))):
                rhs = feats if layer == 0 else hid[0]
                if layer:
                    pe.wait_ge(sem("hid"), 1)
                mm(bank[2 * layer][0:64, :], K(w)[0:rows, :], rhs[0:rows, 0:SEQ_S])
                mm(bank[2 * layer + 1][0:64, 0:SEQ_C], K(w)[0:rows, :], rhs[0:rows, SEQ_S:TOK]).then_inc(sem("hid_mm"), 1)
            pe.wait_ge(sem("hid"), 2)
            for t in range(NT):
                mm(bank[4 + t if t < 4 else 0][:, :], hid[1][:, P * t:P * t + P], K("hy_w3")[0:64, :]).then_inc(sem("filt_mm"), 1)
            full("dftF0")
            pe.wait_ge(sem("filt"), NT)
            spectrum(slot(CH["dftF0"][0]), filt, "fspec", 2)
            pe.wait_ge(sem("filt_abs"), NT)
            for t in range(NT):
                i = mm(bank[1 if t < ST else 2][:, :], ones, absf[:, t, :], t % ST, ST if t < ST else 1)
            i.then_inc(sem("filt_sum"), 1)

            pe.wait_ge(sem("cond"), 2)
            for j in range(4):
                full(f"mod{j}")
            for k in range(KB):
                for j in range(4):
                    i = mm(bank[0][32 * j:32 * j + 32, :], cond32[:, k, :], wslot(CH[f"mod{j}"][0])[:, k, :], k, KB)
            i.then_inc(sem("mod_mm"), 1)
            pe.wait_ge(sem("fspec"), 8)

            def mod_transpose(n):
                pe.wait_ge(sem("mod_row"), n + 1)
                if n:
                    pe.wait_ge(sem("mod_col"), 2 * n + 1)
                for i in range(4):
                    tr = pe.transpose(bank[7][:, P * i:P * i + P], modrow[:, P * i:P * i + P], ident)
                tr.then_inc(sem("mod_tr"), 1)

            def mod_product(c, read=None, value=0):
                full(f"mod{c}")
                if read:
                    pe.wait_ge(sem(read), value)
                for k in range(2):
                    for j in range(4):
                        i = mm(bank[6][32 * j:32 * j + 32, :], cond32[:, 2 * j + k, :], wslot(CH[f"mod{c}"][0])[:, 2 * j + k, :], k, 2)
                i.then_inc(sem("mod_mm"), 1)

            pe.wait_ge(sem("norm_row"), 2)
            for j in range(2):
                for cb in range(4):
                    i = pe.transpose(bank[1 + j][:, P * cb:P * cb + P], filtnorm[:, j, P * cb:P * cb + P], ident)
            i.then_inc(sem("norm_tr"), 1)
            mod_transpose(0)
            pe.wait_ge(sem("fnorm"), 2)
            pe.wait_ge(sem("xn"), NT)
            transpose_tokens(xn, "xnT_mm", "uT")

            done = [0]

            def project(name, before={}):
                s = CH[name][0]
                full(name)
                for b in range(4):
                    n = done[0]
                    if b in before:
                        before[b]()
                    if 2 <= n < CONV + 2:
                        pe.wait_ge(sem("conv"), 4 * (n - 1))
                    elif n >= CONV + 2:
                        pe.wait_ge(sem("zg"), 2 * (n - 1 - CONV))
                    for k in range(KB):
                        mm(bank[n % 2][:, :], wslot(s)[:, k, P * b:P * b + P], uT[:, k, 0:SEQ_S], k, KB)
                        i = mm(bank[2 + n % 2][:, 0:SEQ_C], wslot(s)[:, k, P * b:P * b + P], uT[:, k, SEQ_S:TOK], k, KB)
                    i.then_inc(sem("proj_mm"), 1)
                    done[0] += 1

            pe.wait_ge(sem("uT"), 2 * KB)
            project("hyx1", {1: lambda: mod_product(4), 3: lambda: mod_transpose(1)})
            project("hyv", {1: lambda: mod_product(5), 3: lambda: mod_transpose(2)})
            project("hyx0", {1: lambda: mod_product(6), 3: lambda: mod_transpose(3)})
            pe.wait_ge(sem("uu"), 4)
            for t in range(NT):
                if t >= 2:
                    pe.wait_ge(sem("uutok"), t - 1)
                for cb in range(4):
                    i = pe.transpose(bank[4 + t % 2][:, P * cb:P * cb + P], uuT[:, cb, P * t:P * t + P], ident)
                i.then_inc(sem("uutok_mm"), 1)
            project("q", {1: lambda: mod_product(7), 3: lambda: mod_transpose(4)})
            pe.wait_ge(sem("uutok"), NT)
            pe.wait_ge(sem("mod_col"), 11)
            full("dftF1")
            spectrum(slot(CH["dftF1"][0]), uuTok, "product", 6)
            project("k", {1: lambda: mod_product(8, "product", 6 * (FT + 1)), 3: lambda: mod_transpose(5)})
            pe.wait_ge(sem("mod_col"), 13)
            full("dftI")
            inv = slot(CH["dftI"][0])
            pe.wait_ge(sem("product"), 6 * (FT + 1))
            for cb in range(4):
                A, B = bank[4 + 2 * (cb % 2)], bank[5 + 2 * (cb % 2)]
                if cb >= 2:
                    pe.wait_ge(sem("yb"), 4 * (cb - 1))
                for j in range(2 * FT):
                    mm(A[:, :], uspec[:, j, P * cb:P * cb + P], inv[:, 512 * j:512 * j + 512], j, 2 * FT)
                for j in range(2):
                    at = 2 * FT * 512 + SEQ_C * j
                    i = mm(B[:, 0:SEQ_C], uspec[0:FREQ_C, 2 * FT + j, P * cb:P * cb + P], inv[0:FREQ_C, at:at + SEQ_C], j, 2)
                i.then_inc(sem("inv_mm"), 1)
            project("v", {1: lambda: mod_product(9, "yb", 16), 2: lambda: (mod_transpose(6), mod_product(10)), 3: lambda: mod_transpose(7)})

            pe.wait_ge(sem("yb"), 16)
            wba = K("w_ba").rearrange("p (k n) -> p k n", k=KB)
            for k in range(KB):
                mm(bank[4][0:16, :], wba[:, k, :], uT[:, k, 0:SEQ_S], k, KB)
                i = mm(bank[5][0:16, 0:SEQ_C], wba[:, k, :], uT[:, k, SEQ_S:TOK], k, KB)
            i.then_inc(sem("ba_mm"), 1)
            pe.wait_ge(sem("ba_row"), 2)
            for t in range(NT):
                i = pe.transpose(bank[6][:, 16 * t:16 * t + 16], barow[0:16, P * t:P * t + P], ident[0:16, 0:16])
            i.then_inc(sem("ba_tr"), 1)
            pe.wait_ge(sem("dec"), DEC_G)
            gv = d_g.rearrange("p (t x) -> p t x", t=NT)
            pe.wait_ge(sem("loaded_delta"), 16)
            pe.wait_ge(sem("mod_col"), 17)
            mm(bank[7][:, 0:20], C("tri_f"), gv[:, :, 0:4])
            mm(bank[7][:, 32:52], C("tri_b"), gv[:, :, 4:8])
            mm(bank[7][:, 64:104], ones, d_g).then_inc(sem("gc_mm"), 1)
            for n in range(8):
                pe.wait_ge(sem("sq"), n + 1)
                if n >= 2:
                    pe.wait_ge(sem("norm_root"), 2 * (n - 1))
                elif n == 0:
                    pe.wait_ge(sem("conv"), 4 * CONV)
                mm(bank[n % 2][:, :], ones, sq[n % 2][:, 0:SEQ_S])
                mm(bank[2 + n % 2][:, 0:SEQ_C], ones, sq[n % 2][:, SEQ_S:TOK]).then_inc(sem("norm_mm"), 1)
            pe.wait_ge(sem("qkv_act"), 12)
            for t in range(NT):
                if t >= 2:
                    pe.wait_ge(sem("vtok"), t - 1)
                for hd_ in range(HEADS):
                    i = pe.transpose(bank[4 + t % 2][:, P * hd_:P * hd_ + P], vT[:, hd_, P * t:P * t + P], ident)
                i.then_inc(sem("vtok_mm"), 1)
            pe.wait_ge(sem("vtok"), NT)
            pe.wait_ge(sem("dec"), DEC_ALL)
            pe.wait_ge(sem("qk_normal"), 16)
            delta_pe(pe, mm)

            pe.wait_ge(sem("dn_dve1"), DVE_N * NT)
            pe.wait_ge(sem("dn_dve0"), DVE_N * NT)
            project("z", {1: lambda: mod_product(11), 3: lambda: mod_transpose(8)})
            pe.wait_ge(sem("dn_act1"), ACT_N * NT)
            pe.wait_ge(sem("mod_col"), 19)
            for n in range(HEADS):
                pe.wait_ge(sem("osq"), n + 1)
                if n >= 2:
                    pe.wait_ge(sem("onorm_root"), 2 * (n - 1))
                mm(bank[4 + n % 2][:, :], ones, sq[n % 2][:, 0:SEQ_S])
                mm(bank[6 + n % 2][:, 0:SEQ_C], ones, sq[n % 2][:, SEQ_S:TOK]).then_inc(sem("onorm_mm"), 1)
            for half in range(2):
                if half:
                    pe.wait_ge(sem("mixed"), 20)
                project(f"ga{half}")
                project(f"gb{half}")
                if half == 0:
                    full("upa")
                    full("upb")
                    pe.wait_ge(sem("og"), 2 * HEADS)
                    pe.wait_ge(sem("onorm_root"), 2 * HEADS)
                for b in range(4):
                    n = 4 * half + b
                    if b == 1:
                        pe.wait_ge(sem("zg"), 2 * (12 + 8 * half))
                    if n >= 2:
                        pe.wait_ge(sem("mixed"), 5 * (n - 1))
                    banks = (4, 5, 6, 7) if n % 2 == 0 else (0, 2, 1, 3)
                    for w, src, A, B in (("upa", oG, banks[0], banks[1]), ("upb", ybT, banks[2], banks[3])):
                        for k in range(4):
                            lw = wslot(CH[w][0], 4)[:, k, P * n:P * n + P]
                            mm(bank[A][:, :], lw, src[:, k, 0:SEQ_S], k, 4)
                            i = mm(bank[B][:, 0:SEQ_C], lw, src[:, k, SEQ_S:TOK], k, 4)
                    i.then_inc(sem("up_mm"), 1)
            pe.wait_ge(sem("mixed"), 5 * KB)
            spread_gate(pe, mm, 0)
            pe.wait_ge(sem("gate_row"), 4)
            full("out0")
            full("out1")
            for t in range(NT):
                for c in range(2):
                    n = 2 * t + c
                    if n >= 4:
                        pe.wait_ge(sem("out_read"), n - 3)
                    for k in range(KB):
                        i = mm(bank[n % 4][:, :], mixedT[:, k, P * t:P * t + P], wslot(CH[f"out{c}"][0])[:, k, :], k, KB)
                    i.then_inc(sem("out_mm"), 1)
            pe.wait_ge(sem("xn2"), NT)
            transpose_tokens(xn2, "xn2T_mm", "u2T")
            pe.wait_ge(sem("u2T"), 2 * KB)
            wr = K("w_router").rearrange("p (k n) -> p k n", k=KB)
            for k in range(KB):
                mm(bank[4][0:16, :], wr[:, k, :], u2T[:, k, 0:SEQ_S], k, KB)
                i = mm(bank[5][0:16, 0:SEQ_C], wr[:, k, :], u2T[:, k, SEQ_S:TOK], k, KB)
            i.then_inc(sem("router_mm"), 1)
            pe.wait_ge(sem("logit_row"), 2)
            for t in range(NT):
                i = pe.transpose(bank[2][:, 16 * t:16 * t + 16], rrow[:, P * t:P * t + P], ident[0:16, 0:16])
            i.then_inc(sem("logit_tr"), 1)
            spread_gate(pe, mm, 1)
            pe.wait_ge(sem("probs"), 1)
            for t in range(NT):
                i = pe.transpose(bank[6 + t // 4][0:16, P * (t % 4):P * (t % 4) + P], probs[:, t, 0:E], ident)
            i.then_inc(sem("prob_tr"), 1)
            pe.wait_ge(sem("slot_row"), 1)
            for t in range(NT):
                i = pe.transpose(bank[5][:, 16 * t:16 * t + 16], rrow[:, P * t:P * t + P], ident[0:16, 0:16])
            i.then_inc(sem("slot_tr"), 1)

            def gather(n):
                pe.wait_ge(sem("onehot"), 5 * n + 5)
                for t in range(ST):
                    for half in range(2):
                        mm(bank[3][64 * half:64 * half + 64, :], Gs[:, t, :], xn2[:, t, 512 * half:512 * half + 512], t, ST)
                for q in range(4):
                    i = mm(bank[4][32 * q:32 * q + 32, 0:256], Gc, xn2[:, ST, 256 * q:256 * q + 256])
                i.then_inc(sem("gather_mm"), 1)

            def gather_transpose(n):
                pe.wait_ge(sem("gathered"), 2 * n + 2)
                for j in range(4):
                    pe.transpose(bank[3][:, P * j:P * j + P], xs[:, P * j:P * j + P], ident)
                for j in range(2):
                    i = pe.transpose(bank[4][:, P * j:P * j + P], xsc[:, P * j:P * j + P], ident)
                i.then_inc(sem("xT_mm"), 1)

            pe.wait_ge(sem("g2row"), 4)
            pe.wait_ge(sem("slots"), 2)
            gather(0)
            gather_transpose(0)
            with pe.Fori(0, E) as e:
                pe.wait_ge(sem("xT"), e * 4 + 4)
                for which, out, outc in ((0, bank[0], bank[2][:, 0:256]), (1, bank[1], bank[5][:, 256:512])):
                    if which:
                        pe.wait_ge(sem("ys"), e * 2 + 1)
                    for half in range(2):
                        pe.wait_ge(slot_full[2 * which + half], e * 16 + (16 * fills[2 * which + half] + 16))
                    for k in range(KB):
                        for half in range(2):
                            mm(out[64 * half:64 * half + 64, :], xsT[:, k, :], wslot(2 * which + half)[:, k, :], k, KB)
                    for k in range(KB):
                        for q in range(4):
                            i = mm(outc[32 * q:32 * q + 32, :], xcT[:, k, :],
                                   wslot(2 * which + q // 2)[:, k, 256 * (q % 2):256 * (q % 2) + 256], k, KB)
                    i.then_inc(sem("gu_mm"), 1)
                gather(e + 1)
                pe.wait_ge(sem("hid_e"), e * 2 + 2)
                for j in range(4):
                    i = pe.transpose(bank[6][:, P * j:P * j + P], hd[:, P * j:P * j + P], ident)
                i.then_inc(sem("hidT_mm"), 1)
                for j in range(2):
                    i = pe.transpose(bank[2][:, 256 + P * j:256 + P * j + P], hdc[:, P * j:P * j + P], ident)
                i.then_inc(sem("hidT_mm"), 1)
                gather_transpose(e + 1)
                pe.wait_ge(sem("hidT"), e + 1)
                for half in range(2):
                    pe.wait_ge(slot_full[4 + half], e * 16 + (16 * fills[4 + half] + 16))
                for k in range(KB):
                    for half in range(2):
                        mm(bank[7][64 * half:64 * half + 64, :], hdT[:, k, :], wslot(4 + half)[:, k, :], k, KB)
                pe.wait_ge(sem("hidTc"), e + 1)
                for k in range(KB):
                    for q in range(4):
                        i = mm(bank[5][32 * q:32 * q + 32, 0:256], hdcT[:, k, :],
                               wslot(4 + q // 2)[:, k, 256 * (q % 2):256 * (q % 2) + 256], k, KB)
                i.then_inc(sem("down_mm"), 1)
            pe.wait_ge(sem("weighted"), 5 * E)
            for j in range(PAIRS):
                if j >= 4:
                    pe.wait_ge(sem("ct"), j - 3)
                for t in range(ST):
                    i = pe.transpose(bank[(0, 1, 2, 6)[j % 4]][:, P * t:P * t + P], GA[:, t, P * j:P * j + P], ident)
                i.then_inc(sem("ct_mm"), 1)
            pe.wait_ge(sem("ct"), PAIRS - 3)
            for j in range(2):
                i = pe.transpose(bank[0][:, P * j:P * j + P], GAc[:, P * j:P * j + P], ident)
            i.then_inc(sem("ct_mm"), 1)
            pe.wait_ge(sem("ct"), PAIRS)
            pe.wait_ge(sem("xT"), 4 * E + 4)
            pe.wait_ge(sem("ys_back"), 32)
            for n, t in enumerate(SCATTER_ORDER):
                kn = PAIRS if t < ST else 2
                if n == 1:
                    pe.wait_ge(sem("ct"), PAIRS + 1)
                    pe.wait_ge(sem("ys"), 2 * E + 1)
                if n == len(SCATTER_ORDER) - 1:
                    pe.wait_ge(sem("y_read"), 2)
                for k in range(kn):
                    if n == 0 and k == kn - 1:
                        pe.wait_ge(sem("ys_last"), 32)
                    for half in range(2):
                        cut = slice(512 * half, 512 * half + 512)
                        if t < ST:
                            lw, rhs = CT[:, k, P * t:P * t + P], ysAll[:, k, cut]
                        else:
                            lw, rhs = CTc[:, k, :], yscAll[:, k, cut]
                        i = mm(bank[SCATTER_BANKS[n][half]][:, :], lw, rhs, k, kn)
                i.then_inc(sem("y_mm"), 1)

        @block.scalar
        def _(act):
            A = nc.scalar.activation
            act.wait_ge(sem("loaded"), 64)
            for t in range(NT):
                A(filt[:, t, :], feats[:, TOK:TOK + 512], ACT.Exp, scale=C("offset")[:, t:t + 1]).then_inc(sem("window"), 1)
            for n in range(2):
                act.wait_ge(sem("sin_arg"), 9 * (n + 1))
                A(hid[n], sin_arg, ACT.Sin).then_inc(sem("hid"), 1)
            act.wait_ge(sem("cond"), 1)
            A(cond32[:, :, 0:2], K("cond").rearrange("p (k c) -> p k c", k=KB), ACT.Silu).then_inc(sem("cond"), 1)
            for t in range(NT):
                act.wait_ge(sem("filt"), t + 1)
                A(absf[:, t, :], filt[:, t, :], ACT.Abs).then_inc(sem("filt_abs"), 1)
            for j in range(FT + 1):
                act.wait_ge(sem("spec_mm"), j + 1)
                r = P if j < FT else FREQ_C
                for cs in range(2):
                    A(fspec[0:r, 2 * j + cs, :], bank[4 + 2 * (j % 2) + cs][0:r, :], ACT.Copy).then_inc(sem("fspec"), 1)
                if j == 2:
                    act.wait_ge(sem("moments"), NT)
                    A(rstd, mv[:, :, 1], ACT.Sqrt, bias=eps_ln).then_inc(sem("root"), 1)
            act.wait_ge(sem("filt_sum"), 1)
            for j in range(2):
                A(filtnorm[:, j, :], bank[1 + j][:, :], ACT.Copy).then_inc(sem("norm_row"), 1)
            act.wait_ge(sem("h"), 2)
            act.dma_start(h_spill.rearrange("p (t d) -> p t d", t=NT), h).then_inc(sem("spilled"), 16)

            def modulate(dst, mm_done, out, sc, sh):
                for k in range(KB):
                    act.wait_ge(sem(mm_done), k + 1)
                    for c, (b, a, n) in enumerate(((2 + k % 2, 0, SEQ_S), (k % 2, SEQ_S, SEQ_C))):
                        A(dst[:, k, a:a + n], bank[b][:, 0:n], ACT.Identity, bias=modT[:, 48 * c + sh + k:48 * c + sh + k + 1],
                          scale=modT[:, 48 * c + sc + k:48 * c + sc + k + 1]).then_inc(sem(out), 1)

            act.wait_ge(sem("mod_col"), 3)
            modulate(uT, "xnT_mm", "uT", 8, 0)

            conv_dst = [x1T] * 4 + [uuT] * 4 + [x0T] * 4 + [qT] * 4 + [kT] * 4 + [vT] * 4

            def tap(n):
                act.wait_ge(sem("proj_mm"), n + 1)
                if n == 12:
                    act.wait_ge(sem("spilled"), 16)
                if n < 12:
                    w = K("conv_b").rearrange("p (b j) -> p b j", j=3)[:, HY_BLOCK[n], 1:2]
                    bias = K("conv_bb")[:, HY_BLOCK[n]:HY_BLOCK[n] + 1]
                else:
                    w, bias = K("conv_a").rearrange("p (b j) -> p b j", j=3)[:, n - 12, 1:2], 0.0
                d = conv_dst[n][:, n % 4, :]
                A(d[:, 0:SEQ_S], bank[n % 2][:, :], ACT.Identity, bias=bias, scale=w).then_inc(sem("tap"), 1)
                A(d[:, SEQ_S:TOK], bank[2 + n % 2][:, 0:SEQ_C], ACT.Identity, bias=bias, scale=w).then_inc(sem("tap"), 1)

            def silu(n):
                act.wait_ge(sem("conv"), 4 * (n + 1))
                d = conv_dst[n][:, n % 4, :]
                A(d, d, ACT.Silu).then_inc(sem("qkv_act"), 1)

            def mod_rows(n):
                act.wait_ge(sem("mod_mm"), n + 1)
                if n:
                    act.wait_ge(sem("mod_tr"), n)
                A(modrow, bank[6][:, :], ACT.Copy).then_inc(sem("mod_row"), 1)

            for n in range(12):
                if n % 4 == 1:
                    mod_rows(n // 4 + 1)
                tap(n)
            for t in range(NT):
                act.wait_ge(sem("uutok_mm"), t + 1)
                A(uuTok[:, t, :], bank[4 + t % 2][:, :], ACT.Copy).then_inc(sem("uutok"), 1)
            for n in range(12, CONV):
                if n in MOD_PRODUCT:
                    mod_rows(MOD_PRODUCT[n])
                tap(n)
                if n > 12:
                    silu(n - 1)
            silu(CONV - 1)
            b6 = bank[6][:, 0:80].rearrange("p (t x) -> p t x", t=NT)
            act.wait_ge(sem("ba_tr"), 1)
            act.wait_ge(sem("dec"), 1)
            A(d_tmp.rearrange("p (t x) -> p t x", t=NT), b6[:, :, 0:8], ACT.Exp, scale=-1.0).then_inc(sem("dec_act"), 1)
            A(d_expa[:, 0:8], K("a_log"), ACT.Exp).then_inc(sem("dec_act"), 1)
            act.wait_ge(sem("dec"), DEC_NEG)
            A(d_neg, d_neg, ACT.Exp).then_inc(sem("dec_act"), 1)
            act.wait_ge(sem("dec_act"), 3)
            A(d_neg, d_neg, ACT.Ln, bias=1.0).then_inc(sem("dec_act"), 1)
            act.wait_ge(sem("dec"), DEC_GC)
            A(d_negegc, d_gc, ACT.Exp).then_inc(sem("dec_act"), 1)
            A(d_edk, d_edk, ACT.Exp).then_inc(sem("dec_act"), 1)
            A(d_egl, d_tot, ACT.Exp).then_inc(sem("dec_act"), 1)
            for n in range(9):
                if n < 8:
                    src = (qT if n < 4 else kT)[:, n % 4, :]
                    if n >= 2:
                        act.wait_ge(sem("norm_mm"), n - 1)
                    else:
                        act.wait_ge(sem("qkv_act"), 12)
                    A(sq[n % 2], src, ACT.Square).then_inc(sem("sq"), 1)
                if n >= 1:
                    m = n - 1
                    act.wait_ge(sem("norm_mm"), m + 1)
                    if m >= 2:
                        act.wait_ge(sem("qk_normal"), 2 * (m - 1))
                    scale, bias = (float(P), eps_q) if m < 4 else (1.0, eps_k)
                    A(rn[m % 2][:, 0:SEQ_S], bank[m % 2][:, :], ACT.Sqrt, bias=bias, scale=scale).then_inc(sem("norm_root"), 1)
                    A(rn[m % 2][:, SEQ_S:TOK], bank[2 + m % 2][:, 0:SEQ_C], ACT.Sqrt, bias=bias, scale=scale).then_inc(sem("norm_root"), 1)
            for t in range(NT):
                act.wait_ge(sem("vtok_mm"), t + 1)
                A(vtok[:, t, :], bank[4 + t % 2][:, :], ACT.Copy).then_inc(sem("vtok"), 1)

            for p in range(NT):
                def pe_(r, step):
                    act.wait_ge(sem(f"dn_pe{r}"), PE_N * p + PES[step])

                def dve_(r, step):
                    act.wait_ge(sem(f"dn_dve{r}"), DVE_N * p + DVE[step])

                def bank4(r, b):
                    return bank[4 * r + b][:, :].rearrange("p (h c) -> p h c", h=HEADS)

                if p == 0:
                    act.wait_ge(sem("qk_normal"), 16)
                    act.wait_ge(sem("inv_mm"), 4)
                    for r, name in enumerate(("state_delta_fwd", "state_delta_bwd")):
                        act.dma_start(state[r], T[name].rearrange("h k v -> k h v")).then_inc(sem("state_in"), 16)
                for r in range(2):
                    pe_(r, "R")
                    A(dQG[r], bank4(r, 3), ACT.Exp).then_inc(sem(f"dn_act{r}"), 1)
                for r in range(2):
                    dve_(r, "E")
                    A(dD[r], dD[r], ACT.Exp).then_inc(sem(f"dn_act{r}"), 1)
                for r in range(2):
                    pe_(r, "KT")
                    for hh in range(HEADS):
                        x = 8 * TILE[r][p] + 4 * r + hh
                        A(dKG[r][:, hh, :], bank[4 * r + 2][:, P * hh:P * hh + P], ACT.Copy, scale=d_negegc[:, x:x + 1]) \
                            .then_inc(sem(f"dn_act{r}"), 1)
                    for hh in range(HEADS):
                        x = 8 * TILE[r][p] + 4 * r + hh
                        A(dKD[r][:, hh, :], bank[4 * r + 2][:, P * hh:P * hh + P], ACT.Copy, scale=d_edk[:, x:x + 1]) \
                            .then_inc(sem(f"dn_act{r}"), 1)
                for lev in range(1, LEVELS):
                    for r in range(2):
                        pe_(r, f"W{lev}")
                        A(dW[r], bank4(r, 0), ACT.Copy).then_inc(sem(f"dn_act{r}"), 1)
                for r in range(2):
                    pe_(r, "WT")
                    A(dWT[r], bank4(r, 3), ACT.Copy).then_inc(sem(f"dn_act{r}"), 1)
                if p == NT - 1:
                    for r in range(2):
                        dve_(r, "ST")
                        act.dma_start(O[2 + r].rearrange("h k v -> k h v"), state[r]).then_inc(sem("out_done"), 16)

            def gate(n, f, dst):
                act.wait_ge(sem("proj_mm"), n + 1)
                A(dst[:, 0:SEQ_S], bank[n % 2][:, :], f).then_inc(sem("zg"), 1)
                A(dst[:, SEQ_S:TOK], bank[2 + n % 2][:, 0:SEQ_C], f).then_inc(sem("zg"), 1)

            for n in range(4):
                if n == 1:
                    mod_rows(8)
                gate(CONV + n, ACT.Silu, zT[:, n, :])
            act.wait_ge(sem("out_done"), 32)
            for n in range(HEADS + 1):
                if n < HEADS:
                    if n >= 2:
                        act.wait_ge(sem("onorm_mm"), n - 1)
                    A(sq[n % 2], oT[:, n, :], ACT.Square).then_inc(sem("osq"), 1)
                if n >= 1:
                    m = n - 1
                    act.wait_ge(sem("onorm_mm"), m + 1)
                    if m >= 2:
                        act.wait_ge(sem("og"), 2 * (m - 1))
                    A(rn[m % 2][:, 0:SEQ_S], bank[4 + m % 2][:, :], ACT.Sqrt, bias=eps_k, scale=1.0 / P).then_inc(sem("onorm_root"), 1)
                    A(rn[m % 2][:, SEQ_S:TOK], bank[6 + m % 2][:, 0:SEQ_C], ACT.Sqrt, bias=eps_k, scale=1.0 / P).then_inc(sem("onorm_root"), 1)
            act.wait_ge(sem("og"), 2 * HEADS)
            act.dma_start(h, h_spill.rearrange("p (t d) -> p t d", t=NT)).then_inc(sem("h_back"), 16)
            for half in range(2):
                for b in range(8):
                    gate(CONV + 4 + 8 * half + b, ACT.Sigmoid, sig[:, b, :])
            act.wait_ge(sem("mixed"), 5 * KB)
            for j, w in enumerate(("ln1_g", "ln1_b")):
                act.dma_start(lnrow[:, j, :], T[w].to_broadcast([P, D])).then_inc(sem("ln1_in"), 16)
            for t in range(NT):
                for j in range(2):
                    act.wait_ge(sem("moments1"), 2 * t + j + 1)
                    A(rstd[:, t:t + 1], mv[:, t, 1:2], ACT.Sqrt, bias=eps_ln).then_inc(sem("root1"), 1)
            modulate(u2T, "xn2T_mm", "u2T", 32, 24)
            act.wait_ge(sem("logits"), 3)
            lg = probs[:, :, 0:E]
            A(lg, lg, ACT.Exp).then_inc(sem("exp_logits"), 1)
            for c in range(2):
                act.wait_ge(sem("spread_mm"), 2 + c + 1)
                for j in range(2):
                    A(g2row[:, c, 512 * j:512 * j + 512], bank[SPREAD_BANKS[1][2 * c + j]][:, :], ACT.Copy).then_inc(sem("g2row"), 1)

            def copy_gathered(n):
                act.wait_ge(sem("gather_mm"), n + 1)
                A(xs, bank[3][:, :], ACT.Copy).then_inc(sem("gathered"), 1)
                A(xsc, bank[4][:, 0:256], ACT.Copy).then_inc(sem("gathered"), 1)

            copy_gathered(0)
            with act.Fori(0, E) as e:
                act.wait_ge(sem("gu_mm"), e * 2 + 1)
                A(sil, bank[0][:, :], ACT.Silu).then_inc(sem("sil"), 1)
                A(silc, bank[2][:, 0:256], ACT.Silu).then_inc(sem("sil"), 1)
                copy_gathered(e + 1)
                act.wait_ge(sem("hidT_mm"), e * 2 + 1)
                A(hdT.rearrange("p (h j) s -> p h j s", h=2), by_block(6, 0, 64, 4), ACT.Copy).then_inc(sem("hidT"), 1)
                act.wait_ge(sem("down_mm"), e + 1)
                act.wait_ge(sem("ys_out"), e * 96 + 1)
                A(ys, bank[7][:, :], ACT.Copy).then_inc(sem("ys"), 1)
                A(ysc, bank[5][:, 0:256], ACT.Copy).then_inc(sem("ys"), 1)
                act.wait_ge(sem("ys"), e * 2 + 3)
                for half in range(2):
                    act.dma_start(ys_dram[bass.ds(e * CAP_S, CAP_S), 512 * half:512 * half + 512],
                                  ys[64 * half:64 * half + 64, :]).then_inc(sem("ys_out"), 16)
                for q in range(4):
                    act.dma_start(ysc_dram[bass.ds(e * CAP_C, CAP_C), 256 * q:256 * q + 256],
                                  ysc[32 * q:32 * q + CAP_C, :]).then_inc(sem("ys_out"), 16)
            for j in range(PAIRS + 1):
                act.wait_ge(sem("ct_mm"), j + 1)
                if j < PAIRS:
                    A(CT[:, j, :], bank[(0, 1, 2, 6)[j % 4]][:, :], ACT.Copy).then_inc(sem("ct"), 1)
                else:
                    A(CTc, bank[0][:, 0:2 * P].rearrange("p (j t) -> p j t", j=2), ACT.Copy).then_inc(sem("ct"), 1)
            for n, t in enumerate(SCATTER_ORDER):
                act.wait_ge(sem("moments2"), n + 1)
                A(rstd[:, t:t + 1], mv[:, t, 1:2], ACT.Sqrt, bias=eps_ln).then_inc(sem("root2"), 1)
                act.wait_ge(sem("y"), n + 1)
                act.dma_start(O[1][P * t:P * t + P, :] if t < ST else O[0], h[:, t, :]).then_inc(sem("out_done"), 16)
            act.wait_ge(sem("out_done"), 16 * (2 + NT))

        @block.vector
        def _(dve):
            V = nc.vector

            class Stage:
                def __init__(self, name):
                    self.sem, self.n = sem(name), 0

                def add(self, ins):
                    ins.then_inc(self.sem, 1)
                    self.n += 1

                def settle(self):
                    dve.wait_ge(self.sem, self.n)

            dve.wait_ge(sem("loaded"), 64)
            V.memset(misc[:, 2432:2688], 0.0).then_inc(sem("cond"), 1)
            s = Stage("sin_arg")
            for layer in range(2):
                dve.wait_ge(sem("hid_mm"), layer + 1)
                if layer:
                    dve.wait_ge(sem("hid"), 1)
                for b, a, n in ((2 * layer, 0, SEQ_S), (2 * layer + 1, SEQ_S, SEQ_C)):
                    s.add(V.tensor_scalar(sin_arg[:, a:a + n], bank[b][0:64, 0:n], K("hy_b1" if layer == 0 else "hy_b2")[0:64, :],
                                          K("hy_freq")[0:64, :], ALU.add, ALU.mult))
                s.settle()
                s.add(V.tensor_scalar(sin_n, sin_arg, 1.0 / (2.0 * math.pi), MAGIC, ALU.mult, ALU.add))
                s.settle()
                s.add(V.tensor_scalar(sin_n, sin_n, -MAGIC, None, ALU.add))
                for part in TWO_PI:
                    s.settle()
                    s.add(V.scalar_tensor_tensor(sin_arg, sin_n, -part, sin_arg, ALU.mult, ALU.add))
                s.settle()
                s.add(V.tensor_scalar(sin_arg, sin_arg, PI_BELOW, -PI_BELOW, ALU.min, ALU.max))
                s.settle()
                s.add(V.engine_nop())
            s = Stage("filt")
            dve.wait_ge(sem("window"), NT)
            for t in range(NT):
                dve.wait_ge(sem("filt_mm"), t + 1)
                s.add(V.tensor_tensor(filt[:, t, :], bank[4 + t if t < 4 else 0][:, :], filt[:, t, :], ALU.mult))
            hs = Stage("h")
            dve.wait_ge(sem("x_in"), 64)
            hs.add(V.tensor_tensor(h[:, 0:ST, 0:512], h[:, 0:ST, 0:512], posr, ALU.add))
            hs.add(V.tensor_tensor(h[:, 0:ST, 512:D], h[:, 0:ST, 512:D], posc.unsqueeze(1).to_broadcast([P, ST, 512]), ALU.add))
            hs.settle()
            bs, ms = Stage("bn"), Stage("moments")

            def moments(t, src, stage):
                for j in range(2):
                    bs.add(V.bn_stats(bn[:, t, 6 * j:6 * j + 6], src[:, 512 * j:512 * j + 512]))
                bs.settle()
                stage.add(V.bn_aggr(mv[:, t, :], bn[:, t, :]))

            for t in range(NT):
                moments(t, h[:, t, :], ms)
            rs, xs_ = Stage("rstd"), Stage("xn")
            dve.wait_ge(sem("root"), 1)
            rs.add(V.reciprocal(rstd, rstd))
            rs.settle()
            for t in range(NT):
                xs_.add(V.tensor_scalar(xn[:, t, :], h[:, t, :], mv[:, t, 0:1], rstd[:, t:t + 1], ALU.subtract, ALU.mult))
            ms2 = Stage("mod_col")
            by_cond = modT[:, :].rearrange("p (c b) -> p c b", c=2)
            dve.wait_ge(sem("mod_mm"), 1)
            V.tensor_copy(modrow, bank[0][:, :]).then_inc(sem("mod_row"), 1)
            s = Stage("fnorm")
            dve.wait_ge(sem("norm_tr"), 1)
            for j in range(2):
                s.add(V.tensor_scalar(fnorm[:, 4 * j:4 * j + 4], bank[1 + j][:, :].rearrange("p (b x) -> p b x", b=4)[:, :, 0],
                                      1e-6, None, ALU.add))
            s.settle()
            s.add(V.reciprocal(fnorm_inv, fnorm))
            s.add(V.tensor_tensor(skip_norm.rearrange("p (j b) -> p j b", j=2), fnorm.rearrange("p (j b) -> p j b", j=2),
                                  K("skip").unsqueeze(1).to_broadcast([P, 2, 4]), ALU.mult))
            dve.wait_ge(sem("mod_tr"), 1)
            src = bank[7][:, :].rearrange("p (i j x) -> p j i x", i=4, j=4)
            for c in range(2):
                ms2.add(V.tensor_tensor(modT[:, 48 * c:48 * c + 16].rearrange("p (j i) -> p j i", j=4),
                                        src[:, :, :, c], K("b_mod")[:, 0:16].rearrange("p (j i) -> p j i", j=4), ALU.add))
            ms2.settle()
            ms2.add(V.tensor_scalar(by_cond[:, :, 8:16], by_cond[:, :, 8:16], 1.0, None, ALU.add))

            def mod_column(n):
                dve.wait_ge(sem("mod_tr"), n + 1)
                b = 4 * (n + 3)
                d = by_cond[:, :, b:b + 4]
                ms2.add(V.tensor_reduce(d, bank[7][:, :].rearrange("p (i j x) -> p x i j", i=4, j=4)[:, 0:2], AX, ALU.add))
                ms2.settle()
                ms2.add(V.scalar_tensor_tensor(d, d, 1.0 if 32 <= b < 40 else 0.0,
                                               K("b_mod")[:, b:b + 4].unsqueeze(1).to_broadcast([P, 2, 4]), ALU.add, ALU.add))

            cs_ = Stage("conv")
            conv_dst = [x1T] * 4 + [uuT] * 4 + [x0T] * 4 + [qT] * 4 + [kT] * 4 + [vT] * 4

            def conv(n):
                if n in MOD_TRANSPOSE:
                    mod_column(MOD_TRANSPOSE[n])
                dve.wait_ge(sem("tap"), 2 * (n + 1))
                w = K("conv_b" if n < 12 else "conv_a").rearrange("p (b j) -> p b j", j=3)[:, HY_BLOCK[n] if n < 12 else n - 12, :]
                d = conv_dst[n][:, n % 4, :]
                for tap_, shift in ((0, 1), (2, -1)):
                    if tap_:
                        cs_.settle()
                    for b, a, l in ((n % 2, 0, SEQ_S), (2 + n % 2, SEQ_S, SEQ_C)):
                        o = (1, l) if shift == 1 else (0, l - 1)
                        out = d[:, a + o[0]:a + o[1]]
                        cs_.add(V.scalar_tensor_tensor(out, bank[b][:, o[0] - shift:o[1] - shift], w[:, tap_:tap_ + 1], out,
                                                       ALU.mult, ALU.add))

            us = Stage("uu")
            for n in range(12):
                conv(n)
                if 4 <= n < 8:
                    cs_.settle()
                    us.add(V.tensor_tensor(uuT[:, n - 4, :], x1T[:, n - 4, :], uuT[:, n - 4, :], ALU.mult))
            for n in range(12, 16):
                conv(n)
            s = Stage("product")
            for j in range(FT + 1):
                dve.wait_ge(sem("spec_mm"), FT + 1 + j + 1)
                r = P if j < FT else FREQ_C
                a, b = (bank[4 + 2 * (j % 2) + cs][0:r, :] for cs in range(2))
                fc, fs = (fspec[0:r, 2 * j + cs, :] for cs in range(2))
                s.add(V.tensor_tensor(uspec[0:r, 2 * j, :], a, fc, ALU.mult))
                s.add(V.tensor_tensor(ptmp[0:r, 0, :], b, fs, ALU.mult))
                s.add(V.tensor_tensor(uspec[0:r, 2 * j + 1, :], a, fs, ALU.mult))
                s.add(V.tensor_tensor(ptmp[0:r, 1, :], b, fc, ALU.mult))
                s.settle()
                s.add(V.tensor_tensor(uspec[0:r, 2 * j, :], uspec[0:r, 2 * j, :], ptmp[0:r, 0, :], ALU.subtract))
                s.add(V.tensor_tensor(uspec[0:r, 2 * j + 1, :], uspec[0:r, 2 * j + 1, :], ptmp[0:r, 1, :], ALU.add))
                s.settle()
            for n in range(16, 20):
                conv(n)
            s = Stage("yb")
            dve.wait_ge(sem("fnorm"), 4)
            parts = ((0, 0, SEQ_S), (1, SEQ_S, SEQ_C))
            for cb in range(4):
                dve.wait_ge(sem("inv_mm"), cb + 1)
                for j, a, l in parts:
                    s.add(V.scalar_tensor_tensor(uuT[:, cb, a:a + l], uuT[:, cb, a:a + l], skip_norm[:, 4 * j + cb:4 * j + cb + 1],
                                                 bank[4 + 2 * (cb % 2) + j][:, 0:l], ALU.mult, ALU.add))
                s.settle()
                for j, a, l in parts:
                    s.add(V.scalar_tensor_tensor(x0T[:, cb, a:a + l], uuT[:, cb, a:a + l], fnorm_inv[:, 4 * j + cb:4 * j + cb + 1],
                                                 x0T[:, cb, a:a + l], ALU.mult, ALU.mult))
            for n in range(20, CONV):
                conv(n)
            dve.wait_ge(sem("ba_mm"), 1)
            V.tensor_copy(barow[0:16, 0:SEQ_S], bank[4][0:16, :]).then_inc(sem("ba_row"), 1)
            V.tensor_copy(barow[0:16, SEQ_S:TOK], bank[5][0:16, 0:SEQ_C]).then_inc(sem("ba_row"), 1)
            s = Stage("dec")

            def tx(v):
                return v.rearrange("p (t x) -> p t x", t=NT)

            dve.wait_ge(sem("ba_tr"), 1)
            s.add(V.tensor_tensor(tx(d_xa), bank[6][:, 0:80].rearrange("p (t x) -> p t x", t=NT)[:, :, 8:16],
                                  K("dt_bias").unsqueeze(1).to_broadcast([P, NT, 8]), ALU.add))
            s.settle()
            s.add(V.tensor_scalar(d_relu, d_xa, 0.0, None, ALU.max))
            s.add(V.tensor_scalar(d_neg, d_xa, -1.0, None, ALU.mult))
            s.settle()
            s.add(V.tensor_tensor(d_neg, d_neg, d_xa, ALU.min))
            dve.wait_ge(sem("dec_act"), 2)
            s.add(V.tensor_scalar(d_tmp, d_tmp, 1.0, None, ALU.add))
            s.settle()
            s.add(V.reciprocal(d_beta, d_tmp))
            s.settle()
            s.add(V.tensor_scalar(d_negbeta, d_beta, -1.0, None, ALU.mult))
            dve.wait_ge(sem("dec_act"), 4)
            s.add(V.tensor_tensor(d_relu, d_relu, d_neg, ALU.add))
            s.settle()
            s.add(V.scalar_tensor_tensor(tx(d_g), tx(d_relu), -1.0, d_expa[:, 0:8].unsqueeze(1).to_broadcast([P, NT, 8]),
                                         ALU.mult, ALU.mult))
            dve.wait_ge(sem("gc_mm"), 1)
            s.add(V.tensor_copy(tx(d_gc)[:, :, 0:4], bank[7][:, 0:20].rearrange("p (t x) -> p t x", t=NT)))
            s.add(V.tensor_copy(tx(d_gc)[:, :, 4:8], bank[7][:, 32:52].rearrange("p (t x) -> p t x", t=NT)))
            s.add(V.tensor_copy(d_tot, bank[7][:, 64:104]))
            s.settle()
            s.add(V.tensor_tensor(d_edk, d_tot, d_gc, ALU.subtract))
            dve.wait_ge(sem("dec_act"), 7)
            s.add(V.tensor_scalar(d_negegc, d_negegc, -1.0, None, ALU.mult))
            s = Stage("qk_normal")
            rs = Stage("rn")
            for n in range(8):
                dve.wait_ge(sem("norm_root"), 2 * (n + 1))
                rs.add(V.reciprocal(rn[n % 2], rn[n % 2]))
                rs.settle()
                d = (qT if n < 4 else kT)[:, n % 4, :]
                s.add(V.tensor_tensor(d, d, rn[n % 2], ALU.mult))
                s.add(V.engine_nop())

            dve.wait_ge(sem("loaded_delta"), 16)
            neg = (C("neg_f"), C("neg_b"))
            masks = tuple(C(m).bitcast(U32).rearrange("p (l c) -> p l c", l=LEVELS) for m in ("mask_lo", "mask_up"))
            ds = [Stage("dn_dve0"), Stage("dn_dve1")]
            first = [True] * NT
            for p in range(NT):
                def pe_(r, step):
                    dve.wait_ge(sem(f"dn_pe{r}"), PE_N * p + PES[step])

                def act_(r, step):
                    dve.wait_ge(sem(f"dn_act{r}"), ACT_N * p + ACTS[step])

                def bank4(r, b):
                    return bank[4 * r + b][:, :].rearrange("p (h c) -> p h c", h=HEADS)

                def x(r, hh):
                    return 8 * TILE[r][p] + 4 * r + hh

                def blend(r, lev, which, data):
                    m = masks[(r + which) % 2][:, lev, :].unsqueeze(1).to_broadcast([P, HEADS, P])
                    return V.copy_predicated((dM, dU)[which][r], m, data)

                for r in range(2):
                    act_(r, "EG")
                    for hh in range(HEADS):
                        ds[r].add(V.scalar_tensor_tensor(dD[r][:, hh, :], bank[4 * r + 3][:, P * hh:P * hh + P],
                                                         d_gc[:, x(r, hh):x(r, hh) + 1], neg[r], ALU.subtract, ALU.add))
                for r in range(2):
                    for w in (dM, dU):
                        ds[r].add(V.tensor_copy(w[r], ident.unsqueeze(1).to_broadcast([P, HEADS, P])))
                    act_(r, "D")
                    pe_(r, "KK")
                    for hh in range(HEADS):
                        ds[r].add(V.scalar_tensor_tensor(dLnT[r][:, hh, :], bank[4 * r][:, P * hh:P * hh + P],
                                                         d_negbeta[:, x(r, hh):x(r, hh) + 1], dD[r][:, hh, :], ALU.mult, ALU.mult))
                for r in range(2):
                    pe_(r, "QK")
                    ds[r].add(V.tensor_tensor(dAT[r], bank4(r, 1), dD[r], ALU.mult))
                    t = TILE[r][p]
                    ds[r].add(V.tensor_tensor(dQG[r], qT[:, :, P * t:P * t + P], dQG[r], ALU.mult))
                for r in range(2):
                    ds[r].settle()
                    ds[r].add(blend(r, 0, 1, dLnT[r]))
                    pe_(r, "LN")
                    ds[r].add(blend(r, 0, 0, bank4(r, 0)))
                for lev in range(1, LEVELS):
                    for r in range(2):
                        pe_(r, f"MU{lev}")
                        ds[r].settle()
                        if lev < LEVELS - 1:
                            ds[r].add(blend(r, lev, 0, bank4(r, 1)))
                        ds[r].add(blend(r, lev, 1, bank4(r, 2)))
                for r in range(2):
                    pe_(r, "V")
                    for hh in range(HEADS):
                        ds[r].add(V.tensor_scalar(dVN[r][:, hh, :], bank[4 * r][:, P * hh:P * hh + P],
                                                  d_beta[:, x(r, hh):x(r, hh) + 1], None, ALU.mult))
                for r in range(2):
                    pe_(r, "OS")
                    t = TILE[r][p]
                    o = oT[:, :, P * t:P * t + P]
                    if r:
                        dve.wait_ge(sem("dn_dve0"), ds[0].n)
                    else:
                        dve.wait_ge(sem("dn_dve1"), ds[1].n)
                    if first[t]:
                        ds[r].add(V.tensor_copy(o, bank4(r, 1)))
                        first[t] = False
                    else:
                        ds[r].add(V.tensor_tensor(o, bank4(r, 1), o, ALU.add))
                    if p == ST - 1:
                        ds[r].add(V.memset(state[r], 0.0))
                        for _i in range(3):
                            ds[r].add(V.engine_nop())
                    else:
                        if p == 0:
                            dve.wait_ge(sem("state_in"), 32)
                        for hh in range(HEADS):
                            ds[r].add(V.scalar_tensor_tensor(state[r][:, hh, :], state[r][:, hh, :], d_egl[:, x(r, hh):x(r, hh) + 1],
                                                             bank[4 * r + 2][:, P * hh:P * hh + P], ALU.mult, ALU.add))
                    assert ds[r].n == DVE_N * (p + 1), (ds[r].n, DVE_N)

            mod_column(8)
            s = Stage("og")
            rs2 = rs
            dve.wait_ge(sem("zg"), 8)
            for n in range(HEADS):
                dve.wait_ge(sem("onorm_root"), 2 * (n + 1))
                rs2.add(V.reciprocal(rn[n % 2], rn[n % 2]))
                rs2.settle()
                s.add(V.scalar_tensor_tensor(oG[:, n, :], oT[:, n, :], K("gnorm"), rn[n % 2], ALU.mult, ALU.mult))
                s.settle()
                s.add(V.tensor_tensor(oG[:, n, :], oG[:, n, :], zT[:, n, :], ALU.mult))
            s = Stage("mixed")
            for n in range(KB):
                dve.wait_ge(sem("zg"), 2 * (12 + 8 * (n // 4)))
                dve.wait_ge(sem("up_mm"), n + 1)
                banks = (4, 5, 6, 7) if n % 2 == 0 else (0, 2, 1, 3)
                if n:
                    s.settle()
                s.add(V.tensor_tensor(mixedT[:, n, 0:SEQ_S], bank[banks[0]][:, :], sig[:, n % 4, 0:SEQ_S], ALU.mult))
                s.add(V.tensor_tensor(mixedT[:, n, SEQ_S:TOK], bank[banks[1]][:, 0:SEQ_C], sig[:, n % 4, SEQ_S:TOK], ALU.mult))
                s.add(V.tensor_tensor(uptmp[:, 0:SEQ_S], bank[banks[2]][:, :], sig[:, 4 + n % 4, 0:SEQ_S], ALU.mult))
                s.add(V.tensor_tensor(uptmp[:, SEQ_S:TOK], bank[banks[3]][:, 0:SEQ_C], sig[:, 4 + n % 4, SEQ_S:TOK], ALU.mult))
                s.settle()
                s.add(V.tensor_tensor(mixedT[:, n, :], mixedT[:, n, :], uptmp, ALU.add))
            s.settle()
            dg = Stage("diag")

            for c in range(2):
                for k in range(KB):
                    dg.add(V.tensor_scalar(diag[:, c, k, :], ident, modT[:, 48 * c + 16 + k:48 * c + 16 + k + 1], None, ALU.mult))
            for c in range(2):
                dve.wait_ge(sem("spread_mm"), c + 1)
                for j in range(2):
                    V.tensor_copy(grow[:, c, 512 * j:512 * j + 512], bank[SPREAD_BANKS[0][2 * c + j]][:, :]).then_inc(sem("gate_row"), 1)
            dve.wait_ge(sem("gate_row"), 4)
            dve.wait_ge(sem("h_back"), 16)
            s = Stage("resid1")
            m1, orr, x2 = Stage("moments1"), Stage("out_read"), Stage("xn2")

            def norm(t, src, dst, stage, root, nroot, out):
                moments(t, src, stage)
                dve.wait_ge(sem(root), nroot)
                rs.add(V.reciprocal(rstd[:, t:t + 1], rstd[:, t:t + 1]))
                rs.settle()
                out.add(V.tensor_scalar(dst, src, mv[:, t, 0:1], rstd[:, t:t + 1], ALU.subtract, ALU.mult))

            for t in range(NT):
                c = 0 if t < ST else 1
                for j in range(2):
                    dve.wait_ge(sem("out_mm"), 2 * t + j + 1)
                    orr.add(V.tensor_tensor(otmp[:, t % 2, 512 * j:512 * j + 512], bank[(2 * t + j) % 4][:, :],
                                            grow[:, c, 512 * j:512 * j + 512], ALU.mult))
                orr.settle()
                s.add(V.scalar_tensor_tensor(h[:, t, :], h[:, t, :], ALPHA, otmp[:, t % 2, :], ALU.mult, ALU.add))
                s.settle()
                norm(t, h[:, t, :], h[:, t, :], m1, "root1", 2 * t + 1, s)
                s.settle()
                dve.wait_ge(sem("ln1_in"), 32)
                s.add(V.tensor_tensor(h[:, t, :], h[:, t, :], lnrow[:, 0, :], ALU.mult))
                s.settle()
                s.add(V.tensor_tensor(h[:, t, :], h[:, t, :], lnrow[:, 1, :], ALU.add))
                s.settle()
                norm(t, h[:, t, :], xn2[:, t, :], m1, "root1", 2 * t + 2, x2)
            for c in range(2):
                for k in range(KB):
                    dg.add(V.tensor_scalar(diag2[:, c, k, :], ident, modT[:, 48 * c + 40 + k:48 * c + 40 + k + 1], None, ALU.mult))
            dve.wait_ge(sem("router_mm"), 1)
            V.tensor_copy(rrow[:, 0:SEQ_S], bank[4][0:16, :]).then_inc(sem("logit_row"), 1)
            V.tensor_copy(rrow[:, SEQ_S:TOK], bank[5][0:16, 0:SEQ_C]).then_inc(sem("logit_row"), 1)
            dve.wait_ge(sem("logit_tr"), 1)
            s = Stage("logits")
            b2 = bank[2][:, 0:80].rearrange("p (t e) -> p t e", t=NT)
            s.add(V.tensor_reduce(rmax, b2, AX, ALU.max))
            s.settle()
            s.add(V.tensor_tensor(probs[:, :, 0:E], b2, rmax.unsqueeze(2).to_broadcast([P, NT, E]), ALU.subtract))
            s.add(V.memset(probs[:, :, E:E + 1], 0.0))
            dve.wait_ge(sem("exp_logits"), 1)
            s.add(V.tensor_reduce(rsum, probs[:, :, 0:E], AX, ALU.add))
            s.settle()
            s.add(V.reciprocal(rsum, rsum))
            s.settle()
            V.tensor_tensor(probs[:, :, 0:E], probs[:, :, 0:E], rsum.unsqueeze(2).to_broadcast([P, NT, E]), ALU.mult) \
                .then_inc(sem("probs"), 1)
            s = Stage("topk")
            dve.wait_ge(sem("prob_tr"), 1)
            s.add(V.tensor_copy(rrow[:, 0:SEQ_S], bank[6][0:16, :]))
            s.add(V.tensor_copy(rrow[:, SEQ_S:TOK], bank[7][0:16, 0:SEQ_C]))
            s.settle()
            for a, l, rounds in ((0, SEQ_S, CAP_S // 8), (SEQ_S, SEQ_C, CAP_C // 8)):
                for _r in range(rounds):
                    s.add(V.max(top8, rrow[:, a:a + l]))
                    s.settle()
                    s.add(V.match_replace(rrow[:, a:a + l], top8, rrow[:, a:a + l], -1.0))
                    s.settle()
            s.add(V.tensor_scalar(mask, rrow, 0.0, None, ALU.is_lt))
            s.settle()
            for a, l in ((0, SEQ_S), (SEQ_S, SEQ_C)):
                s.add(V.tensor_tensor_scan(count[:, a:a + l], mask[:, a:a + l], mask[:, a:a + l], 0.0, ALU.add, ALU.max))
            s.settle()
            s.add(V.tensor_tensor(count, count, mask, ALU.mult))
            s.settle()
            V.tensor_scalar(rrow, count, -1.0, None, ALU.add).then_inc(sem("slot_row"), 1)
            dve.wait_ge(sem("slot_tr"), 1)
            V.tensor_copy(slots[:, :, 0:E], bank[5][:, 0:80].rearrange("p (t e) -> p t e", t=NT)).then_inc(sem("slots"), 1)
            V.memset(slots[:, :, E:E + 1], -1.0).then_inc(sem("slots"), 1)
            V.engine_nop().then_inc(sem("ys"), 1)
            V.engine_nop().then_inc(sem("ys_out"), 1)
            dve.wait_ge(sem("slots"), 2)

            def col(v, t, n):
                return v[:, t, bass.ds(n, 1)]

            def onehot(n):
                for t in range(ST):
                    V.tensor_scalar(Gs[:, t, :], C("iota"), col(slots, t, n), None, ALU.is_equal).then_inc(sem("onehot"), 1)
                V.tensor_scalar(Gc, C("iota")[:, 0:32], col(slots, ST, n), None, ALU.is_equal).then_inc(sem("onehot"), 1)

            def xT(n):
                dve.wait_ge(sem("xT_mm"), n + 1)
                for stage, op in ((0, ALU.mult), (1, ALU.add)):
                    if stage:
                        dve.wait_ge(sem("xT"), n * 4 + 2)
                    for c, (dst, b, blocks, width, halves) in enumerate(((xsT, 3, 4, CAP_S, 2), (xcT, 4, 2, 32, 4))):
                        src = dst if stage else bank[b][:, 0:P * blocks].rearrange("p (j h s) -> p h j s", j=blocks, s=width)
                        if stage:
                            src = src.rearrange("p (h j) s -> p h j s", h=halves)
                        m = modT[:, 48 * c + (24 if stage else 32):48 * c + (32 if stage else 40)]
                        m = m.rearrange("p (h j) -> p h j", h=halves).unsqueeze(3).to_broadcast([P, halves, blocks, width])
                        V.tensor_tensor(dst.rearrange("p (h j) s -> p h j s", h=halves), src, m, op).then_inc(sem("xT"), 1)

            onehot(0)
            xT(0)
            with dve.Fori(0, E) as e:
                dve.wait_ge(sem("gather_mm"), e + 1)
                dve.wait_ge(sem("onehot"), e * 5 + 5)
                onehot(e + 1)
                for t in range(ST):
                    V.tensor_scalar(GA[:, t, bass.ds(e * CAP_S, CAP_S)], C("iota"), col(slots, t, e), col(probs, t, e),
                                    ALU.is_equal, ALU.mult).then_inc(sem("weighted"), 1)
                V.tensor_scalar(GAc[:, bass.ds(e * CAP_C, CAP_C)], C("iota")[:, 0:CAP_C], col(slots, ST, e), col(probs, ST, e),
                                ALU.is_equal, ALU.mult).then_inc(sem("weighted"), 1)
                dve.wait_ge(sem("sil"), e * 2 + 2)
                dve.wait_ge(sem("gu_mm"), e * 2 + 2)
                V.tensor_tensor(hd, bank[1][:, :], sil, ALU.mult).then_inc(sem("hid_e"), 1)
                V.tensor_tensor(hdc, bank[5][:, 256:512], silc, ALU.mult).then_inc(sem("hid_e"), 1)
                dve.wait_ge(sem("hidT_mm"), e * 2 + 2)
                V.tensor_copy(hdcT.rearrange("p (h j) s -> p h j s", h=4), by_block(2, 256, 32, 2)).then_inc(sem("hidTc"), 1)
                xT(e + 1)
            s = Stage("resid2")
            m2, yr = Stage("moments2"), Stage("y_read")
            dve.wait_ge(sem("g2row"), 4)
            for n, t in enumerate(SCATTER_ORDER):
                c = 0 if t < ST else 1
                dve.wait_ge(sem("y_mm"), n + 1)
                for j in range(2):
                    yr.add(V.tensor_tensor(ytmp[:, n % 2, 512 * j:512 * j + 512], bank[SCATTER_BANKS[n][j]][:, :],
                                           g2row[:, c, 512 * j:512 * j + 512], ALU.mult))
                yr.settle()
                s.add(V.scalar_tensor_tensor(h[:, t, :], h[:, t, :], ALPHA, ytmp[:, n % 2, :], ALU.mult, ALU.add))
                s.settle()
                norm(t, h[:, t, :], h[:, t, :], m2, "root2", n + 1, s)
                s.settle()
                dve.wait_ge(sem("ln2_in"), 32)
                s.add(V.tensor_tensor(h[:, t, :], h[:, t, :], ln2row[:, 0, :], ALU.mult))
                s.settle()
                V.tensor_tensor(h[:, t, :], h[:, t, :], ln2row[:, 1, :], ALU.add).then_inc(sem("y"), 1)


def steps(*named):
    out, n = {}, 0
    for name, k in named:
        n += k
        out[name] = n
    return out, n


PES, PE_N = steps(("R", 1), ("KK", 1), ("QK", 1), ("KT", 1), ("LN", 1),
                  *[s for lev in range(1, LEVELS) for s in ((f"W{lev}", 1), (f"MU{lev}", 1))], ("WT", 1), ("V", 1), ("OS", 1))
ACTS, ACT_N = steps(("EG", 1), ("D", 1), ("KG", 4), ("KD", 4), *[(f"W{lev}", 1) for lev in range(1, LEVELS)], ("WT", 1))
DVE, DVE_N = steps(("E", 4), ("LT", 6), ("AT", 1), ("QG", 1), ("P0", 2),
                   *[(f"P{lev}", 2 if lev < LEVELS - 1 else 1) for lev in range(1, LEVELS)], ("VN", 4), ("O", 1), ("ST", 4))
TILE = ((0, 1, 2, 3, 4), (3, 2, 1, 0, 4))
MOD_PRODUCT = {13: 4, 17: 5, 21: 6, 22: 7}
MOD_TRANSPOSE = {3: 1, 7: 2, 11: 3, 15: 4, 19: 5, 22: 6, 23: 7}
DEC_NEG, DEC_G, DEC_GC, DEC_ALL = 4, 9, 13, 14
HY_BLOCK = (4, 5, 6, 7, 8, 9, 10, 11, 0, 1, 2, 3)
SPREAD_BANKS = ((4, 5, 6, 7), (0, 1, 3, 4))
SCATTER_ORDER = (0, 4, 1, 2, 3)
SCATTER_BANKS = ((3, 4), (0, 1), (2, 6), (5, 7), (3, 4))

_INS = ["w_mod", "w_in", "w_up_a", "w_up_b", "w_out", "w_e_gate", "w_e_up", "w_e_down"]


def kernel(**inputs):
    import concourse.bacc as _bacc
    from concourse.bass_utils import run_bass_kernel_spmd as _run

    nc = _bacc.Bacc("TRN2", target_bir_lowering=False, num_devices=1)
    arr = {k: np.ascontiguousarray(v) for k, v in inputs.items()}
    arrays = {k: arr[k][0] for k in _INS + ["x_prompt", "x_sample"]}
    for k in ("state_delta_fwd", "state_delta_bwd"):
        arrays[k] = arr[k][0, 0]
    for k in ("ln1_g", "ln1_b", "ln2_g", "ln2_b"):
        arrays[k] = arr[k]
    pk = np.zeros((P, PK_N), np.float32)

    def put(name, v):
        a, n = PK[name]
        v = v.reshape(v.shape[0], -1)
        pk[0:v.shape[0], a:a + v.shape[1]] = v

    def blocks(v, n):
        return v.reshape(n, P, -1).transpose(1, 0, 2)

    put("cond", blocks(np.stack([arr["c"][0], arr["c_ctx"]], 1), KB))
    put("b_mod", blocks(arr["b_mod"][0], 48))
    put("conv_a", blocks(arr["conv_a_w"][0].T, 12))
    put("conv_b", blocks(arr["conv_b_w"][0].T, 12))
    put("conv_bb", blocks(arr["conv_b_b"][0], 12))
    put("skip", blocks(arr["hy_bias"][0], 4))
    put("gnorm", arr["gnorm_w"][0])
    put("a_log", np.tile(arr["a_log"].reshape(1, 8), (P, 1)))
    put("dt_bias", np.tile(arr["dt_bias"].reshape(1, 8), (P, 1)))
    put("hy_b1", arr["hy_b1"][0])
    put("hy_b2", arr["hy_b2"][0])
    put("hy_freq", arr["hy_freq"][0])
    put("w_router", blocks(arr["w_router"][0], KB))
    put("w_ba", blocks(arr["w_in"][0][:, COL_BA:COL_BA + 16], KB))
    put("hy_w1", arr["hy_w1"][0])
    put("hy_w2", arr["hy_w2"][0])
    put("hy_w3", arr["hy_w3"][0])
    arrays["packed"] = pk
    arrays.update(constants())
    arrays = {k: np.ascontiguousarray(v) for k, v in arrays.items()}
    T = {k: nc.dram_tensor(k + "_dram", v.shape, F32, kind="ExternalInput").ap() for k, v in arrays.items()}
    shapes = {"y_prompt": (1, SEQ_C, D), "y_sample": (1, SEQ_S, D), "state_fwd": (1, 1, HEADS, P, P), "state_bwd": (1, 1, HEADS, P, P)}
    outs = {k: nc.dram_tensor(k + "_out", s, F32, kind="ExternalOutput").ap() for k, s in shapes.items()}
    O = [outs["y_prompt"][0], outs["y_sample"][0], outs["state_fwd"][0, 0], outs["state_bwd"][0, 0]]
    build(nc, T, O)
    r = _run(nc, [{k + "_dram": v for k, v in arrays.items()}], core_ids=[0])
    return tuple(r.results[0][k + "_out"] for k in shapes)
```

```python
from contextlib import ExitStack
import math

import numpy as np
import concourse.bass as bass
from concourse import mybir

F32 = mybir.dt.float32
U32 = mybir.dt.uint32
ALU = mybir.AluOpType
ACT = mybir.ActivationFunctionType
AX = mybir.AxisListType.X

P = 128
D = 1024
KB = D // P
SEQ_S, SEQ_C = 512, 128
TOK = SEQ_S + SEQ_C
NT = TOK // P
ST = SEQ_S // P
HEADS = 4
E = 16
CAP_S, CAP_C = 2 * SEQ_S // E, 2 * SEQ_C // E
ALPHA = 2.0 ** 0.25
HYW = 512
HY_EMB = 33
FREQ_S, FREQ_C = 3 * SEQ_S // 4, 3 * SEQ_C // 4
FT = FREQ_S // P
N_IN = 5648
COL_Q, COL_K, COL_V, COL_Z, COL_BA, COL_HY, COL_G = 0, 512, 1024, 1536, 2048, 2064, 3600
LEVELS = 7
GRID_W = 64

PK = {}
_at = 0
for _name, _n in (("cond", KB * 2), ("b_mod", 48), ("conv_a", 36), ("conv_b", 36), ("conv_bb", 12), ("skip", 4),
                  ("gnorm", 1), ("a_log", 8), ("dt_bias", 8), ("hy_b1", 1), ("hy_b2", 1), ("hy_freq", 1),
                  ("w_router", KB * 32), ("w_ba", KB * 32), ("hy_w1", 64), ("hy_w2", 64), ("hy_w3", HYW)):
    PK[_name] = (_at, _n)
    _at += _n
PK_N = _at

CK = {}
_at = 0
for _name, _n in (("ident", P), ("ones", P), ("eps", 4), ("offset", NT), ("iota", CAP_S), ("first_row", P), ("tri_f", P), ("tri_b", P),
                  ("neg_f", P), ("neg_b", P), ("mask_lo", LEVELS * P), ("mask_up", LEVELS * P)):
    CK[_name] = (_at, _n)
    _at += _n
CK_FIRST = CK["tri_f"][0]
CK_N = _at
FEATS_N = TOK + HYW


def filter_features(l):
    f = np.float32
    t = np.linspace(0.0, 1.0, l, dtype=f)[:, None]
    bands = (HY_EMB - 1) // 2
    w = (f(2.0 * math.pi) * np.arange(l, dtype=f) / f(l))[:, None].astype(f)
    ang = (w * np.linspace(1e-4, bands - 1, bands, dtype=f)[None, :]).astype(f)
    return np.concatenate([t, np.cos(ang), -np.sin(ang)], -1).astype(f).T


def constants():
    ck = np.zeros((P, CK_N), np.float32)

    def put(name, v):
        a, n = CK[name]
        ck[:, a:a + n] = np.asarray(v, np.float32).reshape(P, n)

    i = np.arange(P)
    up = (i[:, None] <= i[None, :])
    put("ident", np.eye(P))
    put("ones", np.ones((P, P)))
    put("tri_f", up)
    put("tri_b", up.T)
    put("neg_f", np.where(up, 0.0, -1e30))
    put("neg_b", np.where(up.T, 0.0, -1e30))
    lo = np.zeros((P, LEVELS, P))
    for lev in range(LEVELS):
        b = 1 << lev
        same = (i[:, None] // (2 * b)) == (i[None, :] // (2 * b))
        lo[:, lev] = same & ((i[:, None] % (2 * b)) >= b) & ((i[None, :] % (2 * b)) < b)
    put("mask_lo", lo)
    put("mask_up", lo.transpose(2, 1, 0))
    put("first_row", (i % 32 == 0)[:, None] * np.ones(P))
    put("iota", np.tile(np.arange(CAP_S), (P, 1)))
    put("eps", np.tile([1e-5, 128e-6, 1e-6, 0.0], (P, 1)))
    off = np.concatenate([np.abs(np.arange(l) - l // 2) / (l // 2) for l in (SEQ_S, SEQ_C)])
    put("offset", -off.reshape(NT, P).T)
    feats = np.zeros((P, FEATS_N), np.float32)
    feats[:HY_EMB, 0:SEQ_S] = filter_features(SEQ_S)
    feats[:HY_EMB, SEQ_S:TOK] = filter_features(SEQ_C)
    deltas = np.abs(np.linspace(math.log(1e-2) / 1.5, math.log(1e-2) / 0.3, HYW, dtype=np.float32))
    feats[:, TOK:] = deltas[None, :]

    def dft(l, nf):
        period = 2 * nf
        ang = 2 * np.pi * ((np.arange(nf) + 0.5)[None, :] * np.arange(l)[:, None] % period) / period
        fwd = np.stack([np.cos(ang), np.sin(ang)], 1)
        out = np.arange(l // 2, l // 2 + l)
        ang = 2 * np.pi * ((np.arange(nf) + 0.5)[:, None] * out[None, :] % (2 * period)) / period
        inv = np.stack([np.cos(ang), np.sin(ang)], 1) * (2.0 / period)
        return fwd, inv

    fs, is_ = dft(SEQ_S, FREQ_S)
    fc, ic = dft(SEQ_C, FREQ_C)
    dft_f = np.zeros((P, 4096), np.float32)
    dft_f[:, 0:ST * 2 * FREQ_S] = fs.reshape(ST, P, 2 * FREQ_S).transpose(1, 0, 2).reshape(P, -1)
    dft_f[:, ST * 2 * FREQ_S:ST * 2 * FREQ_S + 2 * FREQ_C] = fc.reshape(P, -1)
    dft_i = np.zeros((P, 4096), np.float32)
    dft_i[:, 0:FT * 2 * SEQ_S] = is_.reshape(FT, P, 2, SEQ_S).transpose(1, 0, 2, 3).reshape(P, -1)
    dft_i[0:FREQ_C, FT * 2 * SEQ_S:FT * 2 * SEQ_S + 2 * SEQ_C] = ic.reshape(FREQ_C, -1)
    quarter = D // 4
    omega = (1.0 / (10000.0 ** (np.arange(quarter, dtype=np.float32) / np.float32(quarter)))).astype(np.float32)

    def enc(n):
        ang = np.arange(n, dtype=np.float32)[:, None] * omega[None, :]
        return np.concatenate([np.sin(ang), np.cos(ang)], -1).astype(np.float32)

    rows = enc(SEQ_S // GRID_W)
    cols = enc(GRID_W)
    token = np.arange(SEQ_S).reshape(ST, P)
    return {"const_ck": ck, "const_feats": feats, "const_dft_f": dft_f, "const_dft_i": dft_i,
            "pos_row": rows[token // GRID_W].transpose(1, 0, 2), "pos_col": cols[np.arange(P) % GRID_W]}


MAGIC = 1.5 * 2.0 ** 23
TWO_PI = (6.28125, 0.0019350051879882812, 3.019916050e-07)
PI_BELOW = 3.1415925


def build(nc, T, O):
    ctx = ExitStack()
    with ctx:
        def sb(name, cols):
            return ctx.enter_context(nc.sbuf_tensor(name, [P, cols], F32))

        sems = {}

        def sem(name):
            if name not in sems:
                sems[name] = ctx.enter_context(nc.semaphore(name))
            return sems[name]

        SLOT = KB * 512
        ring = sb("ring", 4 * SLOT)
        hbuf = sb("hbuf", NT * D)
        front = sb("front", 23040)
        ck = sb("ck", CK_N)
        pk = sb("pk", PK_N)
        modT = sb("modT", 96)
        misc = sb("misc", 2700)
        dec = sb("dec", 13 * 40)
        stats = sb("stats", NT * 12 + NT * 2 + NT + 24 + NT * 16)
        bank = [ctx.enter_context(nc.psum_tensor(f"bank{i}", [P, 512], F32)) for i in range(8)]

        def C(name):
            a, n = CK[name]
            return ck[:, a:a + n]

        def K(name):
            a, n = PK[name]
            return pk[:, a:a + n]

        def reg(a, n):
            return front[:, a:a + n]

        ident, ones = C("ident"), C("ones")
        eps_ln, eps_q, eps_k = (C("eps")[:, i:i + 1] for i in range(3))
        bn = stats[:, 0:NT * 12].rearrange("p (t s) -> p t s", t=NT)
        mv = stats[:, NT * 12:NT * 14].rearrange("p (t s) -> p t s", t=NT)
        rstd = stats[:, NT * 14:NT * 15]
        ba = stats[:, NT * 15 + 24:NT * 15 + 24 + NT * 16].rearrange("p (t x) -> p t x", t=NT)
        fnorm, fnorm_inv, skip_norm = (stats[:, NT * 15 + 8 * i:NT * 15 + 8 * i + 8] for i in range(3))

        W0 = 12800
        feats = misc[:, 0:FEATS_N]
        hid = [misc[0:64, 1152 + TOK * i:1152 + TOK * (i + 1)] for i in range(2)]
        sin_arg, sin_n = reg(2560, TOK)[0:64], reg(2560 + TOK, TOK)[0:64]
        filt = reg(0, NT * 512).rearrange("p (t c) -> p t c", t=NT)
        absf = reg(2560, NT * 512).rearrange("p (t c) -> p t c", t=NT)
        filtnorm = reg(2560, 1024).rearrange("p (j c) -> p j c", j=2)
        fspec = reg(W0 + 512, 4096).rearrange("p (j c) -> p j c", j=8)
        uspec = reg(W0 + 4608, 4096).rearrange("p (j c) -> p j c", j=8)
        ptmp = reg(W0 + 8704, 1024).rearrange("p (j c) -> p j c", j=2)
        xn = reg(W0 + 5120, 5120).rearrange("p (t d) -> p t d", t=NT)
        posc = reg(W0 + 4608, 512)
        posr = xn.rearrange("p t d -> p (t d)")[:, 0:2048].rearrange("p (t c) -> p t c", t=ST)
        cond32 = misc[:, 2432:2688].rearrange("p (k c) -> p k c", k=KB)
        modrow = misc[:, 1920:2432]
        uT = reg(0, 5120).rearrange("p (k t) -> p k t", k=KB)
        R = [reg(5120 + 2560 * i, 2560).rearrange("p (b t) -> p b t", b=4) for i in range(3)]
        x1T, uuT, x0T = R
        ybT = x0T
        uuTok = reg(5120, 2560).rearrange("p (t c) -> p t c", t=NT)
        h = hbuf[:, :].rearrange("p (t d) -> p t d", t=NT)
        kT = R[0]
        vtok = reg(7680, 2560).rearrange("p (t c) -> p t c", t=NT)
        vT = hbuf[:, 0:2560].rearrange("p (b t) -> p b t", b=4)
        qT = hbuf[:, 2560:5120].rearrange("p (b t) -> p b t", b=4)
        oT = vT
        barow = misc[:, 0:TOK]
        sq = [misc[:, TOK * (1 + i):TOK * (2 + i)] for i in range(2)]
        rn = [reg(W0 + 512 + TOK * i, TOK) for i in range(2)]
        rn_o = reg(W0 + 5120, TOK)

        def field(i, n=40):
            return dec[:, 40 * i:40 * i + n]

        (d_tmp, d_beta, d_negbeta, d_xa, d_neg, d_relu, d_g, d_gc, d_tot, d_negegc, d_edk, d_egl, d_expa) = (
            field(i) for i in range(13))

        def dw(r, i):
            return reg(W0 + 4608 * r + 512 * i, 512).rearrange("p (h c) -> p h c", h=HEADS)

        dD, dLnT, dAT, dKG, dKD, dQG, dM, dU, dVN = ([dw(r, i) for r in range(2)] for i in range(9))
        dW = [misc[:, 512 * r:512 * r + 512].rearrange("p (h c) -> p h c", h=HEADS) for r in range(2)]
        dWT = dLnT
        state = [reg(W0 + 9216 + 512 * r, 512).rearrange("p (h v) -> p h v", h=HEADS) for r in range(2)]
        zT, oG = R[0], R[1]
        sig = reg(W0, 5120).rearrange("p (b t) -> p b t", b=8)
        mixedT = reg(W0 + 5120, 5120).rearrange("p (b t) -> p b t", b=KB)
        uptmp = misc[:, 0:TOK]
        diag = ck[:, CK_FIRST:CK_FIRST + 2048].rearrange("p (c k f) -> p c k f", c=2, k=KB)
        grow = reg(5120, 2048).rearrange("p (c d) -> p c d", c=2)
        lnrow = reg(W0 + 2048, 2048).rearrange("p (j d) -> p j d", j=2)
        otmp = reg(10240, 2048).rearrange("p (j d) -> p j d", j=2)
        xn2 = reg(0, 5120).rearrange("p (t d) -> p t d", t=NT)
        u2T = reg(5120, 5120).rearrange("p (k t) -> p k t", k=KB)
        GA = reg(13312, ST * E * CAP_S).rearrange("p (t c) -> p t c", t=ST)
        GAc = reg(13312 + ST * E * CAP_S, E * CAP_C)
        EW = 18432
        rrow, mask, count = (reg(EW + 2048 + TOK * i, TOK)[0:16, :] for i in range(3))
        lrow = reg(EW, TOK)
        logit = reg(EW + TOK, NT * E).rearrange("p (t e) -> p t e", t=NT)
        top8 = reg(EW + 2048 + 3 * TOK, 8)[0:16, :]
        g2row = misc[:, 640:2688].rearrange("p (c d) -> p c d", c=2)
        probs = dec[:, 0:85].rearrange("p (t e) -> p t e", t=NT)
        slots = dec[:, 85:170].rearrange("p (t e) -> p t e", t=NT)
        rmax, rsum = dec[:, 170:175], dec[:, 175:180]

        def ew(a, n, groups=0):
            v = reg(EW + a, n)
            return v.rearrange("p (g c) -> p g c", g=groups) if groups else v

        xs, xsc = ew(0, 512), ew(512, 256)
        xsT, xcT = ew(768, 512, 8), ew(1280, 256, 8)
        sil, silc = ew(1536, 512), ew(2048, 256)
        hd, hdc = ew(2304, 512), ew(2816, 256)
        hdT, hdcT = ew(3072, 512, 8), ew(3584, 256, 8)
        ys, ysc = ew(3840, 512), ew(4352, 256)
        Gs = misc[:, 0:256].rearrange("p (t c) -> p t c", t=ST)
        Gc = misc[:, 256:288]
        PAIRS = E * CAP_S // P
        ysAll = ring[:, 0:PAIRS * D].rearrange("p (j d) -> p j d", j=PAIRS)
        yscAll = ring[:, 2 * SLOT:2 * SLOT + 2 * D].rearrange("p (j d) -> p j d", j=2)
        ln2row = ring[:, 2 * SLOT + 2 * D:3 * SLOT].rearrange("p (j d) -> p j d", j=2)
        CT = ring[:, 3 * SLOT:4 * SLOT].rearrange("p (j t) -> p j t", j=PAIRS)
        CTc = reg(11264, 256).rearrange("p (j t) -> p j t", j=2)
        ytmp = reg(5120, 2048).rearrange("p (j d) -> p j d", j=2)

        ys_dram = nc.dram_tensor("ys_dram", [E * CAP_S, D], F32, kind="Internal").ap()
        ysc_dram = nc.dram_tensor("ysc_dram", [E * CAP_C, D], F32, kind="Internal").ap()
        h_spill = nc.dram_tensor("h_spill", [P, NT * D], F32, kind="Internal").ap()

        def slot(s):
            return ring[:, s * SLOT:(s + 1) * SLOT] if s < 4 else reg(5120 + (s - 4) * SLOT, SLOT)

        def wslot(s, k=KB):
            return slot(s).rearrange("p (k n) -> p k n", k=k)

        slot_full = [sem(f"slot_full{i}") for i in range(6)]
        w_in = T["w_in"].rearrange("(k p) n -> p k n", p=P)
        w_mod = T["w_mod"].rearrange("(k p) n -> p k n", p=P)
        w_out = T["w_out"].rearrange("(k p) n -> p k n", p=P)

        def cols(w, c):
            return w[:, :, c:c + 512]

        chunks = [(f"mod{n}", (1, 2, 4, 5)[n], cols(w_mod, 512 * n), "mod_mm", 1) for n in range(4)]
        chunks += [("dftF0", 0, T["const_dft_f"], "spec_mm", 4)]

        def mod(n, s):
            return (f"mod{n}", s, cols(w_mod, 512 * n), "mod_mm", n - 2)

        chunks += [("hyx1", 3, cols(w_in, COL_HY + 512), "proj_mm", 4), mod(4, 1), ("hyv", 2, cols(w_in, COL_HY + 1024), "proj_mm", 8),
                   mod(5, 0), ("hyx0", 1, cols(w_in, COL_HY), "proj_mm", 12), mod(6, 3), ("q", 2, cols(w_in, COL_Q), "proj_mm", 16),
                   mod(7, 0), ("dftF1", 1, T["const_dft_f"], "spec_mm", 8), ("k", 3, cols(w_in, COL_K), "proj_mm", 20),
                   mod(8, 2), ("dftI", 0, T["const_dft_i"], "inv_mm", 4), ("v", 1, cols(w_in, COL_V), "proj_mm", 24),
                   ("z", 3, cols(w_in, COL_Z), "proj_mm", 28), mod(9, 2), mod(10, 0),
                   ("ga0", 1, cols(w_in, COL_G), "proj_mm", 32), ("gb0", 3, cols(w_in, COL_G + 1024), "proj_mm", 36), mod(11, 0),
                   ("upa", 2, T["w_up_a"].rearrange("(k p) n -> p k n", p=P), "up_mm", 8),
                   ("upb", 0, T["w_up_b"].rearrange("(k p) n -> p k n", p=P), "up_mm", 8),
                   ("ga1", 1, cols(w_in, COL_G + 512), "proj_mm", 40), ("gb1", 3, cols(w_in, COL_G + 1536), "proj_mm", 44),
                   ("out0", 1, cols(w_out, 0), "out_mm", 10), ("out1", 3, cols(w_out, 512), "out_mm", 10)]
        CH, last_use, fills = {}, [None] * 6, [0] * 6
        loads = []
        for name, s, src, used, value in chunks:
            loads.append((s, src, last_use[s]))
            fills[s] += 1
            CH[name] = (s, 16 * fills[s])
            last_use[s] = (used, value)

        CONV = 24
        rows_of = (SEQ_S, FREQ_C)

        block = ctx.enter_context(nc.Block())

        @block.sync
        def _(sp):
            sp.dma_start(pk[:, :], T["packed"]).then_inc(sem("loaded"), 16)
            sp.dma_start(feats[0:HY_EMB, 0:TOK], T["const_feats"][0:HY_EMB, 0:TOK]).then_inc(sem("loaded"), 16)
            sp.dma_start(feats[:, TOK:], T["const_feats"][:, TOK:]).then_inc(sem("loaded"), 16)
            sp.dma_start(ck[:, 0:CK_FIRST], T["const_ck"][:, 0:CK_FIRST]).then_inc(sem("loaded"), 16)
            for n, (s, src, before) in enumerate(loads):
                if before:
                    sp.wait_ge(sem(before[0]), before[1])
                dst = slot(s)
                if src.shape[-1] != SLOT:
                    dst = wslot(s, src.shape[1])
                sp.dma_start(dst, src).then_inc(slot_full[s], 16)
                if n == 4:
                    sp.dma_start(h[:, 0:ST, :], T["x_sample"].rearrange("(t p) d -> p t d", p=P)).then_inc(sem("x_in"), 16)
                    sp.dma_start(h[:, ST, :], T["x_prompt"]).then_inc(sem("x_in"), 16)
                    sp.dma_start(posc, T["pos_col"]).then_inc(sem("x_in"), 16)
                    sp.dma_start(posr, T["pos_row"]).then_inc(sem("x_in"), 16)
                if n == 5:
                    sp.dma_start(ck[:, CK_FIRST:], T["const_ck"][:, CK_FIRST:]).then_inc(sem("loaded_delta"), 16)
            w_e = [T[w].rearrange("e (k p) n -> p (e k) n", p=P) for w in ("w_e_gate", "w_e_up", "w_e_down")]

            def load(e, s):
                src = w_e[s // 2][:, bass.ds(e * KB, KB), 512 * (s % 2):512 * (s % 2) + 512]
                sp.dma_start(wslot(s), src).then_inc(slot_full[s], 16)

            for s in range(6):
                sp.wait_ge(sem(last_use[s][0]), last_use[s][1])
                if s == 4:
                    sp.wait_ge(sem("router_mm"), 1)
                load(0, s)
            with sp.Fori(1, E) as e:
                for s in range(6):
                    if s < 4:
                        sp.wait_ge(sem("gu_mm"), e * 2 - (1 if s < 2 else 0))
                    else:
                        sp.wait_ge(sem("down_mm"), e)
                    load(e, s)
            sp.wait_ge(sem("gu_mm"), 2 * E)
            sp.dma_start(ln2row[:, 0, :], T["ln2_g"].to_broadcast([P, D])).then_inc(sem("ln2_in"), 16)
            sp.dma_start(ln2row[:, 1, :], T["ln2_b"].to_broadcast([P, D])).then_inc(sem("ln2_in"), 16)
            ys_rows = ys_dram.rearrange("(j p) d -> p j d", p=P)
            ysc_rows = ysc_dram.rearrange("(j p) d -> p j d", p=P)
            sp.wait_ge(sem("ys"), 2 * E - 1)
            sp.dma_start(ysAll[:, 0:PAIRS - 1, :], ys_rows[:, 0:PAIRS - 1, :]).then_inc(sem("ys_back"), 16)
            sp.dma_start(yscAll[:, 0, :], ysc_rows[:, 0, :]).then_inc(sem("ys_back"), 16)
            sp.wait_ge(sem("ys_out"), 96 * E + 1)
            sp.dma_start(ysAll[:, PAIRS - 1, :], ys_rows[:, PAIRS - 1, :]).then_inc(sem("ys_last"), 16)
            sp.dma_start(yscAll[:, 1, :], ysc_rows[:, 1, :]).then_inc(sem("ys_last"), 16)

        def spread_gate(pe, mm, which):
            for c in range(2):
                pe.wait_ge(sem("diag"), 16 * which + KB * (c + 1))
                for k in range(KB):
                    i = mm(bank[SPREAD_BANKS[which][2 * c + k // 4]][:, P * (k % 4):P * (k % 4) + P], ones,
                           diag[:, c, k, :])
                i.then_inc(sem("spread_mm"), 1)

        def delta_pe(pe, mm):
            tri = (C("tri_f"), C("tri_b"))

            def heads(r, b, f):
                for hh in range(HEADS):
                    i = f(hh, bank[4 * r + b][:, P * hh:P * hh + P])
                return i

            def issue_R(p, r):
                gcol = d_g.rearrange("p (t x) -> p t x", t=NT)[:, TILE[r][p], :]
                heads(r, 3, lambda hh, o: mm(o, gcol[:, 4 * r + hh:4 * r + hh + 1].to_broadcast([P, P]), tri[r])) \
                    .then_inc(sem(f"dn_R{r}"), 1)

            def tile(p, r, src, hh):
                return src[:, hh, P * TILE[r][p]:P * TILE[r][p] + P]

            def issue_KK(p, r):
                heads(r, 0, lambda hh, o: mm(o, tile(p, r, kT, hh), tile(p, r, kT, hh))).then_inc(sem(f"dn_KK{r}"), 1)

            for r in range(2):
                issue_R(0, r)
                issue_KK(0, r)
            for p in range(NT):
                def dve(r, step):
                    pe.wait_ge(sem(f"dn_dve{r}"), DVE_N * p + DVE[step])

                def act(r, step):
                    pe.wait_ge(sem(f"dn_act{r}"), ACT_N * p + ACTS[step])

                for r in range(2):
                    pe.wait_ge(sem(f"dn_LT{r}"), 4 * (p + 1))
                    heads(r, 0, lambda hh, o: pe.transpose(o, dLnT[r][:, hh, :], ident)).then_inc(sem(f"dn_pe{r}"), 1)
                for lev in range(1, LEVELS):
                    for r in range(2):
                        dve(r, f"PM{lev - 1}")
                        heads(r, 0, lambda hh, o: mm(o, dLnT[r][:, hh, :], dM[r][:, hh, :])).then_inc(sem(f"dn_pe{r}"), 1)
                        if lev == 1:
                            act(r, "EG")
                            heads(r, 3, lambda hh, o: mm(o, tile(p, r, kT, hh), tile(p, r, qT, hh))).then_inc(sem(f"dn_pe{r}"), 1)
                        if lev == KT_LEVEL:
                            dve(r, "AT")
                            heads(r, 3, lambda hh, o: pe.transpose(o, tile(p, r, kT, hh), ident)).then_inc(sem(f"dn_pe{r}"), 1)
                    for r in range(2):
                        if lev == 1 and p:
                            pe.wait_ge(sem(f"dn_o{r}"), 5 * p)
                        act(r, f"W{lev}")
                        dve(r, f"P{lev - 1}")
                        if lev < LEVELS - 1:
                            heads(r, 1, lambda hh, o: mm(o, dU[r][:, hh, :], dW[r][:, hh, :])).then_inc(sem(f"dn_pe{r}"), 1)
                        heads(r, 2, lambda hh, o: mm(o, dW[r][:, hh, :], dU[r][:, hh, :])).then_inc(sem(f"dn_pe{r}"), 1)
                for r in range(2):
                    dve(r, f"P{LEVELS - 1}")
                    pe.wait_ge(sem(f"dn_kgd{r}"), 8 * (p + 1))
                    heads(r, 3, lambda hh, o: mm(o, dKG[r][:, hh, :], dU[r][:, hh, :])).then_inc(sem(f"dn_pe{r}"), 1)
                for r in range(2):
                    act(r, "WT")
                    if p == 0:
                        pe.wait_ge(sem("state_in"), 32)
                    for hh in range(HEADS):
                        o = bank[4 * r][:, P * hh:P * hh + P]
                        mm(o, dU[r][:, hh, :], vtok[:, TILE[r][p], P * hh:P * hh + P], 0, 2)
                        i = mm(o, dWT[r][:, hh, :], state[r][:, hh, :], 1, 2)
                    i.then_inc(sem(f"dn_pe{r}"), 1)
                    if p + 1 < NT:
                        issue_R(p + 1, r)
                for r in range(2):
                    dve(r, "VN")
                    for hh in range(HEADS):
                        o = bank[4 * r + 1][:, P * hh:P * hh + P]
                        mm(o, state[r][:, hh, :], dQG[r][:, hh, :], 0, 2)
                        mm(o, dVN[r][:, hh, :], dAT[r][:, hh, :], 1, 2)
                    heads(r, 2, lambda hh, o: mm(o, dKD[r][:, hh, :], dVN[r][:, hh, :])).then_inc(sem(f"dn_pe{r}"), 1)
                    if p + 1 < NT:
                        issue_KK(p + 1, r)

        def by_block(b, a, width, n):
            return bank[b][:, a:a + P * n].rearrange("p (j h s) -> p h j s", j=n, s=width)

        @block.tensor
        def _(pe):
            def mm(out, lhsT, rhs, k=0, n=1):
                return pe.matmul(out, lhsT, rhs, start=(k == 0), stop=(k == n - 1))

            def full(name):
                pe.wait_ge(slot_full[CH[name][0]], CH[name][1])

            def spectrum(table, src, read, per_output):
                for j in range(FT + 1):
                    A, B = bank[4 + 2 * (j % 2)], bank[5 + 2 * (j % 2)]
                    if j >= 2:
                        pe.wait_ge(sem(read), per_output * (j - 1))
                    for out, cs in ((A, 0), (B, 1)):
                        if j < FT:
                            for t in range(ST):
                                at = 2 * FREQ_S * t + FREQ_S * cs + P * j
                                i = mm(out[:, :], table[:, at:at + P], src[:, t, :], t, ST)
                        else:
                            at = 2 * FREQ_S * ST + FREQ_C * cs
                            i = mm(out[0:FREQ_C, :], table[:, at:at + FREQ_C], src[:, ST, :])
                    i.then_inc(sem("spec_mm"), 1)

            def transpose_tokens(src, ready, read):
                for k in range(KB):
                    if k >= 2:
                        pe.wait_ge(sem(read), k - 1)
                        pe.wait_ge(sem(read + "_prompt"), k - 1)
                    for t in range(ST):
                        pe.transpose(bank[2 + k % 2][:, P * t:P * t + P], src[:, t, P * k:P * k + P], ident)
                    pe.transpose(bank[k % 2][:, 0:P], src[:, ST, P * k:P * k + P], ident).then_inc(sem(ready), 1)

            pe.wait_ge(sem("loaded"), 64)
            for layer, (w, rows) in enumerate((("hy_w1", HY_EMB), ("hy_w2", 64))):
                rhs = feats if layer == 0 else hid[0]
                if layer:
                    pe.wait_ge(sem("hid"), 1)
                mm(bank[2 * layer][0:64, :], K(w)[0:rows, :], rhs[0:rows, 0:SEQ_S])
                mm(bank[2 * layer + 1][0:64, 0:SEQ_C], K(w)[0:rows, :], rhs[0:rows, SEQ_S:TOK]).then_inc(sem("hid_mm"), 1)
            pe.wait_ge(sem("hid"), 2)
            for t in range(NT):
                mm(bank[4 + t if t < 4 else 0][:, :], hid[1][:, P * t:P * t + P], K("hy_w3")[0:64, :]).then_inc(sem("filt_mm"), 1)
            pe.wait_ge(sem("cond"), 2)
            for j in range(4):
                full(f"mod{j}")
            for k in range(KB):
                for j in range(4):
                    i = mm(bank[3][32 * j:32 * j + 32, :], cond32[:, k, :], wslot(CH[f"mod{j}"][0])[:, k, :], k, KB)
            i.then_inc(sem("mod_mm"), 1)

            full("dftF0")
            pe.wait_ge(sem("filt"), NT)
            spectrum(slot(CH["dftF0"][0]), filt, "fspec", 2)
            pe.wait_ge(sem("filt_abs"), NT)
            for t in range(NT):
                i = mm(bank[1 if t < ST else 2][:, :], ones, absf[:, t, :], t % ST, ST if t < ST else 1)
            i.then_inc(sem("filt_sum"), 1)

            pe.wait_ge(sem("fspec"), 8)

            def mod_transpose(n):
                pe.wait_ge(sem("mod_row"), n + 1)
                if n:
                    pe.wait_ge(sem("mod_col"), 2 * n + 1)
                for i in range(4):
                    tr = pe.transpose(bank[7][:, P * i:P * i + P], modrow[:, P * i:P * i + P], ident)
                tr.then_inc(sem("mod_tr"), 1)

            def mod_product(c, read=None, value=0):
                full(f"mod{c}")
                if read:
                    pe.wait_ge(sem(read), value)
                for k in range(2):
                    for j in range(4):
                        i = mm(bank[6][32 * j:32 * j + 32, :], cond32[:, 2 * j + k, :], wslot(CH[f"mod{c}"][0])[:, 2 * j + k, :], k, 2)
                i.then_inc(sem("mod_mm"), 1)

            pe.wait_ge(sem("norm_row"), 2)
            for j in range(2):
                for cb in range(4):
                    i = pe.transpose(bank[1 + j][:, P * cb:P * cb + P], filtnorm[:, j, P * cb:P * cb + P], ident)
            i.then_inc(sem("norm_tr"), 1)
            mod_transpose(0)
            pe.wait_ge(sem("fnorm"), 2)
            pe.wait_ge(sem("xn"), NT)
            transpose_tokens(xn, "xnT_mm", "uT")

            done = [0]

            def project(name, before={}):
                s = CH[name][0]
                full(name)
                for b in range(4):
                    n = done[0]
                    if b in before:
                        before[b]()
                    if 2 <= n < CONV + 2:
                        pe.wait_ge(sem("conv"), 4 * (n - 1))
                    elif n >= CONV + 2:
                        pe.wait_ge(sem("zg"), 2 * (n - 1 - CONV))
                    for k in range(KB):
                        mm(bank[n % 2][:, :], wslot(s)[:, k, P * b:P * b + P], uT[:, k, 0:SEQ_S], k, KB)
                        i = mm(bank[2 + n % 2][:, 0:SEQ_C], wslot(s)[:, k, P * b:P * b + P], uT[:, k, SEQ_S:TOK], k, KB)
                    i.then_inc(sem("proj_mm"), 1)
                    done[0] += 1

            pe.wait_ge(sem("uT"), KB)
            pe.wait_ge(sem("uT_prompt"), KB)
            project("hyx1", {1: lambda: mod_product(4), 3: lambda: mod_transpose(1)})
            project("hyv", {1: lambda: mod_product(5), 3: lambda: mod_transpose(2)})
            project("hyx0", {1: lambda: mod_product(6), 3: lambda: mod_transpose(3)})
            pe.wait_ge(sem("uu"), 4)
            for t in range(NT):
                if t >= 2:
                    pe.wait_ge(sem("uutok"), t - 1)
                for cb in range(4):
                    i = pe.transpose(bank[4 + t % 2][:, P * cb:P * cb + P], uuT[:, cb, P * t:P * t + P], ident)
                i.then_inc(sem("uutok_mm"), 1)
            project("q", {1: lambda: mod_product(7), 3: lambda: mod_transpose(4)})
            pe.wait_ge(sem("uutok"), NT)
            pe.wait_ge(sem("mod_col"), 11)
            full("dftF1")
            spectrum(slot(CH["dftF1"][0]), uuTok, "product", 6)

            def square_sums(done, mm_done, heads_, A, B, n0):
                for n in heads_:
                    pe.wait_ge(sem(done), n0 + n + 1)
                    o = slice(32 * n, 32 * n + 32)
                    mm(bank[A][o, :], ones[:, 0:32], sq[n % 2][:, 0:SEQ_S])
                    mm(bank[B][o, 0:SEQ_C], ones[:, 0:32], sq[n % 2][:, SEQ_S:TOK]).then_inc(sem(mm_done), 1)

            def spread_head(n, v, A, B, spread):
                o = slice(32 * n, 32 * n + 32)
                mm(bank[A][:, :], C("first_row")[o, :], v[o, 0:SEQ_S])
                mm(bank[B][:, 0:SEQ_C], C("first_row")[o, :], v[o, SEQ_S:TOK]).then_inc(sem(spread), 1)

            def k_second():
                square_sums("sq", "norm_mm", (0, 1), 4, 5, 0)

            def k_third():
                mod_transpose(5)
                square_sums("sq", "norm_mm", (2, 3), 4, 5, 0)

            project("k", {1: lambda: mod_product(8, "product", 6 * (FT + 1)), 2: k_second, 3: k_third})
            pe.wait_ge(sem("mod_col"), 13)
            pe.wait_ge(sem("norm_root"), 2)
            full("dftI")
            inv = slot(CH["dftI"][0])
            pe.wait_ge(sem("product"), 6 * (FT + 1))
            for cb in range(4):
                A, B = bank[4 + 2 * (cb % 2)], bank[5 + 2 * (cb % 2)]
                if cb >= 2:
                    pe.wait_ge(sem("yb"), 4 * (cb - 1))
                for j in range(2 * FT):
                    mm(A[:, :], uspec[:, j, P * cb:P * cb + P], inv[:, 512 * j:512 * j + 512], j, 2 * FT)
                for j in range(2):
                    at = 2 * FT * 512 + SEQ_C * j
                    i = mm(B[:, 0:SEQ_C], uspec[0:FREQ_C, 2 * FT + j, P * cb:P * cb + P], inv[0:FREQ_C, at:at + SEQ_C], j, 2)
                i.then_inc(sem("inv_mm"), 1)

            def v_hook(b):
                def f():
                    if b == 1:
                        pe.wait_ge(sem("yb"), 16)
                        pe.wait_ge(sem("rn"), 1)
                    else:
                        pe.wait_ge(sem("qk_normal"), 2 * (b - 1))
                    spread_head(b - 1, rn[0], 6, 7, "qk_spread")
                    if b < 3:
                        square_sums("sq", "norm_mm", (2 * b - 2, 2 * b - 1), 4, 5, 4)
                return f

            project("v", {b: v_hook(b) for b in (1, 2, 3)})

            pe.wait_ge(sem("qk_normal"), 6)
            spread_head(3, rn[0], 6, 7, "qk_spread")
            wba = K("w_ba").rearrange("p (k n) -> p k n", k=KB)
            pe.wait_ge(sem("conv"), 4 * (CONV - 1))
            for k in range(2):
                for j in range(4):
                    mm(bank[0][32 * j:32 * j + 32, :], wba[:, 2 * j + k, :], uT[:, 2 * j + k, 0:SEQ_S], k, 2)
            for k in range(2):
                for j in range(4):
                    i = mm(bank[2][32 * j:32 * j + 32, 0:SEQ_C], wba[:, 2 * j + k, :], uT[:, 2 * j + k, SEQ_S:TOK], k, 2)
            i.then_inc(sem("ba_mm"), 1)
            pe.wait_ge(sem("rn"), 2)
            spread_head(0, rn[1], 4, 5, "qk_spread")
            pe.wait_ge(sem("ba_row"), 2)
            pe.wait_ge(sem("conv"), 4 * CONV)
            for t in range(NT):
                i = pe.transpose(bank[1 if t < ST else 3][:, P * (t % ST):P * (t % ST) + P], barow[:, P * t:P * t + P], ident)
            i.then_inc(sem("ba_tr"), 1)

            def v_tokens(t):
                if t >= 2:
                    pe.wait_ge(sem("vtok"), t - 1)
                for hd_ in range(HEADS):
                    i = pe.transpose(bank[(0, 3)[t % 2]][:, P * hd_:P * hd_ + P], vT[:, hd_, P * t:P * t + P], ident)
                i.then_inc(sem("vtok_mm"), 1)

            pe.wait_ge(sem("qk_normal"), 8)
            spread_head(1, rn[1], 6, 7, "qk_spread")
            pe.wait_ge(sem("qkv_act"), 12)
            v_tokens(0)
            pe.wait_ge(sem("dec"), 2)
            v_tokens(1)
            pe.wait_ge(sem("qk_normal"), 10)
            spread_head(2, rn[1], 4, 5, "qk_spread")
            v_tokens(2)
            pe.wait_ge(sem("dec"), DEC_G)
            pe.wait_ge(sem("loaded_delta"), 16)
            gv = d_g.rearrange("p (t x) -> p t x", t=NT)
            mm(bank[2][:, 0:20], C("tri_f"), gv[:, :, 0:4])
            mm(bank[2][:, 32:52], C("tri_b"), gv[:, :, 4:8])
            mm(bank[2][:, 64:104], ones, d_g).then_inc(sem("gc_mm"), 1)
            v_tokens(3)
            v_tokens(4)
            pe.wait_ge(sem("qk_normal"), 12)
            spread_head(3, rn[1], 6, 7, "qk_spread")
            pe.wait_ge(sem("vtok"), NT)
            pe.wait_ge(sem("dec"), DEC_ALL)
            pe.wait_ge(sem("qk_normal"), 16)
            delta_pe(pe, mm)


            def z_first():
                pe.wait_ge(sem("dn_o1"), 5 * NT)
                mod_product(9)
                square_sums("osq", "onorm_mm", (0, 1), 4, 5, 0)

            def z_second():
                mod_transpose(6)
                mod_product(10)
                square_sums("osq", "onorm_mm", (2, 3), 4, 5, 0)

            pe.wait_ge(sem("dn_o0"), 5 * NT)
            project("z", {1: z_first, 2: z_second, 3: lambda: mod_transpose(7)})
            pe.wait_ge(sem("mod_col"), 17)
            pe.wait_ge(sem("rn"), 3)

            def o_hook(n):
                def f():
                    if n >= 2:
                        pe.wait_ge(sem("og"), 3 * (n - 1))
                    spread_head(n, rn_o, 4 + 2 * (n % 2), 5 + 2 * (n % 2), "o_spread")
                return f

            for half in range(2):
                if half:
                    pe.wait_ge(sem("mixed"), 15)
                    spread_gate(pe, mm, 0)
                    pe.wait_ge(sem("mixed"), 20)
                project(f"ga{half}", {n: o_hook(n) for n in range(HEADS)} if half == 0 else {})
                project(f"gb{half}", {1: lambda: mod_product(11, "og", 3 * HEADS), 3: lambda: mod_transpose(8)} if half == 0 else {})
                if half == 0:
                    full("upa")
                    full("upb")
                    pe.wait_ge(sem("og"), 3 * HEADS)
                    pe.wait_ge(sem("mod_col"), 19)
                if half:
                    pe.wait_ge(sem("gate_row"), 4)
                for b in range(4):
                    n = 4 * half + b
                    if b == 1:
                        pe.wait_ge(sem("zg"), 2 * (12 + 8 * half))
                    if n >= 2:
                        pe.wait_ge(sem("mixed"), 5 * (n - 1))
                    banks = (4, 5, 6, 7) if n % 2 == 0 else (0, 2, 1, 3)
                    for w, src, A, B in (("upa", oG, banks[0], banks[1]), ("upb", ybT, banks[2], banks[3])):
                        for k in range(4):
                            lw = wslot(CH[w][0], 4)[:, k, P * n:P * n + P]
                            mm(bank[A][:, :], lw, src[:, k, 0:SEQ_S], k, 4)
                            i = mm(bank[B][:, 0:SEQ_C], lw, src[:, k, SEQ_S:TOK], k, 4)
                    i.then_inc(sem("up_mm"), 1)
            full("out0")
            full("out1")
            for t in range(NT):
                for c in range(2):
                    n = 2 * t + c
                    if n >= 4:
                        pe.wait_ge(sem("out_read"), n - 3)
                    for k in range(KB):
                        if n == 0 and k == KB - 1:
                            pe.wait_ge(sem("mixed"), 5 * KB)
                        elif n == 0 and k == 0:
                            pe.wait_ge(sem("mixed"), 5 * (KB - 1))
                        i = mm(bank[4 + n % 4][:, :], mixedT[:, k, P * t:P * t + P], wslot(CH[f"out{c}"][0])[:, k, :], k, KB)
                    i.then_inc(sem("out_mm"), 1)
            pe.wait_ge(sem("xn2"), NT)
            transpose_tokens(xn2, "xn2T_mm", "u2T")
            pe.wait_ge(sem("u2T"), KB)
            pe.wait_ge(sem("u2T_prompt"), KB)
            wr = K("w_router").rearrange("p (k n) -> p k n", k=KB)
            for bank_, a, n in ((4, 0, SEQ_S), (5, SEQ_S, SEQ_C)):
                for k in range(2):
                    for j in range(4):
                        i = mm(bank[bank_][32 * j:32 * j + 32, 0:n], wr[:, 2 * j + k, :], u2T[:, 2 * j + k, a:a + n], k, 2)
            i.then_inc(sem("router_mm"), 1)
            pe.wait_ge(sem("logit_row"), 2)
            for t in range(NT):
                i = pe.transpose(bank[2 if t < ST else 6][:, P * (t % ST):P * (t % ST) + P], lrow[:, P * t:P * t + P], ident)
            i.then_inc(sem("logit_tr"), 1)
            spread_gate(pe, mm, 1)
            pe.wait_ge(sem("probs"), 1)
            for t in range(NT):
                i = pe.transpose(bank[6 + t // 4][0:16, P * (t % 4):P * (t % 4) + P], probs[:, t, 0:E], ident)
            i.then_inc(sem("prob_tr"), 1)
            pe.wait_ge(sem("slot_row"), 1)
            for t in range(NT):
                i = pe.transpose(bank[5][:, 16 * t:16 * t + 16], rrow[:, P * t:P * t + P], ident[0:16, 0:16])
            i.then_inc(sem("slot_tr"), 1)

            def gather(n):
                pe.wait_ge(sem("onehot"), 5 * n + 5)
                for t in range(ST):
                    for half in range(2):
                        mm(bank[3][64 * half:64 * half + 64, :], Gs[:, t, :], xn2[:, t, 512 * half:512 * half + 512], t, ST)
                for q in range(4):
                    i = mm(bank[4][32 * q:32 * q + 32, 0:256], Gc, xn2[:, ST, 256 * q:256 * q + 256])
                i.then_inc(sem("gather_mm"), 1)

            def gather_transpose(n):
                pe.wait_ge(sem("gathered"), 2 * n + 2)
                for j in range(4):
                    pe.transpose(bank[3][:, P * j:P * j + P], xs[:, P * j:P * j + P], ident)
                for j in range(2):
                    i = pe.transpose(bank[4][:, P * j:P * j + P], xsc[:, P * j:P * j + P], ident)
                i.then_inc(sem("xT_mm"), 1)

            pe.wait_ge(sem("g2row"), 4)
            pe.wait_ge(sem("slots"), 2)
            gather(0)
            gather_transpose(0)
            with pe.Fori(0, E) as e:
                pe.wait_ge(sem("xT"), e * 4 + 4)
                for which, out, outc in ((0, bank[0], bank[2][:, 0:256]), (1, bank[1], bank[5][:, 256:512])):
                    if which:
                        pe.wait_ge(sem("ys"), e * 2 + 1)
                    for half in range(2):
                        pe.wait_ge(slot_full[2 * which + half], e * 16 + (16 * fills[2 * which + half] + 16))
                    for k in range(KB):
                        for half in range(2):
                            mm(out[64 * half:64 * half + 64, :], xsT[:, k, :], wslot(2 * which + half)[:, k, :], k, KB)
                    for k in range(KB):
                        for q in range(4):
                            i = mm(outc[32 * q:32 * q + 32, :], xcT[:, k, :],
                                   wslot(2 * which + q // 2)[:, k, 256 * (q % 2):256 * (q % 2) + 256], k, KB)
                    i.then_inc(sem("gu_mm"), 1)
                gather(e + 1)
                pe.wait_ge(sem("hid_e"), e * 2 + 2)
                for j in range(4):
                    i = pe.transpose(bank[6][:, P * j:P * j + P], hd[:, P * j:P * j + P], ident)
                i.then_inc(sem("hidT_mm"), 1)
                for j in range(2):
                    i = pe.transpose(bank[2][:, 256 + P * j:256 + P * j + P], hdc[:, P * j:P * j + P], ident)
                i.then_inc(sem("hidT_mm"), 1)
                gather_transpose(e + 1)
                pe.wait_ge(sem("hidT"), e + 1)
                for half in range(2):
                    pe.wait_ge(slot_full[4 + half], e * 16 + (16 * fills[4 + half] + 16))
                for k in range(KB):
                    for half in range(2):
                        mm(bank[7][64 * half:64 * half + 64, :], hdT[:, k, :], wslot(4 + half)[:, k, :], k, KB)
                pe.wait_ge(sem("hidTc"), e + 1)
                for k in range(KB):
                    for q in range(4):
                        i = mm(bank[5][32 * q:32 * q + 32, 0:256], hdcT[:, k, :],
                               wslot(4 + q // 2)[:, k, 256 * (q % 2):256 * (q % 2) + 256], k, KB)
                i.then_inc(sem("down_mm"), 1)
            pe.wait_ge(sem("weighted"), 5 * E)
            for j in range(PAIRS):
                if j >= 4:
                    pe.wait_ge(sem("ct"), j - 3)
                for t in range(ST):
                    i = pe.transpose(bank[(0, 1, 2, 6)[j % 4]][:, P * t:P * t + P], GA[:, t, P * j:P * j + P], ident)
                i.then_inc(sem("ct_mm"), 1)
            pe.wait_ge(sem("ct"), PAIRS - 3)
            for j in range(2):
                i = pe.transpose(bank[0][:, P * j:P * j + P], GAc[:, P * j:P * j + P], ident)
            i.then_inc(sem("ct_mm"), 1)
            pe.wait_ge(sem("ct"), PAIRS)
            pe.wait_ge(sem("xT"), 4 * E + 4)
            pe.wait_ge(sem("ys_back"), 32)
            for n, t in enumerate(SCATTER_ORDER):
                kn = PAIRS if t < ST else 2
                if n == 1:
                    pe.wait_ge(sem("ct"), PAIRS + 1)
                    pe.wait_ge(sem("ys"), 2 * E + 1)
                if n == len(SCATTER_ORDER) - 1:
                    pe.wait_ge(sem("y_read"), 2)
                steps_ = [(k, half) for k in range(kn) for half in range(2)] if n == 0 else \
                         [(k, half) for half in range(2) for k in range(kn)]
                for k, half in steps_:
                    if n == 0 and k == kn - 1 and half == 0:
                        pe.wait_ge(sem("ys_last"), 32)
                    cut = slice(512 * half, 512 * half + 512)
                    if t < ST:
                        lw, rhs = CT[:, k, P * t:P * t + P], ysAll[:, k, cut]
                    else:
                        lw, rhs = CTc[:, k, :], yscAll[:, k, cut]
                    i = mm(bank[SCATTER_BANKS[n][half]][:, :], lw, rhs, k, kn)
                    if k == kn - 1:
                        i.then_inc(sem("y_mm"), 1)

        @block.scalar
        def _(act):
            A = nc.scalar.activation
            act.wait_ge(sem("loaded"), 64)
            for t in range(NT):
                A(filt[:, t, :], feats[:, TOK:TOK + 512], ACT.Exp, scale=C("offset")[:, t:t + 1]).then_inc(sem("window"), 1)
            for n in range(2):
                act.wait_ge(sem("sin_arg"), 9 * (n + 1))
                A(hid[n], sin_arg, ACT.Sin).then_inc(sem("hid"), 1)
            act.wait_ge(sem("cond"), 1)
            A(cond32[:, :, 0:2], K("cond").rearrange("p (k c) -> p k c", k=KB), ACT.Silu).then_inc(sem("cond"), 1)
            for t in range(NT):
                act.wait_ge(sem("filt"), t + 1)
                A(absf[:, t, :], filt[:, t, :], ACT.Abs).then_inc(sem("filt_abs"), 1)
            for j in range(FT + 1):
                act.wait_ge(sem("spec_mm"), j + 1)
                r = P if j < FT else FREQ_C
                for cs in range(2):
                    A(fspec[0:r, 2 * j + cs, :], bank[4 + 2 * (j % 2) + cs][0:r, :], ACT.Copy).then_inc(sem("fspec"), 1)
                if j == 1:
                    act.wait_ge(sem("moments"), NT)
                    A(rstd, mv[:, :, 1], ACT.Sqrt, bias=eps_ln).then_inc(sem("root"), 1)
            act.wait_ge(sem("filt_sum"), 1)
            for j in range(2):
                A(filtnorm[:, j, :], bank[1 + j][:, :], ACT.Copy).then_inc(sem("norm_row"), 1)
            act.wait_ge(sem("h"), 2)
            act.dma_start(h_spill.rearrange("p (t d) -> p t d", t=NT), h).then_inc(sem("spilled"), 16)

            def modulate(dst, mm_done, out, sc, sh):
                for k in range(KB):
                    act.wait_ge(sem(mm_done), k + 1)
                    A(dst[:, k, 0:SEQ_S], bank[2 + k % 2][:, :], ACT.Identity, bias=modT[:, sh + k:sh + k + 1],
                      scale=modT[:, sc + k:sc + k + 1]).then_inc(sem(out), 1)

            act.wait_ge(sem("mod_col"), 3)
            modulate(uT, "xnT_mm", "uT", 8, 0)

            conv_dst = [x1T] * 4 + [uuT] * 4 + [x0T] * 4 + [qT] * 4 + [kT] * 4 + [vT] * 4

            def tap(n):
                act.wait_ge(sem("proj_mm"), n + 1)
                if n == 12:
                    act.wait_ge(sem("spilled"), 16)
                if n < 12:
                    w = K("conv_b").rearrange("p (b j) -> p b j", j=3)[:, HY_BLOCK[n], 1:2]
                    bias = K("conv_bb")[:, HY_BLOCK[n]:HY_BLOCK[n] + 1]
                else:
                    w, bias = K("conv_a").rearrange("p (b j) -> p b j", j=3)[:, n - 12, 1:2], 0.0
                d = conv_dst[n][:, n % 4, :]
                A(d[:, 0:SEQ_S], bank[n % 2][:, :], ACT.Identity, bias=bias, scale=w).then_inc(sem("tap"), 1)
                A(d[:, SEQ_S:TOK], bank[2 + n % 2][:, 0:SEQ_C], ACT.Identity, bias=bias, scale=w).then_inc(sem("tap"), 1)

            def silu(n):
                act.wait_ge(sem("conv"), 4 * (n + 1))
                d = conv_dst[n][:, n % 4, :]
                A(d, d, ACT.Silu).then_inc(sem("qkv_act"), 1)

            def mod_rows(n):
                act.wait_ge(sem("mod_mm"), n + 1)
                if n:
                    act.wait_ge(sem("mod_tr"), n)
                A(modrow, bank[6][:, :], ACT.Copy).then_inc(sem("mod_row"), 1)

            for n in range(12):
                if n % 4 == 1:
                    mod_rows(n // 4 + 1)
                tap(n)
            for t in range(NT):
                act.wait_ge(sem("uutok_mm"), t + 1)
                A(uuTok[:, t, :], bank[4 + t % 2][:, :], ACT.Copy).then_inc(sem("uutok"), 1)
            def square(n):
                if n >= 2:
                    act.wait_ge(sem("norm_mm"), n - 1)
                else:
                    act.wait_ge(sem("qkv_act"), n + 1)
                if n >= 4:
                    act.wait_ge(sem("qkv_act"), n + 1)
                A(sq[n % 2], (qT if n < 4 else kT)[:, n % 4, :], ACT.Square).then_inc(sem("sq"), 1)

            def root(v, mm_done, count_, out, **kw):
                act.wait_ge(sem(mm_done), count_)
                A(v[:, 0:SEQ_S], bank[4][:, :], ACT.Sqrt, **kw).then_inc(sem(out), 1)
                A(v[:, SEQ_S:TOK], bank[5][:, 0:SEQ_C], ACT.Sqrt, **kw).then_inc(sem(out), 1)

            for n in range(12, 16):
                if n == 13:
                    mod_rows(4)
                tap(n)
                if n > 12:
                    silu(n - 1)
            tap(16)
            silu(15)
            square(0)
            square(1)
            mod_rows(5)
            tap(17)
            silu(16)
            square(2)
            square(3)
            tap(18)
            silu(17)
            act.wait_ge(sem("product"), 6 * (FT + 1))
            root(rn[0], "norm_mm", 4, "norm_root", bias=eps_q, scale=float(P))
            tap(19)
            silu(18)
            silu(19)
            square(4)
            square(5)
            tap(20)
            square(6)
            square(7)
            tap(21)
            silu(20)
            root(rn[1], "norm_mm", 8, "norm_root", bias=eps_k, scale=1.0)
            tap(22)
            silu(21)
            tap(23)
            silu(22)
            silu(23)
            act.wait_ge(sem("dec"), 2)
            A(d_tmp.rearrange("p (t x) -> p t x", t=NT), ba[:, :, 0:8], ACT.Exp, scale=-1.0).then_inc(sem("dec_act"), 1)
            A(d_expa[:, 0:8], K("a_log"), ACT.Exp).then_inc(sem("dec_act"), 1)
            act.wait_ge(sem("dec"), DEC_NEG)
            A(d_neg, d_neg, ACT.Exp).then_inc(sem("dec_act"), 1)
            act.wait_ge(sem("dec_act"), 3)
            A(d_neg, d_neg, ACT.Ln, bias=1.0).then_inc(sem("dec_act"), 1)
            for t in range(NT):
                act.wait_ge(sem("vtok_mm"), t + 1)
                A(vtok[:, t, :], bank[(0, 3)[t % 2]][:, :], ACT.Copy).then_inc(sem("vtok"), 1)
            act.wait_ge(sem("dec"), DEC_GC)
            A(d_negegc, d_gc, ACT.Exp).then_inc(sem("dec_act"), 1)
            A(d_edk, d_edk, ACT.Exp).then_inc(sem("dec_act"), 1)
            A(d_egl, d_tot, ACT.Exp).then_inc(sem("dec_act"), 1)
            def decays(p, r):
                act.wait_ge(sem(f"dn_E{r}"), 4 * (p + 1))
                A(dD[r], dD[r], ACT.Exp).then_inc(sem(f"dn_D{r}"), 1)

            for p in range(NT):
                def pe_(r, step):
                    act.wait_ge(sem(f"dn_pe{r}"), PE_N * p + PES[step])

                def bank4(r, b):
                    return bank[4 * r + b][:, :].rearrange("p (h c) -> p h c", h=HEADS)

                if p == 0:
                    act.wait_ge(sem("qk_normal"), 16)
                    act.wait_ge(sem("inv_mm"), 4)
                    for r, name in enumerate(("state_delta_fwd", "state_delta_bwd")):
                        act.dma_start(state[r], T[name].rearrange("h k v -> k h v")).then_inc(sem("state_in"), 16)
                    for r in range(2):
                        decays(0, r)
                for r in range(2):
                    if p:
                        act.wait_ge(sem(f"dn_pe{r}"), PE_N * p)
                    act.wait_ge(sem(f"dn_R{r}"), p + 1)
                    A(dQG[r], bank4(r, 3), ACT.Exp).then_inc(sem(f"dn_act{r}"), 1)
                for lev in range(1, LEVELS):
                    for r in range(2):
                        pe_(r, f"W{lev}")
                        A(dW[r], bank4(r, 0), ACT.Copy).then_inc(sem(f"dn_act{r}"), 1)
                    if lev >= KT_LEVEL and lev < KT_LEVEL + 2:
                        r = lev - KT_LEVEL
                        pe_(r, "KT")
                        for dst, scale in ((dKG, d_negegc), (dKD, d_edk)):
                            for hh in range(HEADS):
                                x = 8 * TILE[r][p] + 4 * r + hh
                                A(dst[r][:, hh, :], bank[4 * r + 3][:, P * hh:P * hh + P], ACT.Copy, scale=scale[:, x:x + 1]) \
                                    .then_inc(sem(f"dn_kgd{r}"), 1)
                for r in range(2):
                    pe_(r, "WT")
                    A(dWT[r], bank4(r, 3), ACT.Copy).then_inc(sem(f"dn_act{r}"), 1)
                if p + 1 < NT:
                    for r in range(2):
                        decays(p + 1, r)
            for r in range(2):
                act.wait_ge(sem(f"dn_o{r}"), 5 * NT)
                act.dma_start(O[2 + r].rearrange("h k v -> k h v"), state[r]).then_inc(sem("out_done"), 16)

            def gate(n, f, dst):
                act.wait_ge(sem("proj_mm"), n + 1)
                A(dst[:, 0:SEQ_S], bank[n % 2][:, :], f).then_inc(sem("zg"), 1)
                A(dst[:, SEQ_S:TOK], bank[2 + n % 2][:, 0:SEQ_C], f).then_inc(sem("zg"), 1)


            def o_square(n):
                if n >= 2:
                    act.wait_ge(sem("onorm_mm"), n - 1)
                A(sq[n % 2], oT[:, n, :], ACT.Square).then_inc(sem("osq"), 1)

            o_square(0)
            o_square(1)
            gate(CONV, ACT.Silu, zT[:, 0, :])
            mod_rows(6)
            o_square(2)
            o_square(3)
            gate(CONV + 1, ACT.Silu, zT[:, 1, :])
            mod_rows(7)
            root(rn_o, "onorm_mm", 4, "onorm_root", bias=eps_k, scale=1.0 / P)
            gate(CONV + 2, ACT.Silu, zT[:, 2, :])
            gate(CONV + 3, ACT.Silu, zT[:, 3, :])
            act.wait_ge(sem("out_done"), 32)
            for half in range(2):
                for b in range(8):
                    if half == 0 and b == 5:
                        mod_rows(8)
                    gate(CONV + 4 + 8 * half + b, ACT.Sigmoid, sig[:, b, :])
                if half == 0:
                    act.wait_ge(sem("og"), 3 * HEADS)
                    act.dma_start(h, h_spill.rearrange("p (t d) -> p t d", t=NT)).then_inc(sem("h_back"), 16)
            act.wait_ge(sem("mixed"), 5 * KB)
            for j, w in enumerate(("ln1_g", "ln1_b")):
                act.dma_start(lnrow[:, j, :], T[w].to_broadcast([P, D])).then_inc(sem("ln1_in"), 16)
            for t in range(NT):
                for j in range(2):
                    act.wait_ge(sem("moments1"), 2 * t + j + 1)
                    A(rstd[:, t:t + 1], mv[:, t, 1:2], ACT.Sqrt, bias=eps_ln).then_inc(sem("root1"), 1)
            modulate(u2T, "xn2T_mm", "u2T", 32, 24)
            act.wait_ge(sem("logits"), 4)
            lg = probs[:, :, 0:E]
            A(lg, lg, ACT.Exp).then_inc(sem("exp_logits"), 1)
            for c in range(2):
                act.wait_ge(sem("spread_mm"), 2 + c + 1)
                for j in range(2):
                    A(g2row[:, c, 512 * j:512 * j + 512], bank[SPREAD_BANKS[1][2 * c + j]][:, :], ACT.Copy).then_inc(sem("g2row"), 1)

            def copy_gathered(n):
                act.wait_ge(sem("gather_mm"), n + 1)
                A(xs, bank[3][:, :], ACT.Copy).then_inc(sem("gathered"), 1)
                A(xsc, bank[4][:, 0:256], ACT.Copy).then_inc(sem("gathered"), 1)

            copy_gathered(0)
            with act.Fori(0, E) as e:
                act.wait_ge(sem("gu_mm"), e * 2 + 1)
                A(sil, bank[0][:, :], ACT.Silu).then_inc(sem("sil"), 1)
                A(silc, bank[2][:, 0:256], ACT.Silu).then_inc(sem("sil"), 1)
                copy_gathered(e + 1)
                act.wait_ge(sem("hidT_mm"), e * 2 + 1)
                A(hdT.rearrange("p (h j) s -> p h j s", h=2), by_block(6, 0, 64, 4), ACT.Copy).then_inc(sem("hidT"), 1)
                act.wait_ge(sem("down_mm"), e + 1)
                act.wait_ge(sem("ys_out"), e * 96 + 1)
                A(ys, bank[7][:, :], ACT.Copy).then_inc(sem("ys"), 1)
                A(ysc, bank[5][:, 0:256], ACT.Copy).then_inc(sem("ys"), 1)
                act.wait_ge(sem("ys"), e * 2 + 3)
                for half in range(2):
                    act.dma_start(ys_dram[bass.ds(e * CAP_S, CAP_S), 512 * half:512 * half + 512],
                                  ys[64 * half:64 * half + 64, :]).then_inc(sem("ys_out"), 16)
                for q in range(4):
                    act.dma_start(ysc_dram[bass.ds(e * CAP_C, CAP_C), 256 * q:256 * q + 256],
                                  ysc[32 * q:32 * q + CAP_C, :]).then_inc(sem("ys_out"), 16)
            for n, t in enumerate(SCATTER_ORDER):
                act.wait_ge(sem("moments2"), n + 1)
                A(rstd[:, t:t + 1], mv[:, t, 1:2], ACT.Sqrt, bias=eps_ln).then_inc(sem("root2"), 1)
                act.wait_ge(sem("y"), n + 1)
                act.dma_start(O[1][P * t:P * t + P, :] if t < ST else O[0], h[:, t, :]).then_inc(sem("out_done"), 16)
            act.wait_ge(sem("out_done"), 16 * (2 + NT))

        @block.vector
        def _(dve):
            V = nc.vector

            class Stage:
                def __init__(self, name):
                    self.sem, self.n = sem(name), 0

                def add(self, ins):
                    ins.then_inc(self.sem, 1)
                    self.n += 1

                def settle(self):
                    dve.wait_ge(self.sem, self.n)

            dve.wait_ge(sem("loaded"), 64)
            V.memset(misc[:, 2432:2688], 0.0).then_inc(sem("cond"), 1)
            s = Stage("sin_arg")
            for layer in range(2):
                dve.wait_ge(sem("hid_mm"), layer + 1)
                if layer:
                    dve.wait_ge(sem("hid"), 1)
                for b, a, n in ((2 * layer, 0, SEQ_S), (2 * layer + 1, SEQ_S, SEQ_C)):
                    s.add(V.tensor_scalar(sin_arg[:, a:a + n], bank[b][0:64, 0:n], K("hy_b1" if layer == 0 else "hy_b2")[0:64, :],
                                          K("hy_freq")[0:64, :], ALU.add, ALU.mult))
                s.settle()
                s.add(V.tensor_scalar(sin_n, sin_arg, 1.0 / (2.0 * math.pi), MAGIC, ALU.mult, ALU.add))
                s.settle()
                s.add(V.tensor_scalar(sin_n, sin_n, -MAGIC, None, ALU.add))
                for part in TWO_PI:
                    s.settle()
                    s.add(V.scalar_tensor_tensor(sin_arg, sin_n, -part, sin_arg, ALU.mult, ALU.add))
                s.settle()
                s.add(V.tensor_scalar(sin_arg, sin_arg, PI_BELOW, -PI_BELOW, ALU.min, ALU.max))
                s.settle()
                s.add(V.engine_nop())
            s = Stage("filt")
            dve.wait_ge(sem("window"), NT)
            for t in range(NT):
                dve.wait_ge(sem("filt_mm"), t + 1)
                s.add(V.tensor_tensor(filt[:, t, :], bank[4 + t if t < 4 else 0][:, :], filt[:, t, :], ALU.mult))
            hs = Stage("h")
            dve.wait_ge(sem("x_in"), 64)
            hs.add(V.tensor_tensor(h[:, 0:ST, 0:512], h[:, 0:ST, 0:512], posr, ALU.add))
            hs.add(V.tensor_tensor(h[:, 0:ST, 512:D], h[:, 0:ST, 512:D], posc.unsqueeze(1).to_broadcast([P, ST, 512]), ALU.add))
            hs.settle()
            bs, ms = Stage("bn"), Stage("moments")

            def moments(t, src, stage):
                for j in range(2):
                    bs.add(V.bn_stats(bn[:, t, 6 * j:6 * j + 6], src[:, 512 * j:512 * j + 512]))
                bs.settle()
                stage.add(V.bn_aggr(mv[:, t, :], bn[:, t, :]))

            for t in range(NT):
                moments(t, h[:, t, :], ms)
            rs, xs_ = Stage("rstd"), Stage("xn")
            rn_st = Stage("rn")
            dve.wait_ge(sem("root"), 1)
            rs.add(V.reciprocal(rstd, rstd))
            rs.settle()
            for t in range(NT):
                xs_.add(V.tensor_scalar(xn[:, t, :], h[:, t, :], mv[:, t, 0:1], rstd[:, t:t + 1], ALU.subtract, ALU.mult))
            ms2 = Stage("mod_col")
            by_cond = modT[:, :].rearrange("p (c b) -> p c b", c=2)
            dve.wait_ge(sem("mod_mm"), 1)
            V.tensor_copy(modrow, bank[3][:, :]).then_inc(sem("mod_row"), 1)
            s = Stage("fnorm")
            dve.wait_ge(sem("norm_tr"), 1)
            for j in range(2):
                s.add(V.tensor_scalar(fnorm[:, 4 * j:4 * j + 4], bank[1 + j][:, :].rearrange("p (b x) -> p b x", b=4)[:, :, 0],
                                      1e-6, None, ALU.add))
            s.settle()
            s.add(V.reciprocal(fnorm_inv, fnorm))
            s.add(V.tensor_tensor(skip_norm.rearrange("p (j b) -> p j b", j=2), fnorm.rearrange("p (j b) -> p j b", j=2),
                                  K("skip").unsqueeze(1).to_broadcast([P, 2, 4]), ALU.mult))
            dve.wait_ge(sem("mod_tr"), 1)
            src = bank[7][:, :].rearrange("p (i j x) -> p j i x", i=4, j=4)
            for c in range(2):
                ms2.add(V.tensor_tensor(modT[:, 48 * c:48 * c + 16].rearrange("p (j i) -> p j i", j=4),
                                        src[:, :, :, c], K("b_mod")[:, 0:16].rearrange("p (j i) -> p j i", j=4), ALU.add))
            ms2.settle()
            ms2.add(V.tensor_scalar(by_cond[:, :, 8:16], by_cond[:, :, 8:16], 1.0, None, ALU.add))

            def modulate_prompt(dst, mm_done, out, sc, sh):
                for k in range(KB):
                    dve.wait_ge(sem(mm_done), k + 1)
                    V.tensor_scalar(dst[:, k, SEQ_S:TOK], bank[k % 2][:, 0:SEQ_C], modT[:, 48 + sc + k:48 + sc + k + 1],
                                    modT[:, 48 + sh + k:48 + sh + k + 1], ALU.mult, ALU.add).then_inc(sem(out), 1)

            ms2.settle()
            modulate_prompt(uT, "xnT_mm", "uT_prompt", 8, 0)

            def mod_column(n):
                dve.wait_ge(sem("mod_tr"), n + 1)
                b = 4 * (n + 3)
                d = by_cond[:, :, b:b + 4]
                ms2.add(V.tensor_reduce(d, bank[7][:, :].rearrange("p (i j x) -> p x i j", i=4, j=4)[:, 0:2], AX, ALU.add))
                ms2.settle()
                ms2.add(V.scalar_tensor_tensor(d, d, 1.0 if 32 <= b < 40 else 0.0,
                                               K("b_mod")[:, b:b + 4].unsqueeze(1).to_broadcast([P, 2, 4]), ALU.add, ALU.add))

            cs_ = Stage("conv")
            conv_dst = [x1T] * 4 + [uuT] * 4 + [x0T] * 4 + [qT] * 4 + [kT] * 4 + [vT] * 4

            def conv(n):
                if n in MOD_TRANSPOSE:
                    mod_column(MOD_TRANSPOSE[n])
                dve.wait_ge(sem("tap"), 2 * (n + 1))
                w = K("conv_b" if n < 12 else "conv_a").rearrange("p (b j) -> p b j", j=3)[:, HY_BLOCK[n] if n < 12 else n - 12, :]
                d = conv_dst[n][:, n % 4, :]
                for tap_, shift in ((0, 1), (2, -1)):
                    if tap_:
                        cs_.settle()
                    for b, a, l in ((n % 2, 0, SEQ_S), (2 + n % 2, SEQ_S, SEQ_C)):
                        o = (1, l) if shift == 1 else (0, l - 1)
                        out = d[:, a + o[0]:a + o[1]]
                        cs_.add(V.scalar_tensor_tensor(out, bank[b][:, o[0] - shift:o[1] - shift], w[:, tap_:tap_ + 1], out,
                                                       ALU.mult, ALU.add))

            us = Stage("uu")
            for n in range(12):
                conv(n)
                if 4 <= n < 8:
                    cs_.settle()
                    us.add(V.tensor_tensor(uuT[:, n - 4, :], x1T[:, n - 4, :], uuT[:, n - 4, :], ALU.mult))
            for n in range(12, 16):
                conv(n)
            s = Stage("product")
            for j in range(FT + 1):
                dve.wait_ge(sem("spec_mm"), FT + 1 + j + 1)
                r = P if j < FT else FREQ_C
                a, b = (bank[4 + 2 * (j % 2) + cs][0:r, :] for cs in range(2))
                fc, fs = (fspec[0:r, 2 * j + cs, :] for cs in range(2))
                s.add(V.tensor_tensor(uspec[0:r, 2 * j, :], a, fc, ALU.mult))
                s.add(V.tensor_tensor(ptmp[0:r, 0, :], b, fs, ALU.mult))
                s.add(V.tensor_tensor(uspec[0:r, 2 * j + 1, :], a, fs, ALU.mult))
                s.add(V.tensor_tensor(ptmp[0:r, 1, :], b, fc, ALU.mult))
                s.settle()
                s.add(V.tensor_tensor(uspec[0:r, 2 * j, :], uspec[0:r, 2 * j, :], ptmp[0:r, 0, :], ALU.subtract))
                s.add(V.tensor_tensor(uspec[0:r, 2 * j + 1, :], uspec[0:r, 2 * j + 1, :], ptmp[0:r, 1, :], ALU.add))
                s.settle()
            qk = Stage("qk_normal")

            def over_norm(n):
                dve.wait_ge(sem("qk_spread"), n + 1)
                A_, B_ = (6, 7) if n < 4 or n % 2 else (4, 5)
                d = (qT if n < 4 else kT)[:, n % 4, :]
                qk.add(V.tensor_tensor(d[:, 0:SEQ_S], bank[A_][:, :], d[:, 0:SEQ_S], ALU.mult))
                qk.add(V.tensor_tensor(d[:, SEQ_S:TOK], bank[B_][:, 0:SEQ_C], d[:, SEQ_S:TOK], ALU.mult))

            for n in range(16, 19):
                conv(n)
            dve.wait_ge(sem("norm_root"), 2)
            rn_st.add(V.reciprocal(rn[0], rn[0]))
            conv(19)
            s = Stage("yb")
            dve.wait_ge(sem("fnorm"), 4)
            parts = ((0, 0, SEQ_S), (1, SEQ_S, SEQ_C))
            for cb in range(4):
                dve.wait_ge(sem("inv_mm"), cb + 1)
                for j, a, l in parts:
                    s.add(V.scalar_tensor_tensor(uuT[:, cb, a:a + l], uuT[:, cb, a:a + l], skip_norm[:, 4 * j + cb:4 * j + cb + 1],
                                                 bank[4 + 2 * (cb % 2) + j][:, 0:l], ALU.mult, ALU.add))
                s.settle()
                for j, a, l in parts:
                    s.add(V.scalar_tensor_tensor(x0T[:, cb, a:a + l], uuT[:, cb, a:a + l], fnorm_inv[:, 4 * j + cb:4 * j + cb + 1],
                                                 x0T[:, cb, a:a + l], ALU.mult, ALU.mult))
            conv(20)
            over_norm(0)
            conv(21)
            over_norm(1)
            dve.wait_ge(sem("norm_root"), 4)
            rn_st.add(V.reciprocal(rn[1], rn[1]))
            conv(22)
            over_norm(2)
            conv(23)
            over_norm(3)
            dve.wait_ge(sem("ba_mm"), 1)
            V.tensor_copy(barow[:, 0:SEQ_S], bank[0][:, :]).then_inc(sem("ba_row"), 1)
            V.tensor_copy(barow[:, SEQ_S:TOK], bank[2][:, 0:SEQ_C]).then_inc(sem("ba_row"), 1)
            over_norm(4)
            s = Stage("dec")

            def tx(v):
                return v.rearrange("p (t x) -> p t x", t=NT)

            dve.wait_ge(sem("ba_tr"), 1)
            for b, t0, t1 in ((1, 0, ST), (3, ST, NT)):
                s.add(V.tensor_reduce(ba[:, t0:t1, :], bank[b][:, 0:P * (t1 - t0)].rearrange("p (t j x) -> p t x j", j=4, x=32)[:, :, 0:16],
                                      AX, ALU.add))
            s.settle()
            s.add(V.tensor_tensor(tx(d_xa), ba[:, :, 8:16], K("dt_bias").unsqueeze(1).to_broadcast([P, NT, 8]), ALU.add))
            s.settle()
            s.add(V.tensor_scalar(d_relu, d_xa, 0.0, None, ALU.max))
            s.add(V.tensor_scalar(d_neg, d_xa, -1.0, None, ALU.mult))
            s.settle()
            s.add(V.tensor_tensor(d_neg, d_neg, d_xa, ALU.min))
            over_norm(5)
            dve.wait_ge(sem("dec_act"), 2)
            s.add(V.tensor_scalar(d_tmp, d_tmp, 1.0, None, ALU.add))
            s.settle()
            s.add(V.reciprocal(d_beta, d_tmp))
            s.settle()
            s.add(V.tensor_scalar(d_negbeta, d_beta, -1.0, None, ALU.mult))
            dve.wait_ge(sem("dec_act"), 4)
            s.add(V.tensor_tensor(d_relu, d_relu, d_neg, ALU.add))
            s.settle()
            s.add(V.scalar_tensor_tensor(tx(d_g), tx(d_relu), -1.0, d_expa[:, 0:8].unsqueeze(1).to_broadcast([P, NT, 8]),
                                         ALU.mult, ALU.mult))
            over_norm(6)
            dve.wait_ge(sem("gc_mm"), 1)
            s.add(V.tensor_copy(tx(d_gc)[:, :, 0:4], bank[2][:, 0:20].rearrange("p (t x) -> p t x", t=NT)))
            s.add(V.tensor_copy(tx(d_gc)[:, :, 4:8], bank[2][:, 32:52].rearrange("p (t x) -> p t x", t=NT)))
            s.add(V.tensor_copy(d_tot, bank[2][:, 64:104]))
            s.settle()
            s.add(V.tensor_tensor(d_edk, d_tot, d_gc, ALU.subtract))
            over_norm(7)
            dve.wait_ge(sem("dec_act"), 7)
            s.add(V.tensor_scalar(d_negegc, d_negegc, -1.0, None, ALU.mult))

            dve.wait_ge(sem("loaded_delta"), 16)
            neg = (C("neg_f"), C("neg_b"))
            masks = tuple(C(m).bitcast(U32).rearrange("p (l c) -> p l c", l=LEVELS) for m in ("mask_lo", "mask_up"))
            ds, pre_E, pre_LT, os_ = ([Stage(f"{v}{r}") for r in range(2)] for v in ("dn_dve", "dn_E", "dn_LT", "dn_o"))
            first = [True] * NT

            def bank4(r, b):
                return bank[4 * r + b][:, :].rearrange("p (h c) -> p h c", h=HEADS)

            def x(p, r, hh):
                return 8 * TILE[r][p] + 4 * r + hh

            def log_decays(p, r):
                dve.wait_ge(sem(f"dn_R{r}"), p + 1)
                for hh in range(HEADS):
                    pre_E[r].add(V.scalar_tensor_tensor(dD[r][:, hh, :], bank[4 * r + 3][:, P * hh:P * hh + P],
                                                        d_gc[:, x(p, r, hh):x(p, r, hh) + 1], neg[r], ALU.subtract, ALU.add))

            def minus_L(p, r):
                dve.wait_ge(sem(f"dn_D{r}"), p + 1)
                dve.wait_ge(sem(f"dn_KK{r}"), p + 1)
                for hh in range(HEADS):
                    pre_LT[r].add(V.scalar_tensor_tensor(dLnT[r][:, hh, :], bank[4 * r][:, P * hh:P * hh + P],
                                                         d_negbeta[:, x(p, r, hh):x(p, r, hh) + 1], dD[r][:, hh, :], ALU.mult, ALU.mult))

            def outputs(p, r):
                dve.wait_ge(sem(f"dn_pe{r}"), PE_N * (p + 1))
                t = TILE[r][p]
                o = oT[:, :, P * t:P * t + P]
                for v in os_:
                    v.settle()
                if first[t]:
                    os_[r].add(V.tensor_copy(o, bank4(r, 1)))
                    first[t] = False
                else:
                    os_[r].add(V.tensor_tensor(o, bank4(r, 1), o, ALU.add))
                if p == ST - 1:
                    os_[r].add(V.memset(state[r], 0.0))
                    for _i in range(3):
                        os_[r].add(V.engine_nop())
                else:
                    if p == 0:
                        dve.wait_ge(sem("state_in"), 32)
                    for hh in range(HEADS):
                        os_[r].add(V.scalar_tensor_tensor(state[r][:, hh, :], state[r][:, hh, :], d_egl[:, x(p, r, hh):x(p, r, hh) + 1],
                                                          bank[4 * r + 2][:, P * hh:P * hh + P], ALU.mult, ALU.add))

            for r in range(2):
                log_decays(0, r)

            def blend(r, lev, which, data):
                m = masks[(r + which) % 2][:, lev, :].unsqueeze(1).to_broadcast([P, HEADS, P])
                return V.copy_predicated((dM, dU)[which][r], m, data)

            def start(p):
                for r in range(2):
                    for w in (dM, dU):
                        ds[r].add(V.tensor_copy(w[r], ident.unsqueeze(1).to_broadcast([P, HEADS, P])))
                for r in range(2):
                    minus_L(p, r)
                    ds[r].settle()
                    if r == 0:
                        pre_LT[r].settle()
                        ds[r].add(blend(r, 0, 1, dLnT[r]))

            start(0)
            for p in range(NT):
                def pe_(r, step):
                    dve.wait_ge(sem(f"dn_pe{r}"), PE_N * p + PES[step])

                for r in range(2):
                    if r:
                        pre_LT[r].settle()
                        ds[r].add(blend(r, 0, 1, dLnT[r]))
                    pe_(r, "LN")
                    ds[r].add(blend(r, 0, 0, bank4(r, 0)))
                if p:
                    for r in range(2):
                        outputs(p - 1, r)
                for lev in range(1, LEVELS):
                    for r in range(2):
                        if lev < LEVELS - 1:
                            pe_(r, f"MM{lev}")
                            ds[r].settle()
                            ds[r].add(blend(r, lev, 0, bank4(r, 1)))
                        pe_(r, f"MU{lev}")
                        if lev == LEVELS - 1:
                            ds[r].settle()
                        ds[r].add(blend(r, lev, 1, bank4(r, 2)))
                    for r in range(2):
                        t = TILE[r][p]
                        if lev == 1:
                            pe_(r, "QK")
                            ds[r].add(V.tensor_tensor(dAT[r], bank4(r, 3), dD[r], ALU.mult))
                        if lev == 2:
                            dve.wait_ge(sem(f"dn_act{r}"), ACT_N * p + ACTS["EG"])
                            ds[r].add(V.tensor_tensor(dQG[r], qT[:, :, P * t:P * t + P], dQG[r], ALU.mult))
                for r in range(2):
                    pe_(r, "V")
                    for hh in range(HEADS):
                        ds[r].add(V.tensor_scalar(dVN[r][:, hh, :], bank[4 * r][:, P * hh:P * hh + P],
                                                  d_beta[:, x(p, r, hh):x(p, r, hh) + 1], None, ALU.mult))
                    assert ds[r].n == DVE_N * (p + 1), (ds[r].n, DVE_N)
                    if p + 1 < NT:
                        log_decays(p + 1, r)
                if p + 1 < NT:
                    start(p + 1)
            for r in range(2):
                outputs(NT - 1, r)

            mod_column(6)
            dve.wait_ge(sem("onorm_root"), 2)
            rn_st.add(V.reciprocal(rn_o, rn_o))
            mod_column(7)
            s = Stage("og")
            for n in range(HEADS):
                dve.wait_ge(sem("o_spread"), n + 1)
                for b, a, l in ((4 + 2 * (n % 2), 0, SEQ_S), (5 + 2 * (n % 2), SEQ_S, SEQ_C)):
                    s.add(V.scalar_tensor_tensor(oG[:, n, a:a + l], oT[:, n, a:a + l], K("gnorm"), bank[b][:, 0:l], ALU.mult, ALU.mult))
                s.settle()
                dve.wait_ge(sem("zg"), 8)
                s.add(V.tensor_tensor(oG[:, n, :], oG[:, n, :], zT[:, n, :], ALU.mult))
            mod_column(8)
            dg = Stage("diag")

            def diagonals(block):
                for c in range(2):
                    for k in range(KB):
                        at = 48 * c + block + k
                        dg.add(V.tensor_scalar(diag[:, c, k, :], ident, modT[:, at:at + 1], None, ALU.mult))

            diagonals(16)
            s = Stage("mixed")
            for n in range(KB):
                if n == 4:
                    for c in range(2):
                        dve.wait_ge(sem("spread_mm"), c + 1)
                        for j in range(2):
                            V.tensor_copy(grow[:, c, 512 * j:512 * j + 512], bank[SPREAD_BANKS[0][2 * c + j]][:, :]).then_inc(sem("gate_row"), 1)
                    dve.wait_ge(sem("gate_row"), 4)
                dve.wait_ge(sem("zg"), 2 * (12 + 8 * (n // 4)))
                dve.wait_ge(sem("up_mm"), n + 1)
                banks = (4, 5, 6, 7) if n % 2 == 0 else (0, 2, 1, 3)
                if n:
                    s.settle()
                s.add(V.tensor_tensor(mixedT[:, n, 0:SEQ_S], bank[banks[0]][:, :], sig[:, n % 4, 0:SEQ_S], ALU.mult))
                s.add(V.tensor_tensor(mixedT[:, n, SEQ_S:TOK], bank[banks[1]][:, 0:SEQ_C], sig[:, n % 4, SEQ_S:TOK], ALU.mult))
                s.add(V.tensor_tensor(uptmp[:, 0:SEQ_S], bank[banks[2]][:, :], sig[:, 4 + n % 4, 0:SEQ_S], ALU.mult))
                s.add(V.tensor_tensor(uptmp[:, SEQ_S:TOK], bank[banks[3]][:, 0:SEQ_C], sig[:, 4 + n % 4, SEQ_S:TOK], ALU.mult))
                s.settle()
                s.add(V.tensor_tensor(mixedT[:, n, :], mixedT[:, n, :], uptmp, ALU.add))
            s.settle()
            dve.wait_ge(sem("h_back"), 16)
            s = Stage("resid1")
            m1, orr, x2 = Stage("moments1"), Stage("out_read"), Stage("xn2")

            def norm(t, src, dst, stage, root, nroot, out):
                moments(t, src, stage)
                dve.wait_ge(sem(root), nroot)
                rs.add(V.reciprocal(rstd[:, t:t + 1], rstd[:, t:t + 1]))
                rs.settle()
                out.add(V.tensor_scalar(dst, src, mv[:, t, 0:1], rstd[:, t:t + 1], ALU.subtract, ALU.mult))

            def residual(t, j, src, tmp, gate_, read, out):
                c = slice(512 * j, 512 * j + 512)
                read.add(V.tensor_tensor(tmp[:, c], src[:, :], gate_[:, c], ALU.mult))
                read.settle()
                out.add(V.scalar_tensor_tensor(h[:, t, c], h[:, t, c], ALPHA, tmp[:, c], ALU.mult, ALU.add))
                out.settle()
                bs.add(V.bn_stats(bn[:, t, 6 * j:6 * j + 6], h[:, t, c]))

            def affine_norm(t, stage, root, nroot, out, rows_in, rows):
                bs.settle()
                stage.add(V.bn_aggr(mv[:, t, :], bn[:, t, :]))
                stage.settle()
                dve.wait_ge(sem(rows_in), 32)
                out.add(V.scalar_tensor_tensor(h[:, t, :], h[:, t, :], mv[:, t, 0:1], rows[:, 0, :], ALU.subtract, ALU.mult))
                dve.wait_ge(sem(root), nroot)
                rs.add(V.reciprocal(rstd[:, t:t + 1], rstd[:, t:t + 1]))
                rs.settle()
                out.settle()

            for t in range(NT):
                c = 0 if t < ST else 1
                for j in range(2):
                    dve.wait_ge(sem("out_mm"), 2 * t + j + 1)
                    residual(t, j, bank[4 + (2 * t + j) % 4], otmp[:, t % 2, :], grow[:, c, :], orr, s)
                affine_norm(t, m1, "root1", 2 * t + 1, s, "ln1_in", lnrow)
                s.add(V.scalar_tensor_tensor(h[:, t, :], h[:, t, :], rstd[:, t:t + 1], lnrow[:, 1, :], ALU.mult, ALU.add))
                s.settle()
                norm(t, h[:, t, :], xn2[:, t, :], m1, "root1", 2 * t + 2, x2)
            modulate_prompt(u2T, "xn2T_mm", "u2T_prompt", 32, 24)
            diagonals(40)
            dve.wait_ge(sem("router_mm"), 1)
            V.tensor_copy(lrow[:, 0:SEQ_S], bank[4][:, :]).then_inc(sem("logit_row"), 1)
            V.tensor_copy(lrow[:, SEQ_S:TOK], bank[5][:, 0:SEQ_C]).then_inc(sem("logit_row"), 1)
            dve.wait_ge(sem("logit_tr"), 1)
            s = Stage("logits")
            for b, t0, t1 in ((2, 0, ST), (6, ST, NT)):
                s.add(V.tensor_reduce(logit[:, t0:t1, :], bank[b][:, 0:P * (t1 - t0)].rearrange("p (t j x) -> p t x j", j=4, x=32)[:, :, 0:E],
                                      AX, ALU.add))
            s.settle()
            s.add(V.tensor_reduce(rmax, logit, AX, ALU.max))
            s.settle()
            s.add(V.tensor_tensor(probs[:, :, 0:E], logit, rmax.unsqueeze(2).to_broadcast([P, NT, E]), ALU.subtract))
            s.add(V.memset(probs[:, :, E:E + 1], 0.0))
            dve.wait_ge(sem("exp_logits"), 1)
            s.add(V.tensor_reduce(rsum, probs[:, :, 0:E], AX, ALU.add))
            s.settle()
            s.add(V.reciprocal(rsum, rsum))
            s.settle()
            V.tensor_tensor(probs[:, :, 0:E], probs[:, :, 0:E], rsum.unsqueeze(2).to_broadcast([P, NT, E]), ALU.mult) \
                .then_inc(sem("probs"), 1)
            s = Stage("topk")
            dve.wait_ge(sem("prob_tr"), 1)
            s.add(V.tensor_copy(rrow[:, 0:SEQ_S], bank[6][0:16, :]))
            s.add(V.tensor_copy(rrow[:, SEQ_S:TOK], bank[7][0:16, 0:SEQ_C]))
            s.settle()
            for a, l, rounds in ((0, SEQ_S, CAP_S // 8), (SEQ_S, SEQ_C, CAP_C // 8)):
                for _r in range(rounds):
                    s.add(V.max(top8, rrow[:, a:a + l]))
                    s.settle()
                    s.add(V.match_replace(rrow[:, a:a + l], top8, rrow[:, a:a + l], -1.0))
                    s.settle()
            s.add(V.tensor_scalar(mask, rrow, 0.0, None, ALU.is_lt))
            s.settle()
            for a, l in ((0, SEQ_S), (SEQ_S, SEQ_C)):
                s.add(V.tensor_tensor_scan(count[:, a:a + l], mask[:, a:a + l], mask[:, a:a + l], 0.0, ALU.add, ALU.max))
            s.settle()
            s.add(V.tensor_tensor(count, count, mask, ALU.mult))
            s.settle()
            V.tensor_scalar(rrow, count, -1.0, None, ALU.add).then_inc(sem("slot_row"), 1)
            dve.wait_ge(sem("slot_tr"), 1)
            V.tensor_copy(slots[:, :, 0:E], bank[5][:, 0:80].rearrange("p (t e) -> p t e", t=NT)).then_inc(sem("slots"), 1)
            V.memset(slots[:, :, E:E + 1], -1.0).then_inc(sem("slots"), 1)
            V.engine_nop().then_inc(sem("ys"), 1)
            V.engine_nop().then_inc(sem("ys_out"), 1)
            dve.wait_ge(sem("slots"), 2)

            def col(v, t, n):
                return v[:, t, bass.ds(n, 1)]

            def onehot(n):
                for t in range(ST):
                    V.tensor_scalar(Gs[:, t, :], C("iota"), col(slots, t, n), None, ALU.is_equal).then_inc(sem("onehot"), 1)
                V.tensor_scalar(Gc, C("iota")[:, 0:32], col(slots, ST, n), None, ALU.is_equal).then_inc(sem("onehot"), 1)

            def xT(n):
                dve.wait_ge(sem("xT_mm"), n + 1)
                for stage, op in ((0, ALU.mult), (1, ALU.add)):
                    if stage:
                        dve.wait_ge(sem("xT"), n * 4 + 2)
                    for c, (dst, b, blocks, width, halves) in enumerate(((xsT, 3, 4, CAP_S, 2), (xcT, 4, 2, 32, 4))):
                        src = dst if stage else bank[b][:, 0:P * blocks].rearrange("p (j h s) -> p h j s", j=blocks, s=width)
                        if stage:
                            src = src.rearrange("p (h j) s -> p h j s", h=halves)
                        m = modT[:, 48 * c + (24 if stage else 32):48 * c + (32 if stage else 40)]
                        m = m.rearrange("p (h j) -> p h j", h=halves).unsqueeze(3).to_broadcast([P, halves, blocks, width])
                        V.tensor_tensor(dst.rearrange("p (h j) s -> p h j s", h=halves), src, m, op).then_inc(sem("xT"), 1)

            onehot(0)
            xT(0)
            with dve.Fori(0, E) as e:
                dve.wait_ge(sem("gather_mm"), e + 1)
                dve.wait_ge(sem("onehot"), e * 5 + 5)
                onehot(e + 1)
                for t in range(ST):
                    V.tensor_scalar(GA[:, t, bass.ds(e * CAP_S, CAP_S)], C("iota"), col(slots, t, e), col(probs, t, e),
                                    ALU.is_equal, ALU.mult).then_inc(sem("weighted"), 1)
                V.tensor_scalar(GAc[:, bass.ds(e * CAP_C, CAP_C)], C("iota")[:, 0:CAP_C], col(slots, ST, e), col(probs, ST, e),
                                ALU.is_equal, ALU.mult).then_inc(sem("weighted"), 1)
                dve.wait_ge(sem("sil"), e * 2 + 2)
                dve.wait_ge(sem("gu_mm"), e * 2 + 2)
                V.tensor_tensor(hd, bank[1][:, :], sil, ALU.mult).then_inc(sem("hid_e"), 1)
                V.tensor_tensor(hdc, bank[5][:, 256:512], silc, ALU.mult).then_inc(sem("hid_e"), 1)
                dve.wait_ge(sem("hidT_mm"), e * 2 + 2)
                V.tensor_copy(hdcT.rearrange("p (h j) s -> p h j s", h=4), by_block(2, 256, 32, 2)).then_inc(sem("hidTc"), 1)
                xT(e + 1)
            for j in range(PAIRS + 1):
                dve.wait_ge(sem("ct_mm"), j + 1)
                if j < PAIRS:
                    V.tensor_copy(CT[:, j, :], bank[(0, 1, 2, 6)[j % 4]][:, :]).then_inc(sem("ct"), 1)
                else:
                    V.tensor_copy(CTc, bank[0][:, 0:2 * P].rearrange("p (j t) -> p j t", j=2)).then_inc(sem("ct"), 1)
            s = Stage("resid2")
            m2, yr = Stage("moments2"), Stage("y_read")
            dve.wait_ge(sem("g2row"), 4)
            for n, t in enumerate(SCATTER_ORDER):
                c = 0 if t < ST else 1
                for j in range(2):
                    dve.wait_ge(sem("y_mm"), 2 * n + j + 1)
                    residual(t, j, bank[SCATTER_BANKS[n][j]], ytmp[:, n % 2, :], g2row[:, c, :], yr, s)
                affine_norm(t, m2, "root2", n + 1, s, "ln2_in", ln2row)
                V.scalar_tensor_tensor(h[:, t, :], h[:, t, :], rstd[:, t:t + 1], ln2row[:, 1, :], ALU.mult, ALU.add).then_inc(sem("y"), 1)


def steps(*named):
    out, n = {}, 0
    for name, k in named:
        n += k
        out[name] = n
    return out, n


KT_LEVEL = 3
PES, PE_N = steps(("LN", 1), *[s for lev in range(1, LEVELS) for s in
                               ((f"W{lev}", 1), *((("QK", 1),) if lev == 1 else ()), *((("KT", 1),) if lev == KT_LEVEL else ()),
                                *(((f"MM{lev}", 1),) if lev < LEVELS - 1 else ()), (f"MU{lev}", 1))], ("WT", 1), ("V", 1), ("OS", 1))
ACTS, ACT_N = steps(("EG", 1), *[(f"W{lev}", 1) for lev in range(1, LEVELS)], ("WT", 1))
DVE, DVE_N = steps(("MU", 2), ("PM0", 2), ("P0", 0), *[v for lev in range(1, LEVELS) for v in
                   (*(((f"PM{lev}", 1),) if lev < LEVELS - 1 else ()), (f"P{lev}", 1),
                    *((("AT", 1),) if lev == 1 else ()), *((("QG", 1),) if lev == 2 else ()))], ("VN", 4))
TILE = ((0, 1, 2, 3, 4), (3, 2, 1, 0, 4))
MOD_TRANSPOSE = {3: 1, 7: 2, 11: 3, 15: 4, 19: 5}
DEC_NEG, DEC_G, DEC_GC, DEC_ALL = 6, 11, 15, 16
HY_BLOCK = (4, 5, 6, 7, 8, 9, 10, 11, 0, 1, 2, 3)
SPREAD_BANKS = ((4, 5, 6, 7), (0, 1, 3, 4))
SCATTER_ORDER = (0, 4, 1, 2, 3)
SCATTER_BANKS = ((3, 4), (0, 1), (2, 6), (5, 7), (3, 4))

_INS = ["w_mod", "w_in", "w_up_a", "w_up_b", "w_out", "w_e_gate", "w_e_up", "w_e_down"]


def kernel(**inputs):
    import concourse.bacc as _bacc
    from concourse.bass_utils import run_bass_kernel_spmd as _run

    nc = _bacc.Bacc("TRN2", target_bir_lowering=False, num_devices=1)
    arr = {k: np.ascontiguousarray(v) for k, v in inputs.items()}
    arrays = {k: arr[k][0] for k in _INS + ["x_prompt", "x_sample"]}
    for k in ("state_delta_fwd", "state_delta_bwd"):
        arrays[k] = arr[k][0, 0]
    for k in ("ln1_g", "ln1_b", "ln2_g", "ln2_b"):
        arrays[k] = arr[k]
    pk = np.zeros((P, PK_N), np.float32)

    def put(name, v):
        a, n = PK[name]
        v = v.reshape(v.shape[0], -1)
        pk[0:v.shape[0], a:a + v.shape[1]] = v

    def blocks(v, n):
        return v.reshape(n, P, -1).transpose(1, 0, 2)

    put("cond", blocks(np.stack([arr["c"][0], arr["c_ctx"]], 1), KB))
    put("b_mod", blocks(arr["b_mod"][0], 48))
    put("conv_a", blocks(arr["conv_a_w"][0].T, 12))
    put("conv_b", blocks(arr["conv_b_w"][0].T, 12))
    put("conv_bb", blocks(arr["conv_b_b"][0], 12))
    put("skip", blocks(arr["hy_bias"][0], 4))
    put("gnorm", arr["gnorm_w"][0])
    put("a_log", np.tile(arr["a_log"].reshape(1, 8), (P, 1)))
    put("dt_bias", np.tile(arr["dt_bias"].reshape(1, 8), (P, 1)))
    put("hy_b1", arr["hy_b1"][0])
    put("hy_b2", arr["hy_b2"][0])
    put("hy_freq", arr["hy_freq"][0])
    w_router = np.zeros((D, 32), np.float32)
    w_router[:, 0:E] = arr["w_router"][0]
    put("w_router", blocks(w_router, KB))
    w_ba = np.zeros((D, 32), np.float32)
    w_ba[:, 0:16] = arr["w_in"][0][:, COL_BA:COL_BA + 16]
    put("w_ba", blocks(w_ba, KB))
    put("hy_w1", arr["hy_w1"][0])
    put("hy_w2", arr["hy_w2"][0])
    put("hy_w3", arr["hy_w3"][0])
    arrays["packed"] = pk
    arrays.update(constants())
    arrays = {k: np.ascontiguousarray(v) for k, v in arrays.items()}
    T = {k: nc.dram_tensor(k + "_dram", v.shape, F32, kind="ExternalInput").ap() for k, v in arrays.items()}
    shapes = {"y_prompt": (1, SEQ_C, D), "y_sample": (1, SEQ_S, D), "state_fwd": (1, 1, HEADS, P, P), "state_bwd": (1, 1, HEADS, P, P)}
    outs = {k: nc.dram_tensor(k + "_out", s, F32, kind="ExternalOutput").ap() for k, s in shapes.items()}
    O = [outs["y_prompt"][0], outs["y_sample"][0], outs["state_fwd"][0, 0], outs["state_bwd"][0, 0]]
    build(nc, T, O)
    r = _run(nc, [{k + "_dram": v for k, v in arrays.items()}], core_ids=[0])
    return tuple(r.results[0][k + "_out"] for k in shapes)
```
